# Optimizing a Trainium2 kernel written in Bass

```python
import jax, jax.numpy as jnp
from jax import lax
import numpy as np

D_MODEL = 1024
BATCH = 1
SEQ = 512
DEPTH = 2
DEC_BATCH = 8
DEC_SEQ = 4
PAST_LEN = 1024
PAGE_SIZE = 128

CONV_DIM = D_MODEL
CONV_W = 3
N_HEADS = 16
HEAD_DIM = 64
N_KV = 4
GROUP = N_HEADS // N_KV
ATT_DIM = N_HEADS * HEAD_DIM
KV_DIM = N_KV * HEAD_DIM
CMP_STRIDE = 16
CMP_BLOCK = 2 * CMP_STRIDE
CMP_HID = 4 * HEAD_DIM
SLC_BLOCK = 64
TOP_N = 16
WINDOW = 512
PLE_DIM = 256
ROPE_THETA = 10000.0
RMS_EPS = 1e-6
Q_BLOCK = 64
N_KV_SLOTS = 4
IN_COLS = 4 * CONV_DIM + 2 * ATT_DIM + 6 * KV_DIM + 3 * N_HEADS + 2 * D_MODEL
NEG_INF = -1e30
FORCE_SCORE = 1e6

kernel_name = "hybrid_shortconv_nsa_decoder_step"

def _rms_norm(x, g):
    xf = x.astype(jnp.float32)
    y = xf * lax.rsqrt(jnp.mean(xf * xf, axis=-1, keepdims=True) + RMS_EPS)
    return (y * g.astype(jnp.float32)).astype(x.dtype)

def _rope(x, pos):
    half = HEAD_DIM // 2
    inv = jnp.power(ROPE_THETA, -jnp.arange(half, dtype=jnp.float32) / half)
    ang = pos.astype(jnp.float32)[:, None] * inv[None, :]
    cos = jnp.cos(ang)[:, None, :]
    sin = jnp.sin(ang)[:, None, :]
    xf = x.astype(jnp.float32)
    x1, x2 = xf[..., :half], xf[..., half:]
    return jnp.concatenate([x1 * cos - x2 * sin, x2 * cos + x1 * sin], axis=-1).astype(x.dtype)

def _masked_probs(s, mask):
    s = jnp.where(mask, s.astype(jnp.float32), NEG_INF)
    m = jnp.max(s, axis=-1, keepdims=True)
    e = jnp.where(mask, jnp.exp(s - m), 0.0)
    return e / jnp.maximum(jnp.sum(e, axis=-1, keepdims=True), 1e-30)

def _project(x, pos, ln_g, w_in):
    B, T, _ = x.shape
    h = _rms_norm(x, ln_g)
    z = jnp.einsum('btd,dc->btc', h, w_in)
    sizes = [CONV_DIM] * 4 + [ATT_DIM] + [KV_DIM] * 6 + [3 * N_HEADS, ATT_DIM, 2 * D_MODEL]
    cuts = np.cumsum(sizes)[:-1].tolist()
    (ba, ca, xa, za, q, kc, vc, ks, vs, kw, vw, g_br, zb, g_mix) = jnp.split(z, cuts, axis=-1)
    q = _rope(q.reshape(B, T, N_HEADS, HEAD_DIM), pos).reshape(B, T, N_KV, GROUP, HEAD_DIM)
    kc = _rope(kc.reshape(B, T, N_KV, HEAD_DIM), pos)
    ks = _rope(ks.reshape(B, T, N_KV, HEAD_DIM), pos)
    kw = _rope(kw.reshape(B, T, N_KV, HEAD_DIM), pos)
    vc = vc.reshape(B, T, N_KV, HEAD_DIM)
    vs = vs.reshape(B, T, N_KV, HEAD_DIM)
    vw = vw.reshape(B, T, N_KV, HEAD_DIM)
    g_br = jax.nn.sigmoid(g_br).reshape(B, T, N_KV, GROUP, 3)
    return ba, ca, xa, za, q, kc, vc, ks, vs, kw, vw, g_br, zb, g_mix

def _short_conv(u, prefix, w):
    T = u.shape[1]
    up = jnp.concatenate([prefix, u], axis=1)
    y = w[0] * up[:, 0:T]
    for j in range(1, CONV_W):
        y = y + w[j] * up[:, j:j + T]
    return y, up[:, T:]

def _compress(k, pos_emb, w1, w2):
    B, L = k.shape[:2]
    n_chunk = L // CMP_STRIDE
    ch = k[:, :n_chunk * CMP_STRIDE].reshape(B, n_chunk, CMP_STRIDE, N_KV, HEAD_DIM)
    first = jnp.einsum('bcsgd,sdh->bcgh', ch + pos_emb[None, None, :CMP_STRIDE, None, :], w1[:CMP_STRIDE])
    second = jnp.einsum('bcsgd,sdh->bcgh', ch + pos_emb[None, None, CMP_STRIDE:, None, :], w1[CMP_STRIDE:])
    hid = jax.nn.silu(first[:, :-1] + second[:, 1:])
    return jnp.einsum('bngh,hd->bngd', hid, w2)

def _to_blocks(k):
    B, L = k.shape[:2]
    n_blk = -(-L // SLC_BLOCK)
    kp = jnp.pad(k, ((0, 0), (0, n_blk * SLC_BLOCK - L), (0, 0), (0, 0)))
    return kp.reshape(B, n_blk, SLC_BLOCK, N_KV, HEAD_DIM).transpose(0, 3, 1, 2, 4)

def _overlap(n_cmp, n_slc):
    start = jnp.arange(n_cmp) * CMP_STRIDE
    sj = jnp.arange(n_slc) * SLC_BLOCK
    ov = (start[:, None] < sj[None, :] + SLC_BLOCK) & (start[:, None] + CMP_BLOCK > sj[None, :])
    return ov.astype(jnp.float32)

def _nsa_core(q, qpos, k_cmp, v_cmp, k_blk, v_blk, overlap, k_win, v_win, kwpos, gates):
    B, Tq = q.shape[:2]
    scale = HEAD_DIM ** -0.5
    n_cmp = k_cmp.shape[1]
    n_slc = k_blk.shape[2]
    n_sel = min(TOP_N, n_slc)
    s_c = jnp.einsum('bqgrd,bngd->bqgrn', q, k_cmp) * scale
    cmp_end = jnp.arange(n_cmp) * CMP_STRIDE + CMP_BLOCK - 1
    mask_c = (cmp_end[None, :] <= qpos[:, None])[None, :, None, None, :]
    p_c = _masked_probs(s_c, mask_c)
    o_c = jnp.einsum('bqgrn,bngd->bqgrd', p_c.astype(v_cmp.dtype), v_cmp)
    imp = jnp.einsum('bqgrn,nj->bqgj', p_c, overlap)
    blk = jnp.arange(n_slc)[None, :]
    cur = (qpos // SLC_BLOCK)[:, None]
    valid = blk <= cur
    forced = (blk == 0) | (blk == cur) | (blk == cur - 1)
    score = jnp.where(forced[None, :, None, :], FORCE_SCORE, imp)
    score = jnp.where(valid[None, :, None, :], score, -1.0)
    top_val, top_idx = lax.top_k(score, n_sel)
    sel_ok = top_val >= 0.0
    idx = top_idx.transpose(0, 2, 1, 3)
    bi = jnp.arange(B)[:, None, None, None]
    gi = jnp.arange(N_KV)[None, :, None, None]
    kg = k_blk[bi, gi, idx].reshape(B, N_KV, Tq, n_sel * SLC_BLOCK, HEAD_DIM)
    vg = v_blk[bi, gi, idx].reshape(B, N_KV, Tq, n_sel * SLC_BLOCK, HEAD_DIM)
    s_s = jnp.einsum('bqgrd,bgqkd->bqgrk', q, kg) * scale
    kpos = top_idx[..., None] * SLC_BLOCK + jnp.arange(SLC_BLOCK)
    mask_s = ((kpos <= qpos[None, :, None, None, None]) & sel_ok[..., None]).reshape(B, Tq, N_KV, n_sel * SLC_BLOCK)
    p_s = _masked_probs(s_s, mask_s[:, :, :, None, :])
    o_s = jnp.einsum('bqgrk,bgqkd->bqgrd', p_s.astype(vg.dtype), vg)
    s_w = jnp.einsum('bqgrd,bkgd->bqgrk', q, k_win) * scale
    dist = qpos[:, None] - kwpos[None, :]
    mask_w = ((dist >= 0) & (dist < WINDOW) & (kwpos[None, :] >= 0))[None, :, None, None, :]
    p_w = _masked_probs(s_w, mask_w)
    o_w = jnp.einsum('bqgrk,bkgd->bqgrd', p_w.astype(v_win.dtype), v_win)
    return gates[..., 0:1] * o_c + gates[..., 1:2] * o_s + gates[..., 2:3] * o_w

def _nsa_prompt(q, kc, vc, ks, vs, kw, vw, gates, cmp_k, cmp_v):
    B, T = q.shape[:2]
    k_cmp = _compress(kc, *cmp_k)
    v_cmp = _compress(vc, *cmp_v)
    k_blk = _to_blocks(ks)
    v_blk = _to_blocks(vs)
    overlap = _overlap(k_cmp.shape[1], k_blk.shape[2])
    pad = ((0, 0), (WINDOW, 0), (0, 0), (0, 0))
    kw_pad = jnp.pad(kw, pad)
    vw_pad = jnp.pad(vw, pad)
    span = WINDOW + Q_BLOCK

    def block(s):
        qpos = s + jnp.arange(Q_BLOCK, dtype=jnp.int32)
        kwpos = s - WINDOW + jnp.arange(span, dtype=jnp.int32)
        return _nsa_core(lax.dynamic_slice_in_dim(q, s, Q_BLOCK, 1), qpos, k_cmp, v_cmp, k_blk, v_blk, overlap,
                         lax.dynamic_slice_in_dim(kw_pad, s, span, 1), lax.dynamic_slice_in_dim(vw_pad, s, span, 1),
                         kwpos, lax.dynamic_slice_in_dim(gates, s, Q_BLOCK, 1))

    starts = jnp.arange(T // Q_BLOCK, dtype=jnp.int32) * Q_BLOCK
    out = lax.map(block, starts)
    return jnp.moveaxis(out, 0, 1).reshape(B, T, ATT_DIM)

def _merge(x, ya, za, yb, zb, g_mix, p_i, w_out_a, w_out_b, w_o, w_ple, w_ple_gate):
    br_a = jnp.einsum('btc,cd->btd', jax.nn.silu(za) * ya, w_out_a)
    br_b = jnp.einsum('btc,cd->btd', jax.nn.silu(zb) * yb, w_out_b)
    g_a, g_b = jnp.split(jax.nn.sigmoid(g_mix), 2, axis=-1)
    x = x + jnp.einsum('btd,de->bte', g_a * br_a + g_b * br_b, w_o)
    gate = jax.nn.sigmoid(jnp.einsum('btd,de->bte', x, w_ple_gate))
    return x + gate * jnp.einsum('btp,pd->btd', p_i, w_ple)

def setup_inputs(seed: int = 0) -> dict:
    key = jax.random.key(seed)
    ks = jax.random.split(key, 24)
    n_pages = PAST_LEN // PAGE_SIZE
    n_pool = (DEC_BATCH * n_pages * 5) // 4
    w_buf = min(WINDOW, PAST_LEN)

    def nrm(k, shape, scale):
        return jax.random.normal(k, shape, jnp.float32) * scale

    page_table = jax.random.permutation(ks[5], n_pool)[:DEC_BATCH * n_pages].reshape(DEC_BATCH, n_pages).astype(jnp.int32)
    return {
        "x_prompt": nrm(ks[0], (BATCH, SEQ, D_MODEL), 1.0),
        "x_sample": nrm(ks[1], (DEC_BATCH, DEC_SEQ, D_MODEL), 1.0),
        "cache_kv": nrm(ks[2], (DEPTH, n_pool, PAGE_SIZE, N_KV_SLOTS, N_KV, HEAD_DIM), 1.0),
        "state_win": nrm(ks[3], (DEPTH, DEC_BATCH, w_buf, 2, N_KV, HEAD_DIM), 1.0),
        "state_conv": nrm(ks[4], (DEPTH, DEC_BATCH, CONV_W - 1, CONV_DIM), 1.0),
        "page_table": page_table,
        "p_prompt": nrm(ks[6], (DEPTH, BATCH, SEQ, PLE_DIM), 1.0),
        "p_sample": nrm(ks[7], (DEPTH, DEC_BATCH, DEC_SEQ, PLE_DIM), 1.0),
        "ln_g": 1.0 + nrm(ks[8], (DEPTH, D_MODEL), 0.05),
        "w_in": nrm(ks[9], (DEPTH, D_MODEL, IN_COLS), D_MODEL ** -0.5),
        "conv_w": nrm(ks[10], (DEPTH, CONV_W, CONV_DIM), CONV_W ** -0.5),
        "cmp_pos_k": nrm(ks[11], (DEPTH, CMP_BLOCK, HEAD_DIM), 0.1),
        "cmp_w1_k": nrm(ks[12], (DEPTH, CMP_BLOCK, HEAD_DIM, CMP_HID), (CMP_BLOCK * HEAD_DIM) ** -0.5),
        "cmp_w2_k": nrm(ks[13], (DEPTH, CMP_HID, HEAD_DIM), CMP_HID ** -0.5),
        "cmp_pos_v": nrm(ks[14], (DEPTH, CMP_BLOCK, HEAD_DIM), 0.1),
        "cmp_w1_v": nrm(ks[15], (DEPTH, CMP_BLOCK, HEAD_DIM, CMP_HID), (CMP_BLOCK * HEAD_DIM) ** -0.5),
        "cmp_w2_v": nrm(ks[16], (DEPTH, CMP_HID, HEAD_DIM), CMP_HID ** -0.5),
        "w_out_a": nrm(ks[17], (DEPTH, CONV_DIM, D_MODEL), CONV_DIM ** -0.5),
        "w_out_b": nrm(ks[18], (DEPTH, ATT_DIM, D_MODEL), ATT_DIM ** -0.5),
        "w_o": nrm(ks[19], (DEPTH, D_MODEL, D_MODEL), D_MODEL ** -0.5),
        "w_ple": nrm(ks[20], (DEPTH, PLE_DIM, D_MODEL), PLE_DIM ** -0.5),
        "w_ple_gate": nrm(ks[21], (DEPTH, D_MODEL, D_MODEL), D_MODEL ** -0.5),
        "final_g": 1.0 + nrm(ks[22], (D_MODEL,), 0.05),
    }

def reference(x_prompt, x_sample, cache_kv, state_win, state_conv, page_table, p_prompt, p_sample,
              ln_g, w_in, conv_w, cmp_pos_k, cmp_w1_k, cmp_w2_k, cmp_pos_v, cmp_w1_v, cmp_w2_v,
              w_out_a, w_out_b, w_o, w_ple, w_ple_gate, final_g):
    n_dec, dec_len = x_sample.shape[0], x_sample.shape[1]
    past_len = page_table.shape[1] * PAGE_SIZE
    w_buf = state_win.shape[2]
    pos_p = jnp.arange(x_prompt.shape[1], dtype=jnp.int32)
    pos_s = past_len + jnp.arange(dec_len, dtype=jnp.int32)
    kwpos_s = past_len - w_buf + jnp.arange(w_buf + dec_len, dtype=jnp.int32)
    w_keep_p = min(WINDOW, x_prompt.shape[1])
    xp, xs = x_prompt, x_sample
    kv_p, kv_s, win_p, win_s, conv_p, conv_s = [], [], [], [], [], []
    for i in range(DEPTH):
        cmp_k = (cmp_pos_k[i], cmp_w1_k[i], cmp_w2_k[i])
        cmp_v = (cmp_pos_v[i], cmp_w1_v[i], cmp_w2_v[i])
        merge_w = (w_out_a[i], w_out_b[i], w_o[i], w_ple[i], w_ple_gate[i])
        ba, ca, xa, za, q, kc, vc, ks, vs, kw, vw, gbr, zb, gmix = _project(xp, pos_p, ln_g[i], w_in[i])
        u = ca * xa
        conv_y, tail = _short_conv(u, jnp.zeros_like(u[:, :CONV_W - 1]), conv_w[i])
        yb = _nsa_prompt(q, kc, vc, ks, vs, kw, vw, gbr, cmp_k, cmp_v)
        xp = _merge(xp, ba * conv_y, za, yb, zb, gmix, p_prompt[i], *merge_w)
        kv_p.append(jnp.stack([kc, vc, ks, vs], axis=2))
        win_p.append(jnp.stack([kw, vw], axis=2)[:, -w_keep_p:])
        conv_p.append(tail)
        ba, ca, xa, za, q, kc, vc, ks, vs, kw, vw, gbr, zb, gmix = _project(xs, pos_s, ln_g[i], w_in[i])
        u = ca * xa
        conv_y, tail = _short_conv(u, state_conv[i], conv_w[i])
        new_kv = jnp.stack([kc, vc, ks, vs], axis=2)
        past = cache_kv[i][page_table].reshape(n_dec, past_len, N_KV_SLOTS, N_KV, HEAD_DIM)
        full = jnp.concatenate([past, new_kv], axis=1)
        win = jnp.concatenate([state_win[i], jnp.stack([kw, vw], axis=2)], axis=1)
        k_cmp = _compress(full[:, :, 0], *cmp_k)
        v_cmp = _compress(full[:, :, 1], *cmp_v)
        k_blk = _to_blocks(full[:, :, 2])
        v_blk = _to_blocks(full[:, :, 3])
        overlap = _overlap(k_cmp.shape[1], k_blk.shape[2])
        yb = _nsa_core(q, pos_s, k_cmp, v_cmp, k_blk, v_blk, overlap, win[:, :, 0], win[:, :, 1], kwpos_s, gbr)
        yb = yb.reshape(n_dec, dec_len, ATT_DIM)
        xs = _merge(xs, ba * conv_y, za, yb, zb, gmix, p_sample[i], *merge_w)
        kv_s.append(new_kv)
        win_s.append(win[:, -w_buf:])
        conv_s.append(tail)
    y_prompt = _rms_norm(xp, final_g)
    y_sample = _rms_norm(xs, final_g)
    return (y_prompt, y_sample, jnp.stack(kv_p), jnp.stack(kv_s), jnp.stack(win_p), jnp.stack(win_s), jnp.stack(conv_p), jnp.stack(conv_s))


_drawn_inputs = setup_inputs


def setup_inputs(seed=0):
    import zlib

    import numpy as np

    out = dict(_drawn_inputs(seed))
    spreads = {}
    factors = {'cache_kv': 2.779,
     'cmp_pos_k': 8.0,
     'cmp_w1_k': 3.168,
     'cmp_w2_k': 3.153,
     'cmp_pos_v': 5.628}
    for name, (base, spread) in spreads.items():
        noise = np.random.default_rng([zlib.crc32(name.encode()), seed]).standard_normal(out[name].shape)
        drawn = base * np.exp(spread * noise) if base else spread * noise
        out[name] = __import__('jax').numpy.asarray(drawn.astype(out[name].dtype))
    for name, factor in factors.items():
        out[name] = (out[name] * factor).astype(out[name].dtype)
    return out
```

```python
from contextlib import ExitStack

import numpy as np

import concourse.bass as bass
from concourse import mybir

F32 = mybir.dt.float32
F32R = mybir.dt.float32r
I32 = mybir.dt.int32
ALU = mybir.AluOpType
ACT = mybir.ActivationFunctionType
AX = mybir.AxisListType
ds = bass.ds

P = 128
D = 1024
NL = 2
SEQ = 512
NSEQ, TS = 8, 4
NSAM = NSEQ * TS
TOK = SEQ + NSAM
HALF = TOK // 2
KT = D // P
NT = SEQ // P
HD = 64
GROUPS, REP = 4, 4
KV = GROUPS * HD
PAGE = 128
NPAGE = 8
PAST = PAGE * NPAGE
WIN = 512
PLE = 256
HC = 8
NWP = SEQ // 16 - 1
NWS = PAST // 16 - 1
HID = 256
SCALE = HD ** -0.5
NEG = -1e30
LOWEST = -1e29
EPS = 1e-6

C_BA, C_CA, C_XA, C_ZA, C_Q = 0, D, 2 * D, 3 * D, 4 * D
N_TM = D + 6 * KV + 48
C_ZB = C_Q + N_TM
C_MIX = C_ZB + D
IN_COLS = C_MIX + 2 * D
N_KVG = 6 * KV + 48
Z_KC, Z_VC, Z_KS, Z_VS, Z_KW, Z_VW, Z_G = (i * KV for i in range(7))
BW = 256
WW = 264
NQB, NKB = D // BW, N_KVG // WW
TM_BLOCKS = NQB + NKB
assert NKB * WW == N_KVG

B_CONV = 0
B_MA = 16
B_TM = 24
B_ZB = 34
B_MB = 38
B_WO = 46
B_PL = 50
NB = 58
PH = 15
C_IN = (2 * 256, 2 * 256 + 80)

def _const_layout():
    at, out = 0, {}
    for name, n in (("ident", P), ("ones", P), ("cos", 5 * 32), ("sin", 5 * 32), ("causal", P),
                    ("cmask", NT * 32), ("wmask", WIN), ("nmask", 4 * NSAM), ("gmask", 48), ("same", P),
                    ("iota", 16), ("pick", 4 * P), ("eps", 1)):
        out[name] = (at, n)
        at += n
    return out, at


CONST, NCONST = _const_layout()


def constants():
    c = np.zeros((P, NCONST), np.float32)

    def put(name, a):
        at, n = CONST[name]
        c[: a.shape[0], at:at + n] = a.reshape(a.shape[0], n)

    put("ident", np.eye(P, dtype=np.float32))
    put("ones", np.ones((P, P), np.float32))
    inv = np.power(10000.0, -np.arange(32) / 32).astype(np.float32)
    pos = np.concatenate([np.arange(SEQ), np.tile(PAST + np.arange(TS), NSEQ), np.zeros(P - NSAM)]).astype(np.float32)
    ang = (pos[:, None] * inv[None, :]).astype(np.float32).reshape(5, P, 32).transpose(1, 0, 2)
    put("cos", np.cos(ang))
    put("sin", np.sin(ang))
    q = np.arange(P)
    put("causal", np.where(q[:, None] >= q[None, :], 0.0, NEG).astype(np.float32))
    n = np.arange(32)
    qq = q[:, None, None] + P * np.arange(NT)[None, :, None]
    put("cmask", np.where((16 * n[None, None, :] + 31 <= qq) & (n < NWP)[None, None, :], 0.0, NEG).astype(np.float32))
    s2, g, t, r = np.unravel_index(q, (2, GROUPS, TS, REP))
    k, p = np.unravel_index(np.arange(WIN), (4, P))
    put("wmask", np.where((4 * p + k)[None, :] > t[:, None], 0.0, NEG).astype(np.float32))
    tok = np.arange(NSAM)
    nm = [np.where((tok[None, :] // TS == (2 * pair + s2)[:, None]) & (tok[None, :] % TS <= t[:, None]), 0.0, NEG)
          for pair in range(4)]
    put("nmask", np.stack(nm, 1).astype(np.float32))
    gr = np.arange(16)
    put("gmask", np.repeat((gr[None, :] == (g * REP + r)[:, None]).astype(np.float32)[:, :, None], 3, 2))
    key = (s2 * GROUPS + g) * TS + t
    put("same", (key[:, None] == key[None, :]).astype(np.float32))
    put("iota", np.tile(np.arange(16, dtype=np.float32), (P, 1)))
    pick = np.stack([(tok[:, None] == ((2 * pair + s2) * TS + t)[None, :]) for pair in range(4)], 1)
    put("pick", pick.astype(np.float32))
    put("eps", np.full((P, 1), EPS, np.float32))
    return c


def build(nc, a):
    ctx = ExitStack()
    with ctx:
        sems = []

        def sem(name, head_start=0):
            handle = ctx.enter_context(nc.semaphore(name))
            sems.append((handle, head_start))
            return handle

        def nth(semaphore, n):
            return n + sum(head for handle, head in sems if handle is semaphore)

        base = [16512]

        def fixed(name, shape, dt=F32):
            t = nc.alloc_sbuf_tensor_at(name, shape, dt, offset=base[0])
            base[0] += (4 * int(np.prod(shape[1:])) + 31) // 32 * 32
            return t

        xT = fixed("xT", [P, KT, TOK])
        m = fixed("m", [P, KT, TOK])
        rstd = fixed("rstd", [P, TOK])
        con = fixed("con", [P, NCONST])
        cols = fixed("cols", [P, KT, 21])
        qs = fixed("qs", [P, 2, 2, P])
        kcT_s = fixed("kcT_s", [P, 2, NSEQ, 64])
        kcT_p = fixed("kcT_p", [P, 2, 32])
        vc_s = fixed("vc_s", [64, NSEQ * KV])
        vc_p = fixed("vc_p", [P, KV])
        knT = fixed("knT", [P, 4, NSAM])
        qsT = fixed("qsT", [P, KT, NSAM])
        hb = fixed("hb", [P, 2])
        small = fixed("small", [P, 128])
        grow = fixed("grow", [P, 4, 3])
        pages = fixed("pages", [1, NSEQ * NPAGE], I32)
        tails = fixed("tails", [P, KT, 18])
        cst = fixed("cst", [P, 2, 21])
        D0 = base[0]

        def at(name, shape, off, dt=F32):
            return nc.alloc_sbuf_tensor_at(name, shape, dt, offset=D0 + off)

        R_Z, R_A, R_T = 86272, 103680, 138496
        w_raw = at("w_raw", [P, 2, KT, WW], 0)
        wH = at("wH", [P, 2, KT, WW], 17152, F32R)
        wL = at("wL", [P, 2, KT, WW], 34304, F32R)
        hH = at("hH", [P, KT, TOK], 51456, F32R)
        hL = at("hL", [P, KT, TOK], 68864, F32R)
        zq = at("zq", [P, 5, D], R_Z)
        zk = at("zk", [P, 5, N_KVG], R_Z + 20480)
        aH = at("aH", [P, KT, TOK], R_A, F32R)
        aL = at("aL", [P, KT, TOK], R_A + 17408, F32R)
        yT = at("yT", [P, KT, TOK], R_Z)
        xin = at("xin", [P, 5, D], R_Z)
        cv_in = at("cv_in", [P, 4, 2, TOK], R_Z)
        UW = SEQ + 2 + NSEQ * 6
        cv_u = at("cv_u", [P, 2, UW], R_T)
        cv_y = at("cv_y", [P, UW], R_T + -(-2 * UW * 4 // 32) * 32)
        sq = at("sq", [P, 2, TOK], R_T)
        rows21 = at("rows21", [21, D], R_A)
        tail_rows = at("tail_rows", [18, D], R_T + 2048)
        rope_a = at("rope_a", [P, 2, 256], R_T)
        w1H = at("w1H", [P, 16, HID], 0, F32R)
        w1L = at("w1L", [P, 16, HID], 16384, F32R)
        chH = at("chH", [P, 2, 2, P, GROUPS], 32768, F32R)
        chL = at("chL", [P, 2, 2, P, GROUPS], 40960, F32R)
        craw = at("craw", [P, 2, 2, HC, KV], 49152)
        hidT = at("hidT", [P, 2, 504], 81920)
        hsg = at("hsg", [P, 2, 504], R_T)
        w2 = at("w2", [P, 2, HD], R_T + 4032)
        qT = at("qT", [P, KT, SEQ], 0)
        kT = at("kT", [P, 2, 2, SEQ], 16384)
        pr = at("pr", [P, 2, 4, SEQ], 24576)
        prT = at("prT", [P, 2, 4, SEQ], 40960)
        qst = at("qst", [P, SEQ], 57344)
        cs = at("cs", [P, 8, 32], 59392)
        cT = at("cT", [P, 2, P], 60416)
        ow = at("ow", [P, 6, HD], 61440)
        yy = at("yy", [P, 2, P], 62976)
        skv = at("skv", [P, 2, 2, HC, 2 * KV], 0)
        swin = at("swin", [P, 2, 4, 2 * KV], 65536)
        R_S = R_Z + 20480
        skT = at("skT", [P, 2, 512], 81920)
        ssel = at("ssel", [P, PAST + NSAM], R_S)
        swsc = at("swsc", [P, WIN + NSAM], R_S + 4224)
        spT = at("spT", [P, 16, P], R_S + 6400)
        pc = at("pc", [P, 64], R_S + 14592)
        sy = at("sy", [P, KV], R_S + 14848)
        vcst = at("vcst", [64, 2 * KV], R_S + 15872)
        assert 15872 + 2048 <= 4 * N_KVG * 4
        t_f = at("t_f", [P, 2, TOK], R_T)
        pin = at("pin", [P, 5, PLE], R_Z)
        pH = at("pH", [P, 2, TOK], R_Z + 5120, F32R)
        pL = at("pL", [P, 2, TOK], R_Z + 9472, F32R)
        out_rows = at("out_rows", [P, 5, D], R_Z)

        ps = ctx.enter_context(nc.psum_tensor("ps", [P, 8, 512], F32))

        def C(name, rows=P):
            o, n = CONST[name]
            return con[0:rows, o:o + n]

        ident = C("ident")

        s_const, s_x, s_zero = sem("s_const"), sem("s_x"), sem("s_zero")
        passed = sem("passed")
        phase = sem("phase")
        w_in_sem = [sem("w_loaded0"), sem("w_loaded1")]
        w_hi = sem("w_hi")
        w_lo = sem("w_lo", 2)
        w_done = sem("w_done", 2)
        x_tp, x_free = sem("x_tp"), sem("x_free", 4)
        sq_ready, sq_used, ss_ready, std_ready = sem("sq_ready"), sem("sq_used", 2), sem("ss_ready"), sem("std_ready")
        st_in, st_tp = sem("st_in"), sem("st_tp")
        h_f, h_hi = sem("h_f"), sem("h_hi")
        cv, cv_act, cv_sg, cv_dve = sem("cv"), sem("cv_act", 8), sem("cv_sg"), sem("cv_dve", 8)
        cv_f, cv_hi, cv_used = sem("cv_f"), sem("cv_hi"), sem("cv_used", 2)
        mg, mg_sg, mg_dve = sem("mg"), sem("mg_sg"), sem("mg_dve", 4)
        tail_tp, tail_cp, tail_out = sem("tail_tp"), sem("tail_cp"), sem("tail_out")
        tm, tm_ev = sem("tm"), sem("tm_ev", 5)
        z_ready, kv_out = sem("z_ready"), sem("kv_out")
        pg_in, w1_in, w1_hi, w1_lo = sem("pg_in"), sem("w1_in"), sem("w1_hi"), sem("w1_lo")
        c_in = [sem("chunks_loaded0"), sem("chunks_loaded1")]
        c_free = sem("c_free", 2)
        c_tp, c_hi, c_lo, c_mm = sem("c_tp"), sem("c_hi"), sem("c_lo", 4), sem("c_mm", 2)
        c_acc, c_sg, c_hid, c_w2, c_out = sem("c_acc"), sem("c_sg"), sem("c_hid", 2), sem("c_w2", 1), sem("c_out", 1)
        tp = [sem("tp_even"), sem("tp_odd")]
        tp_free = [sem("tp_even_free", 4), sem("tp_odd_free", 4)]
        pa_q, pa_qfree = sem("pa_q"), sem("pa_qfree", 1)
        pa_c, pa_csc, pa_cexp, pa_cn, pa_ct, pa_ctev = (sem(n) for n in ("pa_c", "pa_csc", "pa_cexp", "pa_cn", "pa_ct", "pa_ctev"))
        pos_ready = sem("pos_ready")
        pa_s, pa_nm, pa_exp = sem("pa_s"), sem("pa_nm"), sem("pa_exp", 1)
        pa_t, pa_te, pa_pv, pa_o, pa_y = sem("pa_t"), sem("pa_te", 4), sem("pa_pv", 2), sem("pa_o", 2), sem("pa_y")
        s_kv = [sem("s_kv0"), sem("s_kv1")]
        s_win, s_winout, s_fin = sem("s_win"), sem("s_winout"), sem("s_fin", 2)
        sa_g, sa_gr, sa_q, sa_c, sa_nm, sa_cx = (sem(n) for n in ("sa_g", "sa_gr", "sa_q", "sa_c", "sa_nm", "sa_cx"))
        sa_kt, sa_ke, sa_s = sem("sa_kt"), sem("sa_ke", 2), sem("sa_s", 2)
        sa_im, sa_imp, sa_m, sa_e, sa_t, sa_te = (sem(n) for n in ("sa_im", "sa_imp", "sa_m", "sa_e", "sa_t", "sa_te"))
        sa_o, sa_y, sa_yt, sa_ys = (sem(n) for n in ("sa_o", "sa_y", "sa_yt", "sa_ys"))
        zb, zb_sg, zb_f, zb_hi, zb_done = sem("zb"), sem("zb_sg"), sem("zb_f"), sem("zb_hi"), sem("zb_done", 4)
        wo, wo_done = sem("wo"), sem("wo_done", 4)
        sp_hi, p_in, p_tp, p_hi = sem("sp_hi"), sem("p_in"), sem("p_tp"), sem("p_hi")
        pl, pl_sg, pl_done = sem("pl"), sem("pl_sg"), sem("pl_done", 2)
        y_ready, y_tp, y_act, y_dve, out_done = sem("y_ready"), sem("y_tp"), sem("y_act", 4), sem("y_dve", 4), sem("out_done")

        def phase_over(eng, l, k):
            eng.wait_ge(phase, 3 * (l * PH + k + 2))
            eng.sem_inc(passed, 1)

        def end_phase(eng, l, k):
            eng.drain().then_inc(phase, 1)
            phase_over(eng, l, k)

        def make_high(act, l, b, par, nk=KT, width=BW):
            act.wait_ge(w_in_sem[par], 64 * (l * (NB // 2) + b // 2 + 1 if isinstance(b, int) else l * (NB // 2) + b[1] + 1))
            act.wait_ge(w_done, nth(w_done, l * NB + blk(b) - 1))
            act.activation(wH[:, par, 0:nk, 0:width], w_raw[:, par, 0:nk, 0:width], ACT.Copy).then_inc(w_hi, 1)

        def make_low(dve, l, b, par, nk=KT, width=BW):
            dve.wait_ge(w_hi, l * NB + blk(b) + 1)
            dve.tensor_tensor(wL[:, par, 0:nk, 0:width], w_raw[:, par, 0:nk, 0:width],
                              wH[:, par, 0:nk, 0:width].bitcast(F32), ALU.subtract).then_inc(w_lo, 1)

        def blk(b):
            return b if isinstance(b, int) else 2 * b[1] + b[2]

        def pb(base_block, half, odd):
            return ("b", base_block // 2 + half, odd)

        def two(t, c):
            return t[:].rearrange("p k t -> p (k t)")[:, ds(c * TOK, TOK)].rearrange("p (a b) -> p a b", a=2)

        def one(t, c):
            return t[:].rearrange("p k t -> p (k t)")[:, ds(c * TOK, TOK)]

        def bank2(n):
            return ps[:, n:n + 2, 0:HALF]

        def halves(t):
            return t.rearrange("p (a b) -> p a b", a=2)

        block = ctx.enter_context(nc.Block())

        @block.sync
        def _(sp):
            sp.dma_start(con[:], a["consts"]).then_inc(s_const, 16)
            sp.dma_start(pages[:], a["page_table"].rearrange("(o a) b -> o (a b)", o=1)).then_inc(pg_in, 16)
            sp.dma_start(xin[:, 0:NT, :], a["x_prompt"].rearrange("b (t p) d -> p (b t) d", p=P)).then_inc(s_x, 16)
            sp.dma_start(xin[0:NSAM, NT, :], a["x_sample"].rearrange("b t d -> (b t) d")).then_inc(s_x, 16)
            sp.wait_ge(pg_in, 16)
            sp.wait_ge(s_zero, 1)

            def load_w(l, b, par, src, nk=KT, width=BW):
                sp.wait_ge(w_lo, nth(w_lo, l * NB + b - 1))
                sp.dma_start(w_raw[:, par, 0:nk, 0:width], src).then_inc(w_in_sem[par], 64)

            def w_cols(name, l, col, width=BW):
                w = a[name][ds(l, 1)].rearrange("l (k p) c -> p (l k) c", p=P)
                return w[:, :, ds(col, width)]

            def page_rows(l, seq, j, first, n):
                page = sp.value_load(pages[0:1, ds(seq * NPAGE + j, 1)], min_val=0, max_val=a["cache_kv"].shape[1] - 1)
                return a["cache_kv"][ds(l, 1), ds(page, 1), :, first:first + n].rearrange("l o (c t) s g d -> c (l o t) (s g d)", t=HC)

            with sp.Fori(0, NL) as l:
                phase_over(sp, l, -1)
                sp.dma_start(rows21[0:16, :], a["state_conv"][ds(l, 1)].rearrange("l b t c -> (l b t) c")).then_inc(st_in, 16)
                sp.dma_start(rows21[16:19, :], a["conv_w"][ds(l, 1)].rearrange("l t c -> (l t) c")).then_inc(st_in, 16)
                sp.dma_start(rows21[19:20, :], a["ln_g"][ds(l, 1)]).then_inc(st_in, 16)
                sp.dma_start(rows21[20:21, :], a["final_g"].rearrange("(o d) -> o d", o=1)).then_inc(st_in, 16)
                with sp.Fori(0, 4) as i:
                    for n, c0 in enumerate((C_CA, C_XA, C_BA, C_ZA)):
                        load_w(l, B_CONV + 4 * i + n, n % 2, w_cols("w_in", l, c0 + BW * i))
                with sp.Fori(0, 4) as i:
                    load_w(l, B_MA + 2 * i, 0, w_cols("w_in", l, C_MIX + BW * i))
                    load_w(l, B_MA + 2 * i + 1, 1, w_cols("w_out_a", l, BW * i))
                with sp.Fori(0, NQB // 2) as i:
                    for n in range(2):
                        load_w(l, B_TM + 2 * i + n, n, w_cols("w_in", l, 2 * BW * i + C_Q + n * BW, WW), width=WW)
                with sp.Fori(0, NKB // 2) as i:
                    for n in range(2):
                        load_w(l, B_TM + NQB + 2 * i + n, n, w_cols("w_in", l, 2 * WW * i + C_Q + D + n * WW, WW), width=WW)
                sp.wait_ge(z_ready, l + 1)
                sp.dma_start(a["new_kv_prompt"][ds(l, 1)].rearrange("l b (t p) s g d -> p (l b t) (s g d)", p=P),
                             zk[:, 0:NT, 0:4 * KV]).then_inc(kv_out, 16)
                sp.dma_start(a["new_win_prompt"][ds(l, 1)].rearrange("l b (t p) s g d -> p (l b t) (s g d)", p=P),
                             zk[:, 0:NT, Z_KW:Z_KW + 2 * KV]).then_inc(kv_out, 16)
                sp.dma_start(a["new_kv_sample"][ds(l, 1)].rearrange("l b t s g d -> (l b t) (s g d)"),
                             zk[0:NSAM, NT, 0:4 * KV]).then_inc(kv_out, 16)
                sp.dma_start(a["new_win_sample"][ds(l, 1), :, WIN - TS:WIN].rearrange("l b t s g d -> (l b) t (s g d)"),
                             zk[0:NSAM, NT, Z_KW:Z_KW + 2 * KV]).then_inc(kv_out, 16)
                sp.wait_ge(kv_out, 64 * l + 64)

                for kv, (w1, w2n, pos) in enumerate((("cmp_w1_k", "cmp_w2_k", "cmp_pos_k"), ("cmp_w1_v", "cmp_w2_v", "cmp_pos_v"))):
                    phase_over(sp, l, 3 + kv)
                    sp.dma_start(craw[:, 0].rearrange("p s t c -> p (s t c)").rearrange("p (k h) -> p k h", k=16),
                                 a[w1][ds(l, 1)].rearrange("l (k s) d h -> (s d) (l k) h", s=2)).then_inc(w1_in, 16)
                    sp.dma_start(w2[:], a[w2n][ds(l, 1)].rearrange("l (k p) d -> p (l k) d", p=P)).then_inc(w1_in, 16)
                    sp.dma_start(craw[0:64, 1, 0],
                                 a["new_kv_prompt"][ds(l, 1), :, :, kv].rearrange("l b (c t) g d -> c (l b t) (g d)", t=HC)).then_inc(c_in[1], 16)
                    for g in range(GROUPS):
                        sp.dma_start(craw[64:68, 1, 0, :, g * HD:(g + 1) * HD],
                                     a[pos][ds(l, 1)].rearrange("l (c t) d -> (l c) t d", t=HC)).then_inc(c_in[1], 16)
                    sp.wait_ge(w1_lo, 2 * l + kv + 1)
                    sp.sem_inc(passed, 1)
                    with sp.Fori(0, 2) as pp:
                        for par in range(2):
                            sp.wait_ge(c_free, nth(c_free, 10 * l + 2 * pp + (kv * 5 + par)))
                            for s in range(2):
                                for j in range(NPAGE):
                                    src = page_rows(l, 4 * pp + (2 * par + s), j, kv, 1)
                                    sp.dma_start(craw[16 * j:16 * j + 16, par, s], src).then_inc(c_in[par], 16)

                phase_over(sp, l, 7)
                with sp.Fori(0, 2) as pp:
                    for par in range(2):
                        sp.wait_ge(s_fin, nth(s_fin, 4 * l + 2 * pp + (par - 1)))
                        for s in range(2):
                            for j in range(NPAGE):
                                src = page_rows(l, 4 * pp + (2 * par + s), j, 2, 2)
                                sp.dma_start(skv[16 * j:16 * j + 16, par, s], src).then_inc(s_kv[par], 16)

                phase_over(sp, l, 8)
                with sp.Fori(0, 2) as gp:
                    for n in range(2):
                        sp.wait_ge(w_lo, nth(w_lo, l * NB + 2 * gp + (B_ZB + n - 1)))
                        src = w_cols("w_in", l, 512 * gp + C_ZB, 512)
                        for g in range(2):
                            for jj in range(2):
                                to, frm = jj * P + g * HD, g * KV + (2 * n + jj) * HD
                                sp.dma_start(w_raw[:, n, :, to:to + HD], src[:, :, frm:frm + HD]).then_inc(w_in_sem[n], 16)
                with sp.Fori(0, 4) as i:
                    load_w(l, B_MB + 2 * i, 0, w_cols("w_in", l, BW * i + (C_MIX + D)))
                    sp.wait_ge(w_lo, nth(w_lo, l * NB + 2 * i + B_MB))
                    for g in range(2):
                        for gp in range(2):
                            rows = a["w_out_b"][ds(l, 1), 512 * gp + KV * g:512 * gp + KV * g + KV].rearrange("l (c d) n -> d (l c) n", d=HD)
                            sp.dma_start(w_raw[g * 64:(g + 1) * 64, 1, 4 * gp:4 * gp + 4, 0:BW], rows[:, :, ds(BW * i, BW)]).then_inc(w_in_sem[1], 16)
                with sp.Fori(0, 2) as i:
                    for n in range(2):
                        load_w(l, B_WO + 2 * i + n, n, w_cols("w_o", l, 2 * BW * i + BW * n))
                with sp.Fori(0, 4) as i:
                    load_w(l, B_PL + 2 * i, 0, w_cols("w_ple_gate", l, BW * i))
                    load_w(l, B_PL + 2 * i + 1, 1, w_cols("w_ple", l, BW * i), nk=2)

            for tt in range(5):
                sp.wait_ge(y_act, nth(y_act, tt + 1))
                sp.wait_ge(y_dve, nth(y_dve, tt + 1))
                if tt < NT:
                    sp.dma_start(a["y_prompt"][0, tt * P:(tt + 1) * P, :], out_rows[:, tt, :]).then_inc(out_done, 16)
                else:
                    sp.dma_start(a["y_sample"].rearrange("b t d -> (b t) d"), out_rows[0:NSAM, tt, :]).then_inc(out_done, 16)
            sp.wait_ge(out_done, 80)

        @block.gpsimd
        def _(pool):
            for handle, head_start in sems:
                if head_start:
                    pool.sem_inc(handle, head_start)
            pool.memset(qs[:], 0.0)
            pool.memset(vc_p[:], 0.0)
            pool.memset(kcT_p[:], 0.0)
            pool.memset(small[:], 0.0)
            pool.drain()
            pool.memset(small[:, 24:30], 1.0)
            pool.memset(small[:, 76:79], 1.0)
            pool.drain().then_inc(s_zero, 1)
            with pool.Fori(0, NL) as l:
                pool.wait_ge(tail_cp, 2 * l + 2)
                pool.dma_start(a["new_conv_prompt"][ds(l, 1)].rearrange("l b t c -> (l b t) c"), tail_rows[0:2, :]).then_inc(tail_out, 16)
                pool.dma_start(a["new_conv_sample"][ds(l, 1)].rearrange("l b t c -> (l b t) c"), tail_rows[2:18, :]).then_inc(tail_out, 16)
                pool.wait_ge(tail_out, 32 * l + 32)
                phase_over(pool, l, 7)
                with pool.Fori(0, 4) as pair:
                    pool.wait_ge(s_fin, nth(s_fin, 4 * l + pair))
                    for s in range(2):
                        pool.dma_start(swin[:, s].rearrange("p k c -> p (k c)"),
                                       a["state_win"][ds(l, 1), ds(2 * pair + s, 1)].rearrange("l b (p k) s g d -> (l b p) (k s g d)", k=4)
                                       ).then_inc(s_win, 16)
                    pool.wait_ge(s_win, 128 * l + 32 * pair + 32)
                    pool.sem_inc(passed, 1)
                    for s in range(2):
                        dst = a["new_win_sample"][ds(l, 1), ds(2 * pair + s, 1), 0:WIN - TS].rearrange("l b (p k) s g d -> (l b p) (k s g d)", k=4)
                        for lo, hi in ((1, 113), (113, 128)):
                            pool.dma_start(dst[lo - 1:hi - 1], swin[lo:hi, s].rearrange("p k c -> p (k c)")).then_inc(s_winout, 16)
                    pool.wait_ge(s_winout, 256 * l + 64 * pair + 64)
                phase_over(pool, l, 10)
                pool.dma_start(pin[:, 0:NT, :], a["p_prompt"][ds(l, 1)].rearrange("l b (t p) d -> p (l b t) d", p=P)).then_inc(p_in, 16)
                pool.dma_start(pin[0:NSAM, NT, :], a["p_sample"][ds(l, 1)].rearrange("l b t d -> (l b t) d")).then_inc(p_in, 16)

        @block.tensor
        def _(pe):
            def norm_sum(l):
                for c in range(KT):
                    pe.wait_ge(sq_ready, l * KT + c + 1)
                    for hf in range(2):
                        last = nc.tensor.matmul(ps[:, hf, 0:HALF], C("ones"), sq[:, c % 2, hf * HALF:(hf + 1) * HALF],
                                                start=c == 0, stop=c == KT - 1)
                    last.then_inc(sq_used, 1)
                pe.drain().then_inc(ss_ready, 1)

            def fm_tile(par, jj, bank, xH, xL, nk=KT):
                for k in range(nk):
                    for w, x in ((wH, xH), (wH, xL), (wL, xH)):
                        st = w[:, par, k, jj * P:(jj + 1) * P]
                        for hf in range(2):
                            last = nc.tensor.matmul(ps[:, bank + hf, 0:HALF], st, x[:, k, hf * HALF:(hf + 1) * HALF],
                                                    start=k == 0 and w is wH and x is xH, stop=k == nk - 1 and w is wL)
                return last

            pe.wait_ge(s_const, 16)
            pe.wait_ge(s_x, 32)
            for c in range(KT):
                pe.wait_ge(x_free, nth(x_free, c - 3))
                for tt in range(5):
                    rows = P if tt < NT else NSAM
                    last = nc.tensor.transpose(ps[:, 2 * (c % 4) + tt // NT, (tt % NT) * P:(tt % NT) * P + rows],
                                               xin[0:rows, tt, c * P:(c + 1) * P], ident[0:rows, 0:rows])
                last.then_inc(x_tp, 1)
            end_phase(pe, 0, -1)

            with pe.Fori(0, NL) as l:
                pe.wait_ge(st_in, 64 * l + 64)
                pe.sem_inc(passed, 1)
                for c in range(KT):
                    last = nc.tensor.transpose(ps[:, 2, c * 21:(c + 1) * 21], rows21[:, c * P:(c + 1) * P], ident[0:21, 0:21])
                last.then_inc(st_tp, 1)
                norm_sum(l)
                end_phase(pe, l, 0)
                with pe.Fori(0, 4) as i:
                    for kind in range(4):
                        pe.wait_ge(w_lo, nth(w_lo, l * NB + 4 * i + (B_CONV + kind + 1)))
                        for jj in range(2):
                            q = 2 * kind + jj
                            if kind == 0:
                                pe.wait_ge(cv_act, nth(cv_act, 24 * l + 6 * i + (jj - 1)))
                            elif kind == 1:
                                pe.wait_ge(cv_dve, nth(cv_dve, 8 * l + 2 * i + (jj - 1)))
                            else:
                                pe.wait_ge(cv_act, nth(cv_act, 24 * l + 6 * i + (q - 3)))
                            last = fm_tile(kind % 2, jj, 2 * (q % 4), hH, hL)
                            if jj == 0:
                                last.then_inc(cv, 1)
                        last.then_inc(cv, 1)
                        pe.drain().then_inc(w_done, 1)
                end_phase(pe, l, 1)

                def merge(which, first_block, gate, branch):
                    with pe.Fori(0, 4) as i:
                        for n in range(2):
                            pe.wait_ge(w_lo, nth(w_lo, l * NB + 2 * i + (first_block + n + 1)))
                            for jj in range(2):
                                pe.wait_ge(mg_dve, nth(mg_dve, 16 * l + 2 * i + (8 * which + jj - 1)))
                                last = fm_tile(n, jj, 2 * (2 * n + jj), *(branch if n else gate))
                                last.then_inc(mg, 1)
                            pe.drain().then_inc(w_done, 1)

                merge(0, B_MA, (hH, hL), (aH, aL))
                end_phase(pe, l, 2)
                for c in range(KT):
                    last = nc.tensor.transpose(ps[0:18, 6 + c // 4, (c % 4) * P:(c % 4 + 1) * P], tails[:, c, :], ident)
                last.then_inc(tail_tp, 1)

                def token_major(b, half, n, width):
                    pe.wait_ge(w_lo, nth(w_lo, l * NB + 2 * half + (B_TM + b + n + 1)))
                    for tt in range(5):
                        rows = P if tt < NT else NSAM
                        pe.wait_ge(tm_ev, nth(tm_ev, l * (5 * TM_BLOCKS) + 10 * half + (5 * (b + n) + tt - 4)))
                        for k in range(KT):
                            for w, x in ((wH, hH), (wL, hH), (wH, hL)):
                                last = nc.tensor.matmul(ps[0:rows, tt, 0:width], x[:, k, tt * P:tt * P + rows], w[:, n, k, 0:width],
                                                        start=k == 0 and w is wH and x is hH, stop=k == KT - 1 and x is hL)
                        last.then_inc(tm, 1)
                    pe.drain().then_inc(w_done, 1)

                with pe.Fori(0, NQB // 2) as i:
                    for n in range(2):
                        token_major(0, i, n, BW)
                with pe.Fori(0, NKB // 2) as i:
                    for n in range(2):
                        token_major(NQB, i, n, WW)
                end_phase(pe, l, 3)

                for kv in range(2):
                    pe.wait_ge(w1_lo, 2 * l + (kv + 1))

                    def chunk_tp(unit, j, slot, rows, nseq):
                        for s in range(nseq):
                            pe.wait_ge(c_lo, nth(c_lo, 8 * unit + (2 * j + s - 3)))
                            for g in range(GROUPS):
                                for t in range(2):
                                    last = nc.tensor.matmul(ps[t * HD:(t + 1) * HD, (2 * j + s) % 4, g * P:g * P + rows],
                                                            craw[0:rows, slot, s, 2 * j + t, g * HD:(g + 1) * HD], ident[0:rows, 0:rows],
                                                            start=True, stop=True)
                            last.then_inc(c_tp, 1)
                        if nseq == 1:
                            pe.drain().then_inc(c_tp, 1)

                    def compress(unit, slot, rows, nseq, nwin):
                        chunk_tp(unit, 0, slot, rows, nseq)
                        for j in range(4):
                            if j < 3:
                                chunk_tp(unit, j + 1, slot, rows, nseq)
                            if j == 2:
                                pe.drain().then_inc(c_free, 1)
                            pe.wait_ge(c_lo, nth(c_lo, 8 * unit + (2 * j + 2)))
                            if j == 0:
                                pe.wait_ge(c_hid, nth(c_hid, 2 * unit))
                            for hid in range(2):
                                for quarter in range(4):
                                    for w, x in ((w1H, chH), (w1H, chL), (w1L, chH)):
                                        span = slice(quarter, quarter + 2 * nwin - 1, 2)
                                        rhs = x[:, j % 2, :, span, :] if nseq == 2 else x[:, j % 2, 0, span, :]
                                        last = nc.tensor.matmul(ps[:, 4 + hid, 0:nseq * nwin * GROUPS],
                                                                w[:, 4 * quarter + j, hid * P:(hid + 1) * P], rhs,
                                                                start=j == 0 and quarter == 0 and w is w1H and x is chH,
                                                                stop=j == 3 and quarter == 3 and w is w1L)
                            last.then_inc(c_mm, 1)
                        pe.drain().then_inc(c_acc, 1)

                    def project(unit, nseq, nwin):
                        n = nseq * nwin * GROUPS
                        pe.wait_ge(c_hid, nth(c_hid, 2 * unit + 2))
                        pe.wait_ge(c_out, nth(c_out, unit))
                        if kv == 0:
                            for hid in range(2):
                                last = nc.tensor.matmul(ps[0:HD, 6, 0:n], w2[:, hid, :], hidT[:, hid, 0:n], start=hid == 0, stop=hid == 1)
                        else:
                            for s in range(nseq):
                                for g in range(GROUPS):
                                    first = s * nwin * GROUPS + g
                                    o = (s * GROUPS + g) * HD
                                    for hid in range(2):
                                        last = nc.tensor.matmul(ps[0:nwin, 6, o:o + HD],
                                                                hidT[:, hid, first:first + (nwin - 1) * GROUPS + 1:GROUPS], w2[:, hid, :],
                                                                start=hid == 0, stop=hid == 1)
                        last.then_inc(c_w2, 1)

                    pe.wait_ge(c_in[1], C_IN[1] * (2 * l + kv) + 80)
                    compress(10 * l + 5 * kv, 1, 68, 1, NWP + 2)
                    project(10 * l + 5 * kv, 1, NWP)
                    with pe.Fori(0, 2) as pp:
                        for par in range(2):
                            unit = 10 * l + 2 * pp + (5 * kv + par + 1)
                            if par == 0:
                                pe.wait_ge(c_in[0], C_IN[0] * (2 * l + kv) + 256 * pp + 256)
                            else:
                                pe.wait_ge(c_in[1], C_IN[1] * (2 * l + kv) + 256 * pp + (256 + 80))
                            compress(unit, par, P, 2, NWS)
                            project(unit, 2, NWS)
                    end_phase(pe, l, 4 + kv)

                def tp_job(k, parts):
                    pe.wait_ge(tp_free[k % 2], nth(tp_free[k % 2], 7 * l + (k // 2 - 3)))
                    pe.sem_inc(passed, 1)
                    for out, src, n in parts:
                        last = nc.tensor.transpose(out, src, ident[0:n, 0:n])
                    last.then_inc(tp[k % 2], 1)

                def q_cols(tt, rows, gp, r):
                    return zq[0:rows, tt, (4 * gp + r) * P:(4 * gp + r + 1) * P]

                for k in range(8):
                    tp_job(k, [(ps[:, k % 8, tt * P:(tt + 1) * P], q_cols(tt, P, k // 4, k % 4), P) for tt in range(NT)])
                for k in range(8, 12):
                    c0 = (Z_KS, Z_KW)[(k - 8) // 2] + (k % 2) * P
                    tp_job(k, [(ps[:, k % 8, tt * P:(tt + 1) * P], zk[:, tt, c0:c0 + P], P) for tt in range(NT)])
                tp_job(12, [(ps[:, 4, n * NSAM:(n + 1) * NSAM], q_cols(NT, NSAM, n // 4, n % 4), NSAM) for n in range(8)])
                tp_job(13, [(ps[:, 5, n * NSAM:(n + 1) * NSAM],
                             zk[0:NSAM, NT, (Z_KS, Z_KW)[n // 2] + (n % 2) * P:(Z_KS, Z_KW)[n // 2] + (n % 2 + 1) * P], NSAM) for n in range(4)])
                end_phase(pe, l, 6)

                for gp in range(2):
                    with pe.Fori(0, REP) as r:
                        it = 8 * l + r + 4 * gp

                        def bank_free(k):
                            if k < 2:
                                pe.wait_ge(pa_te, nth(pa_te, 20 * it + (k - 1)))
                            elif k < 4:
                                pe.wait_ge((pa_csc, pa_ctev)[k - 2], it + 1)
                            else:
                                pe.wait_ge(pa_te, nth(pa_te, 20 * it + (k - 3)))
                            return 4 + k % 2

                        def scores(u):
                            pe.wait_ge(pa_exp, nth(pa_exp, 4 * it + u))
                            for g in range(2):
                                rows = slice(64 * g, 64 * g + 64)
                                for br in range(2):
                                    n = P * (u + 1)
                                    last = nc.tensor.matmul(ps[:, 2 * g + br, 0:n], qst[rows, u * P:(u + 1) * P], kT[rows, br, gp, 0:n],
                                                            start=True, stop=True)
                            last.then_inc(pa_s, 1)

                        def y_back(u, k):
                            pe.wait_ge(pa_y, 4 * it + (u + 1))
                            b = bank_free(k)
                            nc.tensor.transpose(ps[:, b, 0:P], yy[:, u % 2, :], ident).then_inc(pa_t, 1)

                        pe.wait_ge(pa_q, it + 1)
                        bank_free(0)
                        bank_free(1)
                        for g in range(2):
                            rows = slice(64 * g, 64 * g + 64)
                            for u in range(NT):
                                last = nc.tensor.matmul(ps[:, 4 + g, u * 32:(u + 1) * 32], qst[rows, u * P:(u + 1) * P],
                                                        kcT_p[rows, gp, :], start=True, stop=True)
                        last.then_inc(pa_c, 1)
                        scores(0)
                        pe.wait_ge(pa_cn, it + 1)
                        b = 5
                        for g in range(2):
                            last = nc.tensor.transpose(ps[:, b, g * P:(g + 1) * P], cs[:, 4 * g:4 * g + 4, :].rearrange("p a b -> p (a b)"), ident)
                        last.then_inc(pa_ct, 1)
                        for u in range(NT):
                            k0 = 2 + 4 * u + (0, 0, 1, 2)[u]
                            if u < NT - 1:
                                scores(u + 1)
                                if u == NT - 2:
                                    pe.drain().then_inc(pa_qfree, 1)
                            else:
                                pe.wait_ge(pa_exp, nth(pa_exp, 4 * it + 4))
                            for gb in range(4):
                                b = bank_free(k0 + gb)
                                for kt in range(u + 1):
                                    last = nc.tensor.transpose(ps[:, b, kt * P:(kt + 1) * P], pr[:, u % 2, gb, kt * P:(kt + 1) * P], ident)
                                last.then_inc(pa_t, 1)
                            pe.wait_ge(pa_o, nth(pa_o, 4 * it + (u - 1)))
                            pe.wait_ge(pa_ctev, it + 1)
                            for g in range(2):
                                vcol = slice((2 * gp + g) * HD, (2 * gp + g + 1) * HD)
                                q4 = slice(32 * u, 32 * u + 32)
                                nc.tensor.matmul(ps[:, 6 + u % 2, g * 3 * HD:g * 3 * HD + HD], cT[q4, g, :], vc_p[q4, vcol], start=True, stop=True)
                                for br in range(2):
                                    pe.wait_ge(pa_te, nth(pa_te, 20 * it + (k0 - 2 + 2 * g + br + 1)))
                                    o = (g * 3 + br + 1) * HD
                                    c0 = (Z_VS, Z_VW)[br] + (2 * gp + g) * HD
                                    for kt in range(u + 1):
                                        last = nc.tensor.matmul(ps[:, 6 + u % 2, o:o + HD], prT[:, u % 2, 2 * g + br, kt * P:(kt + 1) * P],
                                                                zk[:, kt, c0:c0 + HD], start=kt == 0, stop=kt == u)
                            last.then_inc(pa_pv, 1)
                            if u > 0:
                                y_back(u - 1, k0 + 4)
                        y_back(NT - 1, 21)
                end_phase(pe, l, 7)

                for pair in range(4):
                    last = nc.tensor.matmul(ps[:, 7, pair * 48:(pair + 1) * 48], C("pick", NSAM)[:, pair * P:(pair + 1) * P],
                                            zk[0:NSAM, NT, Z_G:Z_G + 48], start=True, stop=True)
                last.then_inc(sa_g, 1)
                pe.wait_ge(sa_gr, l + 1)
                pe.sem_inc(passed, 1)
                with pe.Fori(0, 2) as pp:
                    for par in range(2):
                        it = 4 * l + 2 * pp + par
                        pe.wait_ge(sa_q, it + 1)
                        for s in range(2):
                            for gp in range(2):
                                nc.tensor.matmul(ps[:, 3, 0:NWS], qs[:, gp, s, :], kcT_s[:, gp, ds(4 * pp + (2 * par + s), 1), 0:NWS],
                                                 start=s + gp == 0, stop=s + gp == 2)
                        for br in range(2):
                            for s in range(2):
                                for gp in range(2):
                                    last = nc.tensor.matmul(ps[:, 3, 64 + br * NSAM:64 + (br + 1) * NSAM], qs[:, gp, s, :], knT[:, 2 * br + gp, :],
                                                            start=s + gp == 0, stop=s + gp == 2)
                        last.then_inc(sa_c, 1)
                        jobs = [(half, s, gp) for half in range(3) for s in range(2) for gp in range(2)]

                        def key_tp(k):
                            half, s, gp = jobs[k]
                            pe.wait_ge(sa_ke, nth(sa_ke, 12 * it + (k - 1)))
                            if k == 0:
                                pe.wait_ge(s_kv[par], 512 * l + 256 * pp + 256)
                            if k == 8:
                                pe.wait_ge(s_win, 32 * it + 32)
                            for t in range(4):
                                src = swin[:, s, t, gp * P:(gp + 1) * P] if half == 2 else skv[:, par, s, 4 * half + t, gp * P:(gp + 1) * P]
                                last = nc.tensor.transpose(ps[:, 4 + k % 2, t * P:(t + 1) * P], src, ident)
                            last.then_inc(sa_kt, 1)

                        key_tp(0)
                        for k, (half, s, gp) in enumerate(jobs):
                            if k + 1 < len(jobs):
                                key_tp(k + 1)
                            pe.wait_ge(sa_ke, nth(sa_ke, 12 * it + (k + 1)))
                            nc.tensor.matmul(ps[:, half, :], qs[:, gp, s, :], skT[:, k % 2, :], start=s + gp == 0, stop=s + gp == 2
                                             ).then_inc(sa_s, 1)
                            if k == 4:
                                pe.wait_ge(sa_im, it + 1)
                                nc.tensor.matmul(ps[:, 3, 256:270], C("same"), small[:, 32:46], start=True, stop=True).then_inc(sa_imp, 1)
                        pe.wait_ge(sa_e, 2 * it + 1)
                        pe.sem_inc(passed, 1)
                        nc.tensor.transpose(ps[0:NWS, 4, 0:P], pc[:, 0:NWS], ident)
                        nc.tensor.transpose(ps[0:NSAM, 4, P:2 * P], ssel[:, PAST:PAST + NSAM], ident).then_inc(sa_t, 1)
                        for half in range(2):
                            if half:
                                pe.wait_ge(sa_te, 5 * it + 1)
                            for t in range(4):
                                o = (4 * half + t) * P
                                last = nc.tensor.transpose(ps[:, 5 - half, t * P:(t + 1) * P], ssel[:, o:o + P], ident)
                            last.then_inc(sa_t, 1)
                        pe.wait_ge(sa_e, 2 * it + 2)
                        pe.wait_ge(sa_te, 5 * it + 2)
                        for t in range(4):
                            last = nc.tensor.transpose(ps[:, 5, t * P:(t + 1) * P], swsc[:, t * P:(t + 1) * P], ident)
                        last.then_inc(sa_t, 1)
                        pe.wait_ge(sa_te, 5 * it + 3)
                        pe.sem_inc(passed, 1)
                        nc.tensor.transpose(ps[0:NSAM, 4, 0:P], swsc[:, WIN:WIN + NSAM], ident).then_inc(sa_t, 1)
                        for s in range(2):
                            rows = slice(64 * s, 64 * s + 64)
                            nc.tensor.matmul(ps[rows, 6, 0:KV], spT[0:NWS, 13, rows], vcst[0:NWS, s * KV:(s + 1) * KV], start=True, stop=True)
                            for t in range(8):
                                nc.tensor.matmul(ps[rows, 6, KV:2 * KV], spT[:, t, rows], skv[:, par, s, t, KV:2 * KV], start=t == 0, stop=False)
                            nc.tensor.matmul(ps[rows, 6, KV:2 * KV], spT[0:NSAM, 12, rows], zk[0:NSAM, NT, Z_VS:Z_VS + KV], start=False, stop=True)
                        pe.wait_ge(sa_te, 5 * it + 5)
                        for s in range(2):
                            rows = slice(64 * s, 64 * s + 64)
                            for t in range(4):
                                nc.tensor.matmul(ps[rows, 7, 0:KV], spT[:, 8 + t, rows], swin[:, s, t, KV:2 * KV], start=t == 0, stop=False)
                            last = nc.tensor.matmul(ps[rows, 7, 0:KV], spT[0:NSAM, 14, rows], zk[0:NSAM, NT, Z_VW:Z_VW + KV], start=False, stop=True)
                        last.then_inc(sa_o, 1)
                        pe.drain().then_inc(s_fin, 1)
                        pe.wait_ge(sa_y, it + 1)
                        for gp in range(2):
                            last = nc.tensor.transpose(ps[:, 5, gp * P:(gp + 1) * P], sy[:, gp * P:(gp + 1) * P], ident)
                        last.then_inc(sa_yt, 1)
                        pe.wait_ge(sa_ys, it + 1)
                end_phase(pe, l, 8)

                end_phase(pe, l, 9)
                with pe.Fori(0, 2) as i:
                    for n in range(2):
                        pe.wait_ge(w_lo, nth(w_lo, l * NB + 2 * i + (B_ZB + n + 1)))
                        for jj in range(2):
                            pe.wait_ge(zb_done, nth(zb_done, 8 * l + 4 * i + (2 * n + jj - 3)))
                            fm_tile(n, jj, 2 * (2 * n + jj), hH, hL).then_inc(zb, 1)
                        pe.drain().then_inc(w_done, 1)
                end_phase(pe, l, 10)
                merge(1, B_MB, (hH, hL), (aH, aL))
                end_phase(pe, l, 11)
                end_phase(pe, l, 12)
                with pe.Fori(0, 2) as i:
                    for n in range(2):
                        pe.wait_ge(w_lo, nth(w_lo, l * NB + 2 * i + (B_WO + n + 1)))
                        for jj in range(2):
                            pe.wait_ge(wo_done, nth(wo_done, 8 * l + 4 * i + (2 * n + jj - 3)))
                            fm_tile(n, jj, 2 * (2 * n + jj), aH, aL).then_inc(wo, 1)
                        pe.drain().then_inc(w_done, 1)
                pe.wait_ge(p_in, 32 * l + 32)
                pe.wait_ge(wo_done, nth(wo_done, 8 * l + 8))
                for c in range(2):
                    for tt in range(5):
                        rows = P if tt < NT else NSAM
                        last = nc.tensor.transpose(ps[:, 2 * c + tt // NT, (tt % NT) * P:(tt % NT) * P + rows],
                                                   pin[0:rows, tt, c * P:(c + 1) * P], ident[0:rows, 0:rows])
                last.then_inc(p_tp, 1)
                end_phase(pe, l, 13)
                with pe.Fori(0, 4) as i:
                    for n in range(2):
                        pe.wait_ge(w_lo, nth(w_lo, l * NB + 2 * i + (B_PL + n + 1)))
                        for jj in range(2):
                            pe.wait_ge(pl_done, nth(pl_done, 8 * l + 2 * i + (jj - 1)))
                            last = fm_tile(n, jj, 2 * (2 * n + jj), *((pH, pL, 2) if n else (aH, aL, KT)))
                            last.then_inc(pl, 1)
                        pe.drain().then_inc(w_done, 1)
                end_phase(pe, l, 14)

            norm_sum(NL)
            for tt in range(5):
                rows = P if tt < NT else NSAM
                pe.wait_ge(y_ready, 1)
                pe.wait_ge(y_act, nth(y_act, tt - 3))
                pe.wait_ge(y_dve, nth(y_dve, tt - 3))
                for c in range(KT):
                    last = nc.tensor.transpose(ps[0:rows, 2 * (tt % 4) + c // 4, (c % 4) * P:(c % 4 + 1) * P],
                                               xT[:, c, tt * P:tt * P + rows], ident)
                last.then_inc(y_tp, 1)

        @block.scalar
        def _(act):
            def norm_std(l):
                for c in range(KT):
                    act.wait_ge(sq_used, nth(sq_used, l * KT + (c - 1)))
                    act.activation(sq[:, c % 2, :], xT[:, c, :], ACT.Square).then_inc(sq_ready, 1)
                act.wait_ge(ss_ready, l + 1)
                act.activation(halves(rstd[:]), bank2(0), ACT.Sqrt, bias=C("eps"), scale=1.0 / D).then_inc(std_ready, 1)

            def split_h(n):
                for c in range(KT):
                    act.wait_ge(h_f, KT * n + (c + 1))
                    act.activation(hH[:, c, :], t_f[:, c % 2, :], ACT.Copy).then_inc(h_hi, 1)

            def split(n, src):
                for c in range(KT):
                    act.activation(aH[:, c, :], src[:, c, :], ACT.Copy).then_inc(sp_hi, 1)

            act.wait_ge(s_const, 16)
            act.wait_ge(s_zero, 1)
            for c in range(KT):
                act.wait_ge(x_tp, c + 1)
                act.activation(xT[:, c, 0:SEQ], ps[:, 2 * (c % 4), :], ACT.Copy)
                act.activation(xT[:, c, SEQ:TOK], ps[:, 2 * (c % 4) + 1, 0:NSAM], ACT.Copy).then_inc(x_free, 1)
            end_phase(act, 0, -1)

            with act.Fori(0, NL) as l:
                norm_std(l)
                make_high(act, l, pb(B_CONV, 0, 0), 0)
                split_h(2 * l)
                end_phase(act, l, 0)
                with act.Fori(0, 4) as i:
                    n = 4 * l + i
                    for kind in range(4):
                        make_high(act, l, pb(B_CONV, 2 * i + (kind + 1) // 2, (kind + 1) % 2), (kind + 1) % 2)
                        for jj in range(2):
                            act.wait_ge(cv, 8 * n + (2 * kind + jj + 1))
                            bank = bank2(2 * ((2 * kind + jj) % 4))
                            if kind == 0:
                                act.wait_ge(cv_used, nth(cv_used, 2 * n + (jj - 1)))
                            if kind < 3:
                                act.activation(halves(cv_in[:, kind, jj, :]), bank, ACT.Copy).then_inc(cv_act, 1)
                            else:
                                act.activation(halves(cv_in[:, 3, jj, :]), bank, ACT.Sigmoid).then_inc(cv_sg, 1)
                        if kind == 3:
                            for jj in range(2):
                                act.wait_ge(cv_f, 2 * n + (jj + 1))
                                act.activation(one(aH, 2 * i + jj), cv_in[:, 1, jj, :], ACT.Copy).then_inc(cv_hi, 1)
                end_phase(act, l, 1)

                def gates(which, first_block):
                    with act.Fori(0, 4) as i:
                        for n in range(2):
                            make_high(act, l, pb(first_block, i + (n + 1) // 2, (n + 1) % 2), (n + 1) % 2)
                            if n == 0:
                                for jj in range(2):
                                    act.wait_ge(mg, 32 * l + 4 * i + (16 * which + jj + 1))
                                    act.wait_ge(mg_dve, nth(mg_dve, 16 * l + 2 * i + (8 * which + jj - 1)))
                                    act.activation(halves(t_f[:, jj, :]), bank2(2 * jj), ACT.Sigmoid).then_inc(mg_sg, 1)

                gates(0, B_MA)
                end_phase(act, l, 2)
                act.wait_ge(tail_tp, l + 1)
                act.activation(tail_rows[:, 0:SEQ], ps[0:18, 6, :], ACT.Copy).then_inc(tail_cp, 1)
                act.activation(tail_rows[:, SEQ:D], ps[0:18, 7, :], ACT.Copy).then_inc(tail_cp, 1)

                def copy_out(b, half, n, dst, width):
                    col = 2 * width * half + n * width
                    for tt in range(5):
                        rows = P if tt < NT else NSAM
                        act.wait_ge(tm, l * (5 * TM_BLOCKS) + 10 * half + (5 * (b + n) + tt + 1))
                        if dst is zq:
                            out = zq[0:rows, tt, ds(2 * BW * half, 2 * BW)].rearrange("p (r g d) -> p g r d", g=2, d=HD)[:, n]
                            src = ps[0:rows, tt, 0:BW].rearrange("p (r d) -> p r d", d=HD)
                        else:
                            out, src = dst[0:rows, tt, ds(col, width)], ps[0:rows, tt, 0:width]
                        act.activation(out, src, ACT.Copy).then_inc(tm_ev, 1)

                with act.Fori(0, NQB // 2) as i:
                    for n in range(2):
                        make_high(act, l, pb(B_TM, i + (n + 1) // 2, (n + 1) % 2), (n + 1) % 2, width=(BW, WW)[n])
                        copy_out(0, i, n, zq, BW)
                with act.Fori(0, NKB // 2 - 1) as i:
                    for n in range(2):
                        make_high(act, l, pb(B_TM + NQB, i + (n + 1) // 2, (n + 1) % 2), (n + 1) % 2, width=WW)
                        copy_out(NQB, i, n, zk, WW)
                make_high(act, l, pb(B_TM + NQB, NKB // 2 - 1, 1), 1, width=WW)
                for n in range(2):
                    copy_out(NQB, NKB // 2 - 1, n, zk, WW)
                act.drain()
                act.activation(zk[:, 0:NT, Z_G:Z_G + 48], zk[:, 0:NT, Z_G:Z_G + 48], ACT.Sigmoid)
                act.activation(zk[0:NSAM, NT, Z_G:Z_G + 48], zk[0:NSAM, NT, Z_G:Z_G + 48], ACT.Sigmoid)
                act.wait_ge(tail_out, 32 * l + 32)
                act.sem_inc(passed, 1)
                end_phase(act, l, 3)

                for kv in range(2):
                    act.wait_ge(w1_in, 64 * l + (32 * kv + 32))
                    act.activation(w1H[:].rearrange("p k h -> p (k h)"), craw[:, 0].rearrange("p s t c -> p (s t c)"), ACT.Copy).then_inc(w1_hi, 1)

                    def chunks_high(unit, rows, nseq):
                        for j in range(4):
                            act.wait_ge(c_mm, nth(c_mm, 4 * unit + (j - 1)))
                            for s in range(nseq):
                                act.wait_ge(c_tp, 8 * unit + (2 * j + s + 1))
                                src = ps[:, (2 * j + s) % 4, :].rearrange("p (g h) -> p h g", g=GROUPS)[:, 0:rows, :]
                                act.activation(chH[:, j % 2, s, 0:rows, :], src, ACT.Copy).then_inc(c_hi, 1)
                            if nseq == 1:
                                act.drain().then_inc(c_hi, 1)

                    def hidden_gate(unit, n):
                        act.wait_ge(c_acc, unit + 1)
                        for hid in range(2):
                            act.activation(hsg[:, hid, 0:n], ps[:, 4 + hid, 0:n], ACT.Sigmoid, bias=hb[:, hid:hid + 1]).then_inc(c_sg, 1)

                    chunks_high(10 * l + 5 * kv, 68, 1)
                    act.wait_ge(pos_ready, 2 * l + (kv + 1))
                    hidden_gate(10 * l + 5 * kv, NWP * GROUPS)
                    with act.Fori(0, 2) as pp:
                        for par in range(2):
                            unit = 10 * l + 2 * pp + (5 * kv + par + 1)
                            chunks_high(unit, P, 2)
                            hidden_gate(unit, 2 * NWS * GROUPS)
                    end_phase(act, l, 4 + kv)

                for k in range(0, 14, 2):
                    act.wait_ge(tp[0], 7 * l + (k // 2 + 1))
                    if k < 8:
                        act.activation(qT[:, k, :], ps[:, k % 8, :], ACT.Copy).then_inc(tp_free[0], 1)
                    elif k < 12:
                        act.activation(kT[:, (k - 8) // 2, 0, :], ps[:, k % 8, :], ACT.Copy).then_inc(tp_free[0], 1)
                    else:
                        act.activation(qsT[:].rearrange("p k t -> p (k t)"), ps[:, 4, 0:KT * NSAM], ACT.Copy).then_inc(tp_free[0], 1)
                end_phase(act, l, 6)

                for gp in range(2):
                    with act.Fori(0, REP) as r:
                        it = 8 * l + r + 4 * gp

                        def exps(u):
                            act.wait_ge(pa_nm, 4 * it + (u + 1))
                            act.wait_ge(pa_o, nth(pa_o, 4 * it + (u - 1)))
                            n = P * (u + 1)
                            for gb in range(4):
                                o = 4 * (u % 2) + gb
                                last = act.activation(pr[:, u % 2, gb, 0:n], ps[:, gb, 0:n], ACT.Exp, bias=small[:, o:o + 1],
                                                      scale=SCALE, accum_out=small[:, 8 + o:9 + o])
                            act.drain().then_inc(pa_exp, 1)

                        def y_out(u, k):
                            act.wait_ge(pa_t, 20 * it + (k - 1))
                            o = yT[:].rearrange("p k t -> p (k t)")[:, ds(TOK * r + (4 * gp * TOK + u * P), P)]
                            act.activation(o, ps[:, 4 + k % 2, 0:P], ACT.Copy).then_inc(pa_te, 1)

                        act.wait_ge(pa_csc, it + 1)
                        act.activation(cs[:], cs[:], ACT.Exp, scale=SCALE).then_inc(pa_cexp, 1)
                        exps(0)
                        for u in range(NT):
                            k0 = 2 + 4 * u + (0, 0, 1, 2)[u]
                            act.wait_ge(pa_pv, nth(pa_pv, 4 * it + (u - 1)))
                            for gb in range(4):
                                k = k0 + gb
                                act.wait_ge(pa_t, 20 * it + (k - 1))
                                act.activation(prT[:, u % 2, gb, 0:P * (u + 1)], ps[:, 4 + k % 2, 0:P * (u + 1)], ACT.Copy).then_inc(pa_te, 1)
                            if u < NT - 1:
                                exps(u + 1)
                            if u > 0:
                                y_out(u - 1, k0 + 4)
                        y_out(NT - 1, 21)
                end_phase(act, l, 7)

                with act.Fori(0, 2) as pp:
                    for par in range(2):
                        it = 4 * l + 2 * pp + par
                        act.wait_ge(sa_nm, it + 1)
                        act.activation(pc[:, 0:NWS], ps[:, 3, 0:NWS], ACT.Exp, bias=small[:, 64:65], scale=SCALE,
                                       accum_out=small[:, 65:66])
                        act.drain().then_inc(sa_cx, 1)
                        for k in range(12):
                            act.wait_ge(sa_kt, 12 * it + (k + 1))
                            act.wait_ge(sa_s, nth(sa_s, 12 * it + (k - 1)))
                            act.activation(skT[:, k % 2, :], ps[:, 4 + k % 2, :], ACT.Copy).then_inc(sa_ke, 1)
                        act.wait_ge(sa_m, 2 * it + 1)
                        act.activation(ssel[:], ssel[:], ACT.Exp, bias=small[:, 68:69], scale=SCALE, accum_out=small[:, 70:71])
                        act.drain().then_inc(sa_e, 1)
                        for n, (bank, rows, c0, c1, slot) in enumerate(((4, NWS, 0, P, 13), (5, P, 0, 4 * P, 0), (4, P, 0, 4 * P, 4),
                                                                        (5, P, 0, 4 * P, 8), (4, NSAM, 0, P, 14))):
                            if n == 3:
                                act.wait_ge(sa_m, 2 * it + 2)
                                act.activation(swsc[:], swsc[:], ACT.Exp, bias=small[:, 69:70], scale=SCALE, accum_out=small[:, 71:72])
                                act.drain().then_inc(sa_e, 1)
                            act.wait_ge(sa_t, 5 * it + (n + 1))
                            if n == 0:
                                act.activation(spT[0:NSAM, 12, :], ps[0:NSAM, 4, P:2 * P], ACT.Copy)
                            act.activation(spT[0:rows, slot:slot + (c1 - c0) // P, :].rearrange("p a b -> p (a b)"),
                                           ps[0:rows, bank, c0:c1], ACT.Copy).then_inc(sa_te, 1)
                act.wait_ge(s_winout, 256 * l + 256)
                act.sem_inc(passed, 1)
                end_phase(act, l, 8)

                make_high(act, l, pb(B_ZB, 0, 0), 0)
                split_h(2 * l + 1)
                end_phase(act, l, 9)
                with act.Fori(0, 2) as i:
                    for n in range(2):
                        make_high(act, l, pb(B_ZB, i + (n + 1) // 2, (n + 1) % 2), (n + 1) % 2)
                        for jj in range(2):
                            q = 8 * l + 4 * i + (2 * n + jj)
                            act.wait_ge(zb, q + 1)
                            act.wait_ge(zb_done, nth(zb_done, q - 1))
                            act.activation(halves(t_f[:, jj, :]), bank2(2 * (2 * n + jj)), ACT.Sigmoid).then_inc(zb_sg, 1)
                        for jj in range(2):
                            q = 8 * l + 4 * i + (2 * n + jj)
                            act.wait_ge(zb_f, q + 1)
                            act.activation(one(aH, 4 * i + (2 * n + jj)), t_f[:, jj, :], ACT.Copy).then_inc(zb_hi, 1)
                end_phase(act, l, 10)
                gates(1, B_MB)
                end_phase(act, l, 11)
                split(2 * l, m)
                end_phase(act, l, 12)
                with act.Fori(0, 2) as i:
                    for n in range(2):
                        make_high(act, l, pb(B_WO, i + (n + 1) // 2, (n + 1) % 2), (n + 1) % 2)
                act.wait_ge(wo_done, nth(wo_done, 8 * l + 8))
                act.wait_ge(p_tp, l + 1)
                for c in range(2):
                    act.activation(pH[:, c, 0:SEQ], ps[:, 2 * c, :], ACT.Copy)
                    act.activation(pH[:, c, SEQ:TOK], ps[:, 2 * c + 1, 0:NSAM], ACT.Copy).then_inc(p_hi, 1)
                split(2 * l + 1, xT)
                end_phase(act, l, 13)

                def ple(i, prep):
                    for n in range(2):
                        if prep or n == 0:
                            make_high(act, l, pb(B_PL, i + (n + 1) // 2, (n + 1) % 2), (n + 1) % 2, nk=(2, KT)[n])
                        if n == 0:
                            for jj in range(2):
                                act.wait_ge(pl, 16 * l + 4 * i + (jj + 1))
                                act.wait_ge(pl_done, nth(pl_done, 8 * l + 2 * i + (jj - 1)))
                                act.activation(halves(t_f[:, jj, :]), bank2(2 * jj), ACT.Sigmoid).then_inc(pl_sg, 1)

                with act.Fori(0, 3) as i:
                    ple(i, True)
                ple(3, False)
                end_phase(act, l, 14)

            norm_std(NL)
            for tt in range(5):
                rows = P if tt < NT else NSAM
                act.wait_ge(y_tp, tt + 1)
                act.activation(out_rows[0:rows, tt, 0:SEQ], ps[0:rows, 2 * (tt % 4), :], ACT.Copy).then_inc(y_act, 1)

        @block.vector
        def _(dve):
            def norm_recip(l):
                dve.wait_ge(std_ready, l + 1)
                dve.reciprocal(rstd[:], rstd[:])
                dve.drain()

            def make_h(n):
                def low(c):
                    dve.wait_ge(h_hi, KT * n + (c + 1))
                    dve.tensor_tensor(hL[:, c, :], t_f[:, c % 2, :], hH[:, c, :].bitcast(F32), ALU.subtract)

                for c in range(KT):
                    if c >= 2:
                        low(c - 2)
                        dve.drain()
                    dve.scalar_tensor_tensor(out=t_f[:, c % 2, :], in0=xT[:, c, :], scalar=cols[:, c, 19:20], in1=rstd[:],
                                             op0=ALU.mult, op1=ALU.mult).then_inc(h_f, 1)
                low(KT - 2)
                low(KT - 1)

            def split(n, src):
                for c in range(KT):
                    dve.wait_ge(sp_hi, KT * n + (c + 1))
                    dve.tensor_tensor(aL[:, c, :], src[:, c, :], aH[:, c, :].bitcast(F32), ALU.subtract)

            end_phase(dve, 0, -1)
            with dve.Fori(0, NL) as l:
                dve.wait_ge(st_tp, l + 1)
                dve.tensor_copy(cols[:].rearrange("p k n -> p (k n)"), ps[:, 2, 0:21 * KT])
                norm_recip(l)
                make_low(dve, l, pb(B_CONV, 0, 0), 0)
                make_h(2 * l)
                dve.drain()
                dve.memset(cv_u[:, :, 0:2], 0.0)
                dve.drain()
                end_phase(dve, l, 0)
                with dve.Fori(0, 4) as i:
                    n = 4 * l + i
                    for kind in range(4):
                        make_low(dve, l, pb(B_CONV, 2 * i + (kind + 1) // 2, (kind + 1) % 2), (kind + 1) % 2)
                        if kind == 0:
                            for jj in range(2):
                                dve.tensor_copy(cst[:, jj, :], cols[:].rearrange("p k n -> p (k n)")[:, ds(42 * i + 21 * jj, 21)])
                            dve.drain()
                        for jj in range(2):
                            if kind == 1:
                                dve.wait_ge(cv_act, nth(cv_act, 6 * n + (3 + jj)))
                                u = cv_u[:, jj, :]
                                us = u[:, SEQ + 2:UW].rearrange("p (b t) -> p b t", t=6)
                                ca, xa = cv_in[:, 0, jj, :], cv_in[:, 1, jj, :]
                                dve.tensor_tensor(u[:, 2:SEQ + 2], ca[:, 0:SEQ], xa[:, 0:SEQ], ALU.mult)
                                dve.tensor_tensor(us[:, :, 2:6], ca[:, SEQ:TOK].rearrange("p (b t) -> p b t", t=TS),
                                                  xa[:, SEQ:TOK].rearrange("p (b t) -> p b t", t=TS), ALU.mult)
                                dve.tensor_copy(us[:, :, 0:2], cst[:, jj, 0:16].rearrange("p (b t) -> p b t", t=2))
                                dve.drain()
                                tl = tails[:].rearrange("p k n -> p (k n)")
                                dve.tensor_copy(tl[:, ds(36 * i + 18 * jj, 2)], u[:, SEQ:SEQ + 2])
                                dve.tensor_copy(tl[:, ds(36 * i + (18 * jj + 2), 16)].rearrange("p (b t) -> p b t", t=2), us[:, :, 4:6])
                            elif kind == 2:
                                dve.wait_ge(cv_act, nth(cv_act, 6 * n + (5 + jj)))
                                w = UW - 2
                                dve.tensor_scalar(cv_y[:, 0:w], cv_u[:, jj, 0:w], cst[:, jj, 16:17], None, ALU.mult)
                                for tap in (1, 2):
                                    dve.drain()
                                    dve.scalar_tensor_tensor(out=cv_y[:, 0:w], in0=cv_u[:, jj, tap:tap + w], scalar=cst[:, jj, 16 + tap:17 + tap],
                                                             in1=cv_y[:, 0:w], op0=ALU.mult, op1=ALU.add)
                                dve.drain()
                                ba = cv_in[:, 2, jj, :]
                                ys = cv_y[:, SEQ + 2:UW].rearrange("p (b t) -> p b t", t=6)[:, :, 0:TS]
                                bs = ba[:, SEQ:TOK].rearrange("p (b t) -> p b t", t=TS)
                                dve.tensor_tensor(ba[:, 0:SEQ], ba[:, 0:SEQ], cv_y[:, 0:SEQ], ALU.mult)
                                dve.tensor_tensor(bs, bs, ys, ALU.mult)
                                dve.drain()
                            elif kind == 3:
                                dve.wait_ge(cv_sg, 2 * n + (jj + 1))
                                dve.tensor_tensor(halves(cv_in[:, 0, jj, :]), bank2(4 + 2 * jj), halves(cv_in[:, 3, jj, :]), ALU.mult).then_inc(cv_dve, 1)
                                dve.drain()
                                dve.tensor_tensor(cv_in[:, 1, jj, :], cv_in[:, 0, jj, :], cv_in[:, 2, jj, :], ALU.mult).then_inc(cv_f, 1)
                        if kind == 3:
                            dve.drain()
                            for jj in range(2):
                                dve.wait_ge(cv_hi, 2 * n + (jj + 1))
                                dve.tensor_tensor(one(aL, 2 * i + jj), cv_in[:, 1, jj, :], one(aH, 2 * i + jj).bitcast(F32), ALU.subtract
                                                  ).then_inc(cv_used, 1)
                end_phase(dve, l, 1)

                def products(which, first_block):
                    with dve.Fori(0, 4) as i:
                        for n in range(2):
                            make_low(dve, l, pb(first_block, i + (n + 1) // 2, (n + 1) % 2), (n + 1) % 2)
                            if n == 1:
                                for jj in range(2):
                                    dve.wait_ge(mg_sg, 16 * l + 2 * i + (8 * which + jj + 1))
                                    dve.wait_ge(mg, 32 * l + 4 * i + (16 * which + 2 + jj + 1))
                                    if which == 0:
                                        dve.tensor_tensor(two(m, 2 * i + jj), bank2(4 + 2 * jj), halves(t_f[:, jj, :]), ALU.mult).then_inc(mg_dve, 1)
                                    else:
                                        dve.tensor_tensor(halves(t_f[:, jj, :]), bank2(4 + 2 * jj), halves(t_f[:, jj, :]), ALU.mult)
                                        dve.drain()
                                        dve.tensor_tensor(one(m, 2 * i + jj), one(m, 2 * i + jj), t_f[:, jj, :], ALU.add).then_inc(mg_dve, 1)

                products(0, B_MA)
                end_phase(dve, l, 2)

                def rope(z, rows, tts, c0, heads):
                    nt = tts[1] - tts[0]
                    v = z[0:rows, tts[0]:tts[1], ds(c0, heads * HD)].rearrange("p t (h c) -> p t h c", c=HD)
                    x1, x2 = v[:, :, :, 0:32], v[:, :, :, 32:64]
                    tab = [C(n, rows).rearrange("p (t c) -> p t c", c=32)[:, tts[0]:tts[1], :].unsqueeze(2).to_broadcast([rows, nt, heads, 32])
                           for n in ("cos", "sin")]
                    ta, tb = (rope_a[0:rows, k, 0:nt * heads * 32].rearrange("p (t h c) -> p t h c", t=nt, h=heads) for k in range(2))
                    dve.tensor_tensor(ta, x2, tab[1], ALU.mult)
                    dve.tensor_tensor(tb, x1, tab[1], ALU.mult)
                    dve.drain()
                    dve.tensor_tensor(x1, x1, tab[0], ALU.mult)
                    dve.tensor_tensor(x2, x2, tab[0], ALU.mult)
                    dve.drain()
                    dve.tensor_tensor(x1, x1, ta, ALU.subtract)
                    dve.tensor_tensor(x2, x2, tb, ALU.add)
                    dve.drain()

                def rope_all(z, c0, heads, blocks):
                    dve.wait_ge(tm_ev, nth(tm_ev, l * (5 * TM_BLOCKS) + 5 * blocks))
                    for tt in range(NT):
                        rope(z, P, (tt, tt + 1), c0, heads)
                    rope(z, NSAM, (NT, NT + 1), c0, heads)

                with dve.Fori(0, NQB // 2) as i:
                    for n in range(2):
                        make_low(dve, l, pb(B_TM, i + (n + 1) // 2, (n + 1) % 2), (n + 1) % 2, width=(BW, WW)[n])
                    rope_all(zq, 512 * i, 8, 2 * i + 2)
                with dve.Fori(0, NKB // 2 - 1) as i:
                    for n in range(2):
                        make_low(dve, l, pb(B_TM + NQB, i + (n + 1) // 2, (n + 1) % 2), (n + 1) % 2, width=WW)
                    rope_all(zk, 512 * i, 4, 2 * i + (NQB + 2))
                make_low(dve, l, pb(B_TM + NQB, NKB // 2 - 1, 1), 1, width=WW)
                rope_all(zk, Z_KW, 4, TM_BLOCKS)
                dve.drain().then_inc(z_ready, 1)
                end_phase(dve, l, 3)

                for kv in range(2):
                    dve.wait_ge(w1_hi, 2 * l + (kv + 1))
                    dve.tensor_tensor(w1L[:].rearrange("p k h -> p (k h)"), craw[:, 0].rearrange("p s t c -> p (s t c)"),
                                      w1H[:].rearrange("p k h -> p (k h)").bitcast(F32), ALU.subtract).then_inc(w1_lo, 1)

                    def chunks_low(unit, rows, nseq):
                        for j in range(4):
                            for s in range(nseq):
                                dve.wait_ge(c_hi, 8 * unit + (2 * j + s + 1))
                                src = ps[:, (2 * j + s) % 4, :].rearrange("p (g h) -> p h g", g=GROUPS)[:, 0:rows, :]
                                dve.tensor_tensor(chL[:, j % 2, s, 0:rows, :], src, chH[:, j % 2, s, 0:rows, :].bitcast(F32), ALU.subtract
                                                  ).then_inc(c_lo, 1)
                            if nseq == 1:
                                dve.drain().then_inc(c_lo, 1)

                    def hidden(unit, n):
                        dve.wait_ge(c_w2, nth(c_w2, unit))
                        for hid in range(2):
                            dve.wait_ge(c_sg, 2 * unit + (hid + 1))
                            dve.scalar_tensor_tensor(out=hidT[:, hid, 0:n], in0=ps[:, 4 + hid, 0:n], scalar=hb[:, hid:hid + 1],
                                                     in1=hsg[:, hid, 0:n], op0=ALU.add, op1=ALU.mult).then_inc(c_hid, 1)

                    unit = 10 * l + 5 * kv
                    chunks_low(unit, 68, 1)
                    dve.wait_ge(c_acc, unit + 1)
                    for hid in range(2):
                        dve.tensor_copy(hb[:, hid:hid + 1], ps[:, 4 + hid, (NWP + 1) * GROUPS:(NWP + 1) * GROUPS + 1])
                    dve.drain().then_inc(pos_ready, 1)
                    hidden(unit, NWP * GROUPS)
                    dve.wait_ge(c_w2, nth(c_w2, unit + 1))
                    if kv == 0:
                        src = ps[0:HD, 6, 0:NWP * GROUPS].rearrange("p (n a g) -> p g a n", a=2, g=2)
                        for g in range(2):
                            dve.tensor_copy(kcT_p[64 * g:64 * g + 64, :, 0:NWP], src[:, g])
                    else:
                        for q in range(4):
                            dve.tensor_copy(vc_p[32 * q:32 * q + NWP, :], ps[0:NWP, 6, 0:KV])
                    dve.drain().then_inc(c_out, 1)
                    with dve.Fori(0, 2) as pp:
                        for par in range(2):
                            unit = 10 * l + 2 * pp + (5 * kv + par + 1)
                            chunks_low(unit, P, 2)
                            hidden(unit, 2 * NWS * GROUPS)
                            dve.wait_ge(c_w2, nth(c_w2, unit + 1))
                            if kv == 0:
                                for s in range(2):
                                    src = ps[0:HD, 6, s * NWS * GROUPS:(s + 1) * NWS * GROUPS].rearrange("p (n a g) -> p g a n", a=2, g=2)
                                    for g in range(2):
                                        dst = kcT_s[64 * g:64 * g + 64].rearrange("p a s n -> p a (s n)")
                                        dve.tensor_copy(dst[:, :, ds(256 * pp + 64 * (2 * par + s), NWS)], src[:, g])
                            else:
                                dve.tensor_copy(vc_s[0:NWS, ds(1024 * pp + 512 * par, 512)], ps[0:NWS, 6, :])
                            dve.drain().then_inc(c_out, 1)
                    end_phase(dve, l, 4 + kv)

                for k in range(1, 14, 2):
                    dve.wait_ge(tp[1], 7 * l + (k // 2 + 1))
                    if k < 8:
                        dve.tensor_copy(qT[:, k, :], ps[:, k % 8, :]).then_inc(tp_free[1], 1)
                    elif k < 12:
                        dve.tensor_copy(kT[:, (k - 8) // 2, 1, :], ps[:, k % 8, :]).then_inc(tp_free[1], 1)
                    else:
                        dve.tensor_copy(knT[:].rearrange("p k t -> p (k t)"), ps[:, 5, 0:4 * NSAM]).then_inc(tp_free[1], 1)
                end_phase(dve, l, 6)

                for gp in range(2):
                    with dve.Fori(0, REP) as r:
                        it = 8 * l + r + 4 * gp

                        def softmax(u):
                            o = 4 * (u % 2)
                            dve.wait_ge(pa_s, 4 * it + (u + 1))
                            dg = ps[:, 0:4, u * P:(u + 1) * P]
                            dve.tensor_tensor(dg, dg, C("causal").unsqueeze(1).to_broadcast([P, 4, P]), ALU.add)
                            dve.drain()
                            dve.tensor_reduce(out=small[:, o:o + 4], in_=ps[:, 0:4, 0:P * (u + 1)], op=ALU.max, axis=AX.X, negate=True)
                            dve.drain()
                            dve.tensor_scalar(small[:, o:o + 4], small[:, o:o + 4], SCALE, None, ALU.mult).then_inc(pa_nm, 1)

                        def combine(u, y_event):
                            o = 8 + 4 * (u % 2)
                            dve.wait_ge(pa_pv, nth(pa_pv, 4 * it + (u + 1)))
                            sums = small[:, o:o + 4]
                            wts = small[:, 48:54]
                            dve.tensor_scalar(sums, sums, 1e-30, None, ALU.max)
                            dve.drain()
                            dve.reciprocal(small[:, 24:30].rearrange("p (g b) -> p g b", g=2)[:, :, 1:3], sums.rearrange("p (g b) -> p g b", g=2))
                            dve.drain()
                            gt = zk[:, u, Z_G + 24 * gp:Z_G + 24 * gp + 24].rearrange("p (g c) -> p g c", g=2)[:, :, ds(3 * r, 3)]
                            dve.tensor_tensor(wts.rearrange("p (g b) -> p g b", g=2), gt, small[:, 24:30].rearrange("p (g b) -> p g b", g=2), ALU.mult)
                            dve.drain()
                            dve.tensor_tensor(ow[:], ps[:, 6 + u % 2, 0:6 * HD].rearrange("p (k d) -> p k d", d=HD),
                                              wts.unsqueeze(2).to_broadcast([P, 6, HD]), ALU.mult)
                            dve.drain().then_inc(pa_o, 1)
                            dve.wait_ge(pa_te, nth(pa_te, 20 * it + y_event))
                            dve.tensor_reduce(out=yy[:, u % 2, :].rearrange("p (g d) -> p g d", g=2),
                                              in_=ow[:].rearrange("p (g b) d -> p g d b", g=2), op=ALU.add, axis=AX.X).then_inc(pa_y, 1)

                        dve.wait_ge(pa_qfree, nth(pa_qfree, it))
                        dve.tensor_copy(qst[:], qT[:].rearrange("p k t -> p (k t)")[:, ds(SEQ * r + 4 * gp * SEQ, SEQ)]).then_inc(pa_q, 1)
                        dve.wait_ge(pa_c, it + 1)
                        c8 = cs[:].rearrange("p (g q) n -> p g (q n)", g=2)
                        dve.tensor_tensor(c8, ps[:, 4:6, 0:P],
                                          C("cmask").unsqueeze(1).to_broadcast([P, 2, P]), ALU.add)
                        dve.drain()
                        mx = small[:, 16:24]
                        dve.tensor_reduce(out=mx, in_=cs[:], op=ALU.max, axis=AX.X)
                        dve.drain()
                        dve.tensor_scalar(mx, mx, LOWEST, None, ALU.max)
                        dve.drain()
                        dve.tensor_tensor(cs[:], cs[:], mx.unsqueeze(2).to_broadcast([P, 8, 32]), ALU.subtract).then_inc(pa_csc, 1)
                        softmax(0)
                        dve.wait_ge(pa_cexp, it + 1)
                        dve.tensor_reduce(out=mx, in_=cs[:], op=ALU.add, axis=AX.X)
                        dve.drain()
                        dve.tensor_scalar(mx, mx, 1e-30, None, ALU.max)
                        dve.drain()
                        dve.reciprocal(mx, mx)
                        dve.drain()
                        dve.tensor_tensor(cs[:], cs[:], mx.unsqueeze(2).to_broadcast([P, 8, 32]), ALU.mult).then_inc(pa_cn, 1)
                        dve.wait_ge(pa_ct, it + 1)
                        dve.tensor_copy(cT[:].rearrange("p g q -> p (g q)"), ps[:, 5, 0:256]).then_inc(pa_ctev, 1)
                        for u in range(NT):
                            if u < NT - 1:
                                softmax(u + 1)
                            combine(u, (-1, 0, 9, 14)[u])
                end_phase(dve, l, 7)

                dve.memset(pc[:, 63:64], 0.0)
                dve.wait_ge(sa_g, l + 1)
                g3 = ssel[:, 0:192].rearrange("p (a c) -> p a c", a=4)
                dve.tensor_tensor(g3, ps[:, 7, 0:192].rearrange("p (a c) -> p a c", a=4), C("gmask").unsqueeze(1).to_broadcast([P, 4, 48]), ALU.mult)
                dve.drain()
                dve.tensor_reduce(out=grow[:], in_=ssel[:, 0:192].rearrange("p (a k b) -> p a b k", a=4, b=3), op=ALU.add, axis=AX.X)
                dve.drain().then_inc(sa_gr, 1)
                with dve.Fori(0, 2) as pp:
                    for par in range(2):
                        it = 4 * l + 2 * pp + par
                        dve.wait_ge(s_fin, nth(s_fin, it))
                        for g in range(2):
                            rows = slice(64 * g, 64 * g + 64)
                            for gp in range(2):
                                for s in range(2):
                                    c0 = 64 * s + 16 * (2 * gp + g)
                                    src = qsT[rows, 4 * gp:4 * gp + 4, ds(8 * pp * 2 + (2 * par + s) * TS, TS)].rearrange("p r t -> p t r")
                                    dve.tensor_copy(qs[rows, gp, s, c0:c0 + 16].rearrange("p (t r) -> p t r", t=TS), src)
                        dve.tensor_copy(vcst[0:NWS, :], vc_s[0:NWS, ds(1024 * pp + 512 * par, 512)])
                        dve.drain().then_inc(sa_q, 1)
                        dve.wait_ge(sa_c, it + 1)
                        dve.tensor_reduce(out=small[:, 64:65], in_=ps[:, 3, 0:NWS], op=ALU.max, axis=AX.X, negate=True)
                        nm = C("nmask")[:, ds(2 * NSAM * pp + NSAM * par, NSAM)]
                        dve.tensor_tensor(ssel[:, PAST:PAST + NSAM], ps[:, 3, 64:64 + NSAM], nm, ALU.add)
                        dve.tensor_tensor(swsc[:, WIN:WIN + NSAM], ps[:, 3, 64 + NSAM:64 + 2 * NSAM], nm, ALU.add)
                        dve.drain()
                        dve.tensor_scalar(small[:, 64:65], small[:, 64:65], -LOWEST, SCALE, ALU.min, ALU.mult).then_inc(sa_nm, 1)
                        dve.wait_ge(sa_cx, it + 1)
                        dve.tensor_scalar(small[:, 65:66], small[:, 65:66], 1e-30, None, ALU.max)
                        dve.drain()
                        dve.reciprocal(small[:, 65:66], small[:, 65:66])
                        dve.drain()
                        dve.tensor_scalar(pc[:, 0:NWS], pc[:, 0:NWS], small[:, 65:66], None, ALU.mult)
                        dve.drain()
                        dve.tensor_reduce(out=small[:, 32:46], in_=pc[:, 4:60].rearrange("p (j k) -> p j k", k=4), op=ALU.add, axis=AX.X)
                        dve.drain()
                        dve.tensor_tensor(small[:, 32:46], small[:, 32:46], pc[:, 3:56:4], ALU.add).then_inc(sa_im, 1)
                        dve.wait_ge(sa_imp, it + 1)
                        imp = ps[:, 3, 256:270]
                        dve.tensor_reduce(out=small[:, 66:67], in_=imp, op=ALU.min, axis=AX.X)
                        dve.drain()
                        dve.scalar_tensor_tensor(out=small[:, 80:94], in0=imp, scalar=small[:, 66:67], in1=C("iota")[:, 1:15],
                                                 op0=ALU.is_equal, op1=ALU.mult)
                        dve.drain()
                        dve.tensor_reduce(out=small[:, 67:68], in_=small[:, 80:94], op=ALU.max, axis=AX.X)
                        dve.drain()
                        dve.tensor_scalar(small[:, 96:112], C("iota"), small[:, 67:68], NEG, ALU.is_equal, ALU.mult)
                        dve.drain()
                        dve.wait_ge(sa_s, nth(sa_s, 12 * it + 8))
                        drop = small[:, 96:112].unsqueeze(1).unsqueeze(3).to_broadcast([P, 8, 16, 8])
                        dve.tensor_tensor(ssel[:, 0:PAST].rearrange("p (t j c) -> p t j c", t=8, j=16),
                                          ps[:, 0:2, :].rearrange("p a (t j c) -> p (a t) j c", t=4, j=16), drop, ALU.add)
                        dve.drain()
                        dve.tensor_reduce(out=small[:, 68:69], in_=ssel[:], op=ALU.max, axis=AX.X, negate=True)
                        dve.drain()
                        dve.tensor_scalar(small[:, 68:69], small[:, 68:69], SCALE, None, ALU.mult).then_inc(sa_m, 1)
                        dve.wait_ge(sa_s, nth(sa_s, 12 * it + 12))
                        dve.tensor_tensor(swsc[:, 0:WIN], ps[:, 2, :], C("wmask"), ALU.add)
                        dve.drain()
                        dve.tensor_reduce(out=small[:, 69:70], in_=swsc[:], op=ALU.max, axis=AX.X, negate=True)
                        dve.drain()
                        dve.tensor_scalar(small[:, 69:70], small[:, 69:70], SCALE, None, ALU.mult).then_inc(sa_m, 1)
                        dve.wait_ge(sa_o, it + 1)
                        dve.tensor_scalar(small[:, 70:72], small[:, 70:72], 1e-30, None, ALU.max)
                        dve.drain()
                        dve.reciprocal(small[:, 77:79], small[:, 70:72])
                        dve.drain()
                        dve.tensor_tensor(small[:, 72:75], grow[:].rearrange("p a b -> p (a b)")[:, ds(6 * pp + 3 * par, 3)], small[:, 76:79], ALU.mult)
                        dve.drain()
                        dve.tensor_scalar(sy[:], ps[:, 6, 0:KV], small[:, 72:73], None, ALU.mult)
                        dve.drain()
                        dve.scalar_tensor_tensor(out=sy[:], in0=ps[:, 6, KV:2 * KV], scalar=small[:, 73:74], in1=sy[:], op0=ALU.mult, op1=ALU.add)
                        dve.drain()
                        dve.scalar_tensor_tensor(out=sy[:], in0=ps[:, 7, 0:KV], scalar=small[:, 74:75], in1=sy[:], op0=ALU.mult, op1=ALU.add
                                                 ).then_inc(sa_y, 1)
                        dve.wait_ge(sa_yt, it + 1)
                        for gp in range(2):
                            for g in range(2):
                                rows = slice(64 * g, 64 * g + 64)
                                src = ps[rows, 5, gp * P:(gp + 1) * P].rearrange("p (s g t r) -> p g r s t", s=2, g=4, t=TS)[:, 2 * gp + g]
                                dst = yT[rows, 4 * gp:4 * gp + 4, ds(16 * pp + (8 * par + SEQ), 8)].rearrange("p r (s t) -> p r s t", s=2)
                                last = dve.tensor_copy(dst, src)
                        dve.drain().then_inc(sa_ys, 1)
                dve.wait_ge(s_winout, 256 * l + 256)
                dve.sem_inc(passed, 1)
                end_phase(dve, l, 8)

                make_low(dve, l, pb(B_ZB, 0, 0), 0)
                make_h(2 * l + 1)
                end_phase(dve, l, 9)
                with dve.Fori(0, 2) as i:
                    for n in range(2):
                        make_low(dve, l, pb(B_ZB, i + (n + 1) // 2, (n + 1) % 2), (n + 1) % 2)
                        for jj in range(2):
                            q = 8 * l + 4 * i + (2 * n + jj)
                            dve.wait_ge(zb_sg, q + 1)
                            dve.tensor_tensor(halves(t_f[:, jj, :]), bank2(2 * (2 * n + jj)), halves(t_f[:, jj, :]), ALU.mult)
                            dve.drain()
                            dve.tensor_tensor(t_f[:, jj, :], t_f[:, jj, :], one(yT, 4 * i + (2 * n + jj)), ALU.mult).then_inc(zb_f, 1)
                        dve.drain()
                        for jj in range(2):
                            q = 8 * l + 4 * i + (2 * n + jj)
                            dve.wait_ge(zb_hi, q + 1)
                            c = 4 * i + (2 * n + jj)
                            dve.tensor_tensor(one(aL, c), t_f[:, jj, :], one(aH, c).bitcast(F32), ALU.subtract).then_inc(zb_done, 1)
                end_phase(dve, l, 10)
                products(1, B_MB)
                end_phase(dve, l, 11)
                split(2 * l, m)
                end_phase(dve, l, 12)
                with dve.Fori(0, 2) as i:
                    for n in range(2):
                        make_low(dve, l, pb(B_WO, i + (n + 1) // 2, (n + 1) % 2), (n + 1) % 2)
                        for jj in range(2):
                            c = 4 * i + (2 * n + jj)
                            dve.wait_ge(wo, 8 * l + c + 1)
                            dve.tensor_tensor(two(xT, c), two(xT, c), bank2(2 * (2 * n + jj)), ALU.add).then_inc(wo_done, 1)
                dve.drain()
                for c in range(2):
                    dve.wait_ge(p_hi, 2 * l + (c + 1))
                    dve.tensor_tensor(pL[:, c, 0:SEQ], ps[:, 2 * c, :], pH[:, c, 0:SEQ].bitcast(F32), ALU.subtract)
                    dve.tensor_tensor(pL[:, c, SEQ:TOK], ps[:, 2 * c + 1, 0:NSAM], pH[:, c, SEQ:TOK].bitcast(F32), ALU.subtract)
                split(2 * l + 1, xT)
                end_phase(dve, l, 13)

                def ple(i, prep):
                    for n in range(2):
                        if prep or n == 0:
                            make_low(dve, l, pb(B_PL, i + (n + 1) // 2, (n + 1) % 2), (n + 1) % 2, nk=(2, KT)[n])
                    for jj in range(2):
                        dve.wait_ge(pl_sg, 8 * l + 2 * i + (jj + 1))
                        dve.wait_ge(pl, 16 * l + 4 * i + (2 + jj + 1))
                        dve.tensor_tensor(halves(t_f[:, jj, :]), bank2(4 + 2 * jj), halves(t_f[:, jj, :]), ALU.mult)
                        dve.drain()
                        dve.tensor_tensor(one(xT, 2 * i + jj), one(xT, 2 * i + jj), t_f[:, jj, :], ALU.add).then_inc(pl_done, 1)

                with dve.Fori(0, 3) as i:
                    ple(i, True)
                ple(3, False)
                end_phase(dve, l, 14)

            norm_recip(NL)
            for c in range(KT):
                last = dve.scalar_tensor_tensor(out=xT[:, c, :], in0=xT[:, c, :], scalar=cols[:, c, 20:21], in1=rstd[:], op0=ALU.mult, op1=ALU.mult)
            dve.drain().then_inc(y_ready, 1)
            for tt in range(5):
                rows = P if tt < NT else NSAM
                dve.wait_ge(y_tp, tt + 1)
                dve.tensor_copy(out_rows[0:rows, tt, SEQ:D], ps[0:rows, 2 * (tt % 4) + 1, :]).then_inc(y_dve, 1)


INPUTS = ["x_prompt", "x_sample", "cache_kv", "state_win", "state_conv", "page_table", "p_prompt", "p_sample",
          "ln_g", "w_in", "conv_w", "cmp_pos_k", "cmp_w1_k", "cmp_w2_k", "cmp_pos_v", "cmp_w1_v", "cmp_w2_v",
          "w_out_a", "w_out_b", "w_o", "w_ple", "w_ple_gate", "final_g"]
OUTPUTS = [("y_prompt", (1, SEQ, D)), ("y_sample", (NSEQ, TS, D)),
           ("new_kv_prompt", (NL, 1, SEQ, 4, GROUPS, HD)), ("new_kv_sample", (NL, NSEQ, TS, 4, GROUPS, HD)),
           ("new_win_prompt", (NL, 1, WIN, 2, GROUPS, HD)), ("new_win_sample", (NL, NSEQ, WIN, 2, GROUPS, HD)),
           ("new_conv_prompt", (NL, 1, 2, D)), ("new_conv_sample", (NL, NSEQ, 2, D))]


def kernel(**inputs):
    import concourse.bacc as bacc
    from concourse.bass_utils import run_bass_kernel_spmd

    nc = bacc.Bacc("TRN2", target_bir_lowering=False, num_devices=1)
    arrays, aps = {}, {}
    data = {name: np.ascontiguousarray(inputs[name]) for name in INPUTS}
    data["consts"] = constants()
    for name, x in data.items():
        arrays["in_" + name] = x
        aps[name] = nc.dram_tensor("in_" + name, x.shape, mybir.dt.from_np(x.dtype), kind="ExternalInput").ap()
    for name, shape in OUTPUTS:
        aps[name] = nc.dram_tensor("out_" + name, shape, F32, kind="ExternalOutput").ap()
    build(nc, aps)
    r = run_bass_kernel_spmd(nc, [arrays], core_ids=[0])
    return tuple(r.results[0]["out_" + name] for name, _ in OUTPUTS)
```

```python
from contextlib import ExitStack

import numpy as np

import concourse.bass as bass
from concourse import mybir

F32 = mybir.dt.float32
F32R = mybir.dt.float32r
BF16 = mybir.dt.bfloat16
I32 = mybir.dt.int32
ALU = mybir.AluOpType
ACT = mybir.ActivationFunctionType
AX = mybir.AxisListType
ds = bass.ds

P = 128
D = 1024
NL = 2
SEQ = 512
NSEQ, TS = 8, 4
NSAM = NSEQ * TS
TOK = SEQ + NSAM
HALF = TOK // 2
KT = D // P
NT = SEQ // P
HD = 64
GROUPS, REP = 4, 4
KV = GROUPS * HD
PAGE = 128
NPAGE = 8
PAST = PAGE * NPAGE
WIN = 512
PLE = 256
HC = 8
NWP = SEQ // 16 - 1
NWS = PAST // 16 - 1
HID = 256
SCALE = HD ** -0.5
NEG = -1e30
LOWEST = -1e29
EPS = 1e-6

C_BA, C_CA, C_XA, C_ZA, C_Q = 0, D, 2 * D, 3 * D, 4 * D
N_TM = D + 6 * KV + 48
C_ZB = C_Q + N_TM
C_MIX = C_ZB + D
IN_COLS = C_MIX + 2 * D
N_KVG = 6 * KV + 48
Z_KC, Z_VC, Z_KS, Z_VS, Z_KW, Z_VW, Z_G = (i * KV for i in range(7))
BW = 256
WW = 264
NQB, NKB = D // BW, N_KVG // WW
TM_BLOCKS = NQB + NKB
assert NKB * WW == N_KVG

B_CONV = 0
B_MA = 16
B_TM = 24
B_ZB = 34
B_MB = 38
B_WO = 46
B_PL = 50
NB = 58
PH = 15
C_IN = (2 * 256, 2 * 256 + 80)

def _const_layout():
    at, out = 0, {}
    for name, n in (("ident", P), ("ones", P), ("cos", 5 * 32), ("sin", 5 * 32), ("causal", P),
                    ("cmask", NT * 32), ("wmask", WIN), ("nmask", 4 * NSAM), ("gmask", 48), ("same", P),
                    ("iota", 16), ("pick", 4 * P), ("eps", 1)):
        out[name] = (at, n)
        at += n
    return out, at


CONST, NCONST = _const_layout()


def constants():
    c = np.zeros((P, NCONST), np.float32)

    def put(name, a):
        at, n = CONST[name]
        c[: a.shape[0], at:at + n] = a.reshape(a.shape[0], n)

    put("ident", np.eye(P, dtype=np.float32))
    put("ones", np.ones((P, P), np.float32))
    inv = np.power(10000.0, -np.arange(32) / 32).astype(np.float32)
    pos = np.concatenate([np.arange(SEQ), np.tile(PAST + np.arange(TS), NSEQ), np.zeros(P - NSAM)]).astype(np.float32)
    ang = (pos[:, None] * inv[None, :]).astype(np.float32).reshape(5, P, 32).transpose(1, 0, 2)
    put("cos", np.cos(ang))
    put("sin", np.sin(ang))
    q = np.arange(P)
    put("causal", np.where(q[:, None] >= q[None, :], 0.0, NEG).astype(np.float32))
    n = np.arange(32)
    qq = q[:, None, None] + P * np.arange(NT)[None, :, None]
    put("cmask", np.where((16 * n[None, None, :] + 31 <= qq) & (n < NWP)[None, None, :], 0.0, NEG).astype(np.float32))
    s2, g, t, r = np.unravel_index(q, (2, GROUPS, TS, REP))
    k, p = np.unravel_index(np.arange(WIN), (4, P))
    put("wmask", np.where((4 * p + k)[None, :] > t[:, None], 0.0, NEG).astype(np.float32))
    tok = np.arange(NSAM)
    nm = [np.where((tok[None, :] // TS == (2 * pair + s2)[:, None]) & (tok[None, :] % TS <= t[:, None]), 0.0, NEG)
          for pair in range(4)]
    put("nmask", np.stack(nm, 1).astype(np.float32))
    gr = np.arange(16)
    put("gmask", np.repeat((gr[None, :] == (g * REP + r)[:, None]).astype(np.float32)[:, :, None], 3, 2))
    key = (s2 * GROUPS + g) * TS + t
    put("same", (key[:, None] == key[None, :]).astype(np.float32))
    put("iota", np.tile(np.arange(16, dtype=np.float32), (P, 1)))
    pick = np.stack([(tok[:, None] == ((2 * pair + s2) * TS + t)[None, :]) for pair in range(4)], 1)
    put("pick", pick.astype(np.float32))
    put("eps", np.full((P, 1), EPS, np.float32))
    return c


def build(nc, a):
    ctx = ExitStack()
    with ctx:
        sems = []

        def sem(name, head_start=0):
            handle = ctx.enter_context(nc.semaphore(name))
            sems.append((handle, head_start))
            return handle

        def nth(semaphore, n):
            return n + sum(head for handle, head in sems if handle is semaphore)

        base = [16512]

        def fixed(name, shape, dt=F32):
            t = nc.alloc_sbuf_tensor_at(name, shape, dt, offset=base[0])
            base[0] += (4 * int(np.prod(shape[1:])) + 31) // 32 * 32
            return t

        xT = fixed("xT", [P, KT, TOK])
        m = fixed("m", [P, KT, TOK])
        rstd = fixed("rstd", [P, TOK])
        con = fixed("con", [P, NCONST])
        cols = fixed("cols", [P, KT, 21])
        qs = fixed("qs", [P, 2, 2, P])
        kcT_s = fixed("kcT_s", [P, 2, NSEQ, 64])
        kcT_p = fixed("kcT_p", [P, 2, 32])
        vc_s = fixed("vc_s", [64, NSEQ * KV])
        vc_p = fixed("vc_p", [P, KV])
        knT = fixed("knT", [P, 4, NSAM])
        qsT = fixed("qsT", [P, KT, NSAM])
        hb = fixed("hb", [P, 2])
        small = fixed("small", [P, 128])
        grow = fixed("grow", [P, 4, 3])
        mask2 = fixed("mask2", [P, 2, P], BF16)
        pages = fixed("pages", [1, NSEQ * NPAGE], I32)
        tails = fixed("tails", [P, KT, 18])
        cst = fixed("cst", [P, 2, 21])
        D0 = base[0]

        def at(name, shape, off, dt=F32):
            return nc.alloc_sbuf_tensor_at(name, shape, dt, offset=D0 + off)

        R_Z, R_A, R_T = 86272, 103680, 138496
        w_raw = at("w_raw", [P, 2, KT, WW], 0)
        wH = at("wH", [P, 2, KT, WW], 17152, F32R)
        wL = at("wL", [P, 2, KT, WW], 34304, F32R)
        hH = at("hH", [P, KT, TOK], 51456, F32R)
        hL = at("hL", [P, KT, TOK], 68864, F32R)
        zq = at("zq", [P, 5, D], R_Z)
        zk = at("zk", [P, 5, N_KVG], R_Z + 20480)
        aH = at("aH", [P, KT, TOK], R_A, F32R)
        aL = at("aL", [P, KT, TOK], R_A + 17408, F32R)
        yT = at("yT", [P, KT, TOK], R_Z)
        xin = at("xin", [P, 5, D], R_Z)
        cv_in = at("cv_in", [P, 4, 2, TOK], R_Z)
        UW = SEQ + 2 + NSEQ * 6
        cv_u = at("cv_u", [P, 2, UW], R_T)
        cv_y = at("cv_y", [P, UW], R_T + -(-2 * UW * 4 // 32) * 32)
        sq = at("sq", [P, 2, TOK], R_T)
        rows21 = at("rows21", [21, D], R_A)
        tail_rows = at("tail_rows", [18, D], R_T + 2048)
        rope_a = at("rope_a", [P, 2, 256], R_T)
        w1H = at("w1H", [P, 16, HID], 0, F32R)
        w1L = at("w1L", [P, 16, HID], 16384, F32R)
        chH = at("chH", [P, 2, 2, P, GROUPS], 32768, F32R)
        chL = at("chL", [P, 2, 2, P, GROUPS], 40960, F32R)
        craw = at("craw", [P, 2, 2, HC, KV], 49152)
        hidT = at("hidT", [P, 2, 504], 81920)
        hsg = at("hsg", [P, 2, 504], R_T)
        w2 = at("w2", [P, 2, HD], R_T + 4032)
        qT = at("qT", [P, KT, SEQ], 0)
        kT = at("kT", [P, 2, 2, SEQ], 16384)
        pr = at("pr", [P, 2, 2, SEQ], 24576)
        prT = at("prT", [P, 2, 2, SEQ], 32768)
        qst = at("qst", [P, 2, SEQ], 40960)
        cs = at("cs", [P, 2 * KT * NT, 32], 45056)
        cT = at("cT", [P, 2, KT, P], 53248)
        cTs = at("cTs", [P, 2, 2, P], 61440)
        cmx = at("cmx", [P, 2 * KT * NT], 63488)
        yy = at("yy", [P, 2, P], 63744)
        ow = at("ow", [P, 6, HD], 64768)
        skv = at("skv", [P, 2, 2, HC, 2 * KV], 0)
        swin = at("swin", [P, 2, 4, 2 * KV], 65536)
        R_S = R_Z + 20480
        skT = at("skT", [P, 2, 512], 81920)
        ssel = at("ssel", [P, PAST + NSAM], R_S)
        swsc = at("swsc", [P, WIN + NSAM], R_S + 4224)
        spT = at("spT", [P, 16, P], R_S + 6400)
        pc = at("pc", [P, 64], R_S + 14592)
        sy = at("sy", [P, KV], R_S + 14848)
        vcst = at("vcst", [64, 2 * KV], R_S + 15872)
        assert 15872 + 2048 <= 4 * N_KVG * 4
        t_f = at("t_f", [P, 2, TOK], R_T)
        pin = at("pin", [P, 5, PLE], R_Z)
        pH = at("pH", [P, 2, TOK], R_Z + 5120, F32R)
        pL = at("pL", [P, 2, TOK], R_Z + 9472, F32R)
        out_rows = at("out_rows", [P, 5, D], R_Z)

        ps = ctx.enter_context(nc.psum_tensor("ps", [P, 8, 512], F32))

        def C(name, rows=P):
            o, n = CONST[name]
            return con[0:rows, o:o + n]

        ident = C("ident")

        s_const, s_x, s_zero = sem("s_const"), sem("s_x"), sem("s_zero")
        passed = sem("passed")
        phase = sem("phase")
        w_in_sem = [sem("w_loaded0"), sem("w_loaded1")]
        w_hi = sem("w_hi")
        w_lo = sem("w_lo", 2)
        w_done = sem("w_done", 2)
        x_tp, x_free = sem("x_tp"), sem("x_free", 4)
        sq_ready, sq_used, ss_ready, std_ready = sem("sq_ready"), sem("sq_used", 2), sem("ss_ready"), sem("std_ready")
        st_in, st_tp = sem("st_in"), sem("st_tp")
        h_f, h_hi = sem("h_f"), sem("h_hi")
        cv, cv_act, cv_sg, cv_dve = sem("cv"), sem("cv_act", 8), sem("cv_sg"), sem("cv_dve", 8)
        cv_f, cv_hi, cv_used = sem("cv_f"), sem("cv_hi"), sem("cv_used", 2)
        mg, mg_sg, mg_dve = sem("mg"), sem("mg_sg"), sem("mg_dve", 4)
        tail_tp, tail_cp, tail_out = sem("tail_tp"), sem("tail_cp"), sem("tail_out")
        tm, tm_ev = sem("tm"), sem("tm_ev", 5)
        z_ready, kv_out = sem("z_ready"), sem("kv_out")
        pg_in, w1_in, w1_hi, w1_lo, w2_in = sem("pg_in"), sem("w1_in"), sem("w1_hi"), sem("w1_lo"), sem("w2_in")
        pos_ready = sem("pos_ready")
        c_in = [sem("chunks_loaded0"), sem("chunks_loaded1")]
        c_free = sem("c_free", 2)
        c_tp, c_hi, c_lo, c_mm = sem("c_tp"), sem("c_hi"), sem("c_lo", 4), sem("c_mm", 2)
        c_acc, c_sg, c_hid, c_w2, c_out = sem("c_acc"), sem("c_sg"), sem("c_hid", 2), sem("c_w2", 1), sem("c_out", 1)
        tp = [sem("tp_even"), sem("tp_odd")]
        tp_free = [sem("tp_even_free", 4), sem("tp_odd_free", 4)]
        pa_c, pa_csub, pa_cexp = sem("pa_c"), sem("pa_csub"), sem("pa_cexp")
        pa_cn, pa_ct = sem("pa_cn"), sem("pa_ct")
        pa_ctev = [sem("pa_ctev_act"), sem("pa_ctev_dve")]
        pa_q, pa_cst = sem("pa_q"), sem("pa_cst")
        pa_s = sem("pa_s")
        pa_nm = sem("pa_nm")
        pa_exp = sem("pa_exp", 4)
        pa_t, pa_te = sem("pa_t", 2), sem("pa_te", 4)
        pa_pv = sem("pa_pv", 2)
        pa_o, pa_y = sem("pa_o", 2), sem("pa_y", 2)
        pa_yt, pa_yo = sem("pa_yt", 1), sem("pa_yo", 3)
        s_kv = [sem("s_kv0"), sem("s_kv1")]
        s_win, s_winout, s_fin = sem("s_win"), sem("s_winout"), sem("s_fin", 2)
        sa_g, sa_gr, sa_q, sa_c, sa_nm, sa_cx = (sem(n) for n in ("sa_g", "sa_gr", "sa_q", "sa_c", "sa_nm", "sa_cx"))
        sa_kt, sa_ke, sa_s = sem("sa_kt"), sem("sa_ke", 2), sem("sa_s", 2)
        sa_im, sa_imp, sa_m, sa_e, sa_t, sa_te = (sem(n) for n in ("sa_im", "sa_imp", "sa_m", "sa_e", "sa_t", "sa_te"))
        sa_o, sa_y, sa_yt, sa_ys = (sem(n) for n in ("sa_o", "sa_y", "sa_yt", "sa_ys"))
        zb, zb_sg, zb_f, zb_hi, zb_done = sem("zb"), sem("zb_sg"), sem("zb_f"), sem("zb_hi"), sem("zb_done", 4)
        wo, wo_done = sem("wo"), sem("wo_done", 4)
        sp_hi, p_in, p_tp, p_hi = sem("sp_hi"), sem("p_in"), sem("p_tp"), sem("p_hi")
        pl, pl_sg, pl_done = sem("pl"), sem("pl_sg"), sem("pl_done", 2)
        y_ready, y_tp, y_act, y_dve, out_done = sem("y_ready"), sem("y_tp"), sem("y_act", 4), sem("y_dve", 4), sem("out_done")

        def phase_over(eng, l, k):
            eng.wait_ge(phase, 3 * (l * PH + k + 2))
            eng.sem_inc(passed, 1)

        def end_phase(eng, l, k):
            eng.drain().then_inc(phase, 1)
            phase_over(eng, l, k)

        def make_high(act, l, b, par, nk=KT, width=BW):
            act.wait_ge(w_in_sem[par], 64 * (l * (NB // 2) + b // 2 + 1 if isinstance(b, int) else l * (NB // 2) + b[1] + 1))
            act.wait_ge(w_done, nth(w_done, l * NB + blk(b) - 1))
            act.activation(wH[:, par, 0:nk, 0:width], w_raw[:, par, 0:nk, 0:width], ACT.Copy).then_inc(w_hi, 1)

        def make_low(dve, l, b, par, nk=KT, width=BW):
            dve.wait_ge(w_hi, l * NB + blk(b) + 1)
            dve.tensor_tensor(wL[:, par, 0:nk, 0:width], w_raw[:, par, 0:nk, 0:width],
                              wH[:, par, 0:nk, 0:width].bitcast(F32), ALU.subtract).then_inc(w_lo, 1)

        def blk(b):
            return b if isinstance(b, int) else 2 * b[1] + b[2]

        def pb(base_block, half, odd):
            return ("b", base_block // 2 + half, odd)

        def two(t, c):
            return t[:].rearrange("p k t -> p (k t)")[:, ds(c * TOK, TOK)].rearrange("p (a b) -> p a b", a=2)

        def one(t, c):
            return t[:].rearrange("p k t -> p (k t)")[:, ds(c * TOK, TOK)]

        def bank2(n):
            return ps[:, n:n + 2, 0:HALF]

        def halves(t):
            return t.rearrange("p (a b) -> p a b", a=2)

        block = ctx.enter_context(nc.Block())

        @block.sync
        def _(sp):
            sp.dma_start(con[:], a["consts"]).then_inc(s_const, 16)
            sp.dma_start(pages[:], a["page_table"].rearrange("(o a) b -> o (a b)", o=1)).then_inc(pg_in, 16)
            sp.dma_start(xin[:, 0:NT, :], a["x_prompt"].rearrange("b (t p) d -> p (b t) d", p=P)).then_inc(s_x, 16)
            sp.dma_start(xin[0:NSAM, NT, :], a["x_sample"].rearrange("b t d -> (b t) d")).then_inc(s_x, 16)
            sp.wait_ge(pg_in, 16)
            sp.wait_ge(s_zero, 1)

            def load_w(l, b, par, src, nk=KT, width=BW):
                sp.wait_ge(w_lo, nth(w_lo, l * NB + b - 1))
                sp.dma_start(w_raw[:, par, 0:nk, 0:width], src).then_inc(w_in_sem[par], 64)

            def w_cols(name, l, col, width=BW):
                w = a[name][ds(l, 1)].rearrange("l (k p) c -> p (l k) c", p=P)
                return w[:, :, ds(col, width)]

            def page_rows(l, seq, j, first, n):
                page = sp.value_load(pages[0:1, ds(seq * NPAGE + j, 1)], min_val=0, max_val=a["cache_kv"].shape[1] - 1)
                return a["cache_kv"][ds(l, 1), ds(page, 1), :, first:first + n].rearrange("l o (c t) s g d -> c (l o t) (s g d)", t=HC)

            with sp.Fori(0, NL) as l:
                phase_over(sp, l, -1)
                sp.dma_start(rows21[0:16, :], a["state_conv"][ds(l, 1)].rearrange("l b t c -> (l b t) c")).then_inc(st_in, 16)
                sp.dma_start(rows21[16:19, :], a["conv_w"][ds(l, 1)].rearrange("l t c -> (l t) c")).then_inc(st_in, 16)
                sp.dma_start(rows21[19:20, :], a["ln_g"][ds(l, 1)]).then_inc(st_in, 16)
                sp.dma_start(rows21[20:21, :], a["final_g"].rearrange("(o d) -> o d", o=1)).then_inc(st_in, 16)
                with sp.Fori(0, 4) as i:
                    for n, c0 in enumerate((C_CA, C_XA, C_BA, C_ZA)):
                        load_w(l, B_CONV + 4 * i + n, n % 2, w_cols("w_in", l, c0 + BW * i))
                with sp.Fori(0, 4) as i:
                    load_w(l, B_MA + 2 * i, 0, w_cols("w_in", l, C_MIX + BW * i))
                    load_w(l, B_MA + 2 * i + 1, 1, w_cols("w_out_a", l, BW * i))
                with sp.Fori(0, NQB // 2) as i:
                    for n in range(2):
                        load_w(l, B_TM + 2 * i + n, n, w_cols("w_in", l, 2 * BW * i + C_Q + n * BW, WW), width=WW)
                with sp.Fori(0, NKB // 2) as i:
                    for n in range(2):
                        load_w(l, B_TM + NQB + 2 * i + n, n, w_cols("w_in", l, 2 * WW * i + C_Q + D + n * WW, WW), width=WW)
                sp.wait_ge(z_ready, l + 1)
                sp.dma_start(a["new_kv_prompt"][ds(l, 1)].rearrange("l b (t p) s g d -> p (l b t) (s g d)", p=P),
                             zk[:, 0:NT, 0:4 * KV]).then_inc(kv_out, 16)
                sp.dma_start(a["new_win_prompt"][ds(l, 1)].rearrange("l b (t p) s g d -> p (l b t) (s g d)", p=P),
                             zk[:, 0:NT, Z_KW:Z_KW + 2 * KV]).then_inc(kv_out, 16)
                sp.dma_start(a["new_kv_sample"][ds(l, 1)].rearrange("l b t s g d -> (l b t) (s g d)"),
                             zk[0:NSAM, NT, 0:4 * KV]).then_inc(kv_out, 16)
                sp.dma_start(a["new_win_sample"][ds(l, 1), :, WIN - TS:WIN].rearrange("l b t s g d -> (l b) t (s g d)"),
                             zk[0:NSAM, NT, Z_KW:Z_KW + 2 * KV]).then_inc(kv_out, 16)
                sp.wait_ge(kv_out, 64 * l + 64)

                phase_over(sp, l, 3)
                for kv, (w1, w2n, pos) in enumerate((("cmp_w1_k", "cmp_w2_k", "cmp_pos_k"), ("cmp_w1_v", "cmp_w2_v", "cmp_pos_v"))):
                    sp.wait_ge(c_free, nth(c_free, 10 * l + 4 * kv))
                    sp.dma_start(craw[:, 0].rearrange("p s t c -> p (s t c)").rearrange("p (k h) -> p k h", k=16),
                                 a[w1][ds(l, 1)].rearrange("l (k s) d h -> (s d) (l k) h", s=2)).then_inc(w1_in, 16)
                    sp.wait_ge(c_free, nth(c_free, 10 * l + 5 * kv))
                    sp.dma_start(craw[0:64, 1, 0],
                                 a["new_kv_prompt"][ds(l, 1), :, :, kv].rearrange("l b (c t) g d -> c (l b t) (g d)", t=HC)).then_inc(c_in[1], 16)
                    for g in range(GROUPS):
                        sp.dma_start(craw[64:68, 1, 0, :, g * HD:(g + 1) * HD],
                                     a[pos][ds(l, 1)].rearrange("l (c t) d -> (l c) t d", t=HC)).then_inc(c_in[1], 16)
                    sp.wait_ge(c_w2, nth(c_w2, 10 * l + 5 * kv))
                    sp.dma_start(w2[:], a[w2n][ds(l, 1)].rearrange("l (k p) d -> p (l k) d", p=P)).then_inc(w2_in, 16)
                    sp.wait_ge(w1_lo, 8 * l + (4 * kv + 4))
                    sp.sem_inc(passed, 1)
                    with sp.Fori(0, 2) as pp:
                        for par in range(2):
                            sp.wait_ge(c_free, nth(c_free, 10 * l + 2 * pp + (kv * 5 + par)))
                            for s in range(2):
                                for j in range(NPAGE):
                                    src = page_rows(l, 4 * pp + (2 * par + s), j, kv, 1)
                                    sp.dma_start(craw[16 * j:16 * j + 16, par, s], src).then_inc(c_in[par], 16)

                phase_over(sp, l, 7)
                sp.wait_ge(pa_cst, 9 * l + 9)
                sp.sem_inc(passed, 1)
                with sp.Fori(0, 2) as pp:
                    for par in range(2):
                        sp.wait_ge(s_fin, nth(s_fin, 4 * l + 2 * pp + (par - 1)))
                        for s in range(2):
                            for j in range(NPAGE):
                                src = page_rows(l, 4 * pp + (2 * par + s), j, 2, 2)
                                sp.dma_start(skv[16 * j:16 * j + 16, par, s], src).then_inc(s_kv[par], 16)

                phase_over(sp, l, 8)
                with sp.Fori(0, 2) as gp:
                    for n in range(2):
                        sp.wait_ge(w_lo, nth(w_lo, l * NB + 2 * gp + (B_ZB + n - 1)))
                        src = w_cols("w_in", l, 512 * gp + C_ZB, 512)
                        for g in range(2):
                            for jj in range(2):
                                to, frm = jj * P + g * HD, g * KV + (2 * n + jj) * HD
                                sp.dma_start(w_raw[:, n, :, to:to + HD], src[:, :, frm:frm + HD]).then_inc(w_in_sem[n], 16)
                with sp.Fori(0, 4) as i:
                    load_w(l, B_MB + 2 * i, 0, w_cols("w_in", l, BW * i + (C_MIX + D)))
                    sp.wait_ge(w_lo, nth(w_lo, l * NB + 2 * i + B_MB))
                    for g in range(2):
                        for gp in range(2):
                            rows = a["w_out_b"][ds(l, 1), 512 * gp + KV * g:512 * gp + KV * g + KV].rearrange("l (c d) n -> d (l c) n", d=HD)
                            sp.dma_start(w_raw[g * 64:(g + 1) * 64, 1, 4 * gp:4 * gp + 4, 0:BW], rows[:, :, ds(BW * i, BW)]).then_inc(w_in_sem[1], 16)
                with sp.Fori(0, 2) as i:
                    for n in range(2):
                        load_w(l, B_WO + 2 * i + n, n, w_cols("w_o", l, 2 * BW * i + BW * n))
                with sp.Fori(0, 4) as i:
                    load_w(l, B_PL + 2 * i, 0, w_cols("w_ple_gate", l, BW * i))
                    load_w(l, B_PL + 2 * i + 1, 1, w_cols("w_ple", l, BW * i), nk=2)

            for tt in range(5):
                sp.wait_ge(y_act, nth(y_act, tt + 1))
                sp.wait_ge(y_dve, nth(y_dve, tt + 1))
                if tt < NT:
                    sp.dma_start(a["y_prompt"][0, tt * P:(tt + 1) * P, :], out_rows[:, tt, :]).then_inc(out_done, 16)
                else:
                    sp.dma_start(a["y_sample"].rearrange("b t d -> (b t) d"), out_rows[0:NSAM, tt, :]).then_inc(out_done, 16)
            sp.wait_ge(out_done, 80)

        @block.gpsimd
        def _(pool):
            for handle, head_start in sems:
                if head_start:
                    pool.sem_inc(handle, head_start)
            pool.memset(qs[:], 0.0)
            pool.memset(vc_p[:], 0.0)
            pool.memset(kcT_p[:], 0.0)
            pool.memset(small[:], 0.0)
            pool.drain()
            pool.memset(small[:, 24:30], 1.0)
            pool.memset(small[:, 76:79], 1.0)
            pool.drain().then_inc(s_zero, 1)
            with pool.Fori(0, NL) as l:
                pool.wait_ge(tail_cp, 2 * l + 2)
                pool.dma_start(a["new_conv_prompt"][ds(l, 1)].rearrange("l b t c -> (l b t) c"), tail_rows[0:2, :]).then_inc(tail_out, 16)
                pool.dma_start(a["new_conv_sample"][ds(l, 1)].rearrange("l b t c -> (l b t) c"), tail_rows[2:18, :]).then_inc(tail_out, 16)
                pool.wait_ge(tail_out, 32 * l + 32)
                flat_q, flat_c = qT[:].rearrange("p k t -> p (k t)"), cT[:].rearrange("p g h q -> p g (h q)")
                phase_over(pool, l, 6)
                pool.tensor_copy(qst[:, 0, :], qT[:, 0, :]).then_inc(pa_q, 1)
                for n in range(2):
                    pool.wait_ge(pa_ctev[n], l + 1)
                pool.sem_inc(passed, 1)
                pool.tensor_copy(cTs[:, 0], cT[:, :, 0, :]).then_inc(pa_cst, 1)
                with pool.Fori(0, REP) as r:
                    for gp in range(2):
                        pool.wait_ge(pa_pv, nth(pa_pv, 64 * l + 16 * r + 8 * gp))
                        pool.sem_inc(passed, 1)
                        head = (REP, 1)[gp]
                        pool.tensor_copy(qst[:, 1 - gp, :], flat_q[:, ds(SEQ * r + SEQ * head, SEQ)]).then_inc(pa_q, 1)
                        pool.tensor_copy(cTs[:, 1 - gp], flat_c[:, :, ds(P * r + P * head, P)]).then_inc(pa_cst, 1)
                phase_over(pool, l, 7)
                with pool.Fori(0, 4) as pair:
                    pool.wait_ge(s_fin, nth(s_fin, 4 * l + pair))
                    for s in range(2):
                        pool.dma_start(swin[:, s].rearrange("p k c -> p (k c)"),
                                       a["state_win"][ds(l, 1), ds(2 * pair + s, 1)].rearrange("l b (p k) s g d -> (l b p) (k s g d)", k=4)
                                       ).then_inc(s_win, 16)
                    pool.wait_ge(s_win, 128 * l + 32 * pair + 32)
                    pool.sem_inc(passed, 1)
                    for s in range(2):
                        dst = a["new_win_sample"][ds(l, 1), ds(2 * pair + s, 1), 0:WIN - TS].rearrange("l b (p k) s g d -> (l b p) (k s g d)", k=4)
                        for lo, hi in ((1, 113), (113, 128)):
                            pool.dma_start(dst[lo - 1:hi - 1], swin[lo:hi, s].rearrange("p k c -> p (k c)")).then_inc(s_winout, 16)
                    pool.wait_ge(s_winout, 256 * l + 64 * pair + 64)
                phase_over(pool, l, 10)
                pool.dma_start(pin[:, 0:NT, :], a["p_prompt"][ds(l, 1)].rearrange("l b (t p) d -> p (l b t) d", p=P)).then_inc(p_in, 16)
                pool.dma_start(pin[0:NSAM, NT, :], a["p_sample"][ds(l, 1)].rearrange("l b t d -> (l b t) d")).then_inc(p_in, 16)

        @block.tensor
        def _(pe):
            def norm_sum(l):
                for c in range(KT):
                    pe.wait_ge(sq_ready, l * KT + c + 1)
                    for hf in range(2):
                        last = nc.tensor.matmul(ps[:, hf, 0:HALF], C("ones"), sq[:, c % 2, hf * HALF:(hf + 1) * HALF],
                                                start=c == 0, stop=c == KT - 1)
                    last.then_inc(sq_used, 1)
                pe.drain().then_inc(ss_ready, 1)

            def fm_tile(par, jj, bank, xH, xL, nk=KT):
                for k in range(nk):
                    for w, x in ((wH, xH), (wH, xL), (wL, xH)):
                        st = w[:, par, k, jj * P:(jj + 1) * P]
                        for hf in range(2):
                            last = nc.tensor.matmul(ps[:, bank + hf, 0:HALF], st, x[:, k, hf * HALF:(hf + 1) * HALF],
                                                    start=k == 0 and w is wH and x is xH, stop=k == nk - 1 and w is wL)
                return last

            pe.wait_ge(s_const, 16)
            pe.wait_ge(s_x, 32)
            for c in range(KT):
                pe.wait_ge(x_free, nth(x_free, c - 3))
                for tt in range(5):
                    rows = P if tt < NT else NSAM
                    last = nc.tensor.transpose(ps[:, 2 * (c % 4) + tt // NT, (tt % NT) * P:(tt % NT) * P + rows],
                                               xin[0:rows, tt, c * P:(c + 1) * P], ident[0:rows, 0:rows])
                last.then_inc(x_tp, 1)
            end_phase(pe, 0, -1)

            with pe.Fori(0, NL) as l:
                pe.wait_ge(st_in, 64 * l + 64)
                pe.sem_inc(passed, 1)
                for c in range(KT):
                    last = nc.tensor.transpose(ps[:, 2, c * 21:(c + 1) * 21], rows21[:, c * P:(c + 1) * P], ident[0:21, 0:21])
                last.then_inc(st_tp, 1)
                norm_sum(l)
                end_phase(pe, l, 0)
                with pe.Fori(0, 4) as i:
                    for kind in range(4):
                        pe.wait_ge(w_lo, nth(w_lo, l * NB + 4 * i + (B_CONV + kind + 1)))
                        for jj in range(2):
                            q = 2 * kind + jj
                            if kind == 0:
                                pe.wait_ge(cv_act, nth(cv_act, 24 * l + 6 * i + (jj - 1)))
                            elif kind == 1:
                                pe.wait_ge(cv_dve, nth(cv_dve, 8 * l + 2 * i + (jj - 1)))
                            else:
                                pe.wait_ge(cv_act, nth(cv_act, 24 * l + 6 * i + (q - 3)))
                            last = fm_tile(kind % 2, jj, 2 * (q % 4), hH, hL)
                            if jj == 0:
                                last.then_inc(cv, 1)
                        last.then_inc(cv, 1)
                        pe.drain().then_inc(w_done, 1)
                end_phase(pe, l, 1)

                def merge(which, first_block, gate, branch):
                    with pe.Fori(0, 4) as i:
                        for n in range(2):
                            pe.wait_ge(w_lo, nth(w_lo, l * NB + 2 * i + (first_block + n + 1)))
                            for jj in range(2):
                                pe.wait_ge(mg_dve, nth(mg_dve, 16 * l + 2 * i + (8 * which + jj - 1)))
                                last = fm_tile(n, jj, 2 * (2 * n + jj), *(branch if n else gate))
                                last.then_inc(mg, 1)
                            pe.drain().then_inc(w_done, 1)

                merge(0, B_MA, (hH, hL), (aH, aL))
                end_phase(pe, l, 2)
                for c in range(KT):
                    last = nc.tensor.transpose(ps[0:18, 6 + c // 4, (c % 4) * P:(c % 4 + 1) * P], tails[:, c, :], ident)
                last.then_inc(tail_tp, 1)

                def token_major(b, half, n, width):
                    pe.wait_ge(w_lo, nth(w_lo, l * NB + 2 * half + (B_TM + b + n + 1)))
                    for tt in range(5):
                        rows = P if tt < NT else NSAM
                        pe.wait_ge(tm_ev, nth(tm_ev, l * (5 * TM_BLOCKS) + 10 * half + (5 * (b + n) + tt - 4)))
                        for k in range(KT):
                            for w, x in ((wH, hH), (wL, hH), (wH, hL)):
                                last = nc.tensor.matmul(ps[0:rows, tt, 0:width], x[:, k, tt * P:tt * P + rows], w[:, n, k, 0:width],
                                                        start=k == 0 and w is wH and x is hH, stop=k == KT - 1 and x is hL)
                        last.then_inc(tm, 1)
                    pe.drain().then_inc(w_done, 1)

                with pe.Fori(0, NQB // 2) as i:
                    for n in range(2):
                        token_major(0, i, n, BW)
                with pe.Fori(0, NKB // 2) as i:
                    for n in range(2):
                        token_major(NQB, i, n, WW)
                end_phase(pe, l, 3)

                for kv in range(2):
                    def chunk_tp(unit, j, slot, rows, nseq):
                        for s in range(nseq):
                            pe.wait_ge(c_lo, nth(c_lo, 8 * unit + (2 * j + s - 3)))
                            for n in range(4):
                                t, g2 = n // 2, n % 2
                                last = nc.tensor.transpose(ps[:, (2 * j + s) % 4, n * P:n * P + rows],
                                                           craw[0:rows, slot, s, 2 * j + t, g2 * P:(g2 + 1) * P], ident[0:rows, 0:rows])
                            last.then_inc(c_tp, 1)
                        if nseq == 1:
                            pe.drain().then_inc(c_tp, 1)

                    def project(unit, nseq, nwin):
                        n = nseq * nwin * GROUPS
                        pe.wait_ge(c_hid, nth(c_hid, 2 * unit + 2))
                        pe.wait_ge(c_out, nth(c_out, unit))
                        if kv == 0:
                            for hid in range(2):
                                last = nc.tensor.matmul(ps[0:HD, 6, 0:n], w2[:, hid, :], hidT[:, hid, 0:n], start=hid == 0, stop=hid == 1)
                        else:
                            for s in range(nseq):
                                for g in range(GROUPS):
                                    first = s * nwin * GROUPS + g
                                    o = (s * GROUPS + g) * HD
                                    for hid in range(2):
                                        last = nc.tensor.matmul(ps[0:nwin, 6, o:o + HD],
                                                                hidT[:, hid, first:first + (nwin - 1) * GROUPS + 1:GROUPS], w2[:, hid, :],
                                                                start=hid == 0, stop=hid == 1)
                        last.then_inc(c_w2, 1)

                    def compress(unit, slot, rows, nseq, nwin, before=None):
                        chunk_tp(unit, 0, slot, rows, nseq)
                        chunk_tp(unit, 1, slot, rows, nseq)
                        if before:
                            project(unit - 1, *before)
                        for j in range(4):
                            if 0 < j < 3:
                                chunk_tp(unit, j + 1, slot, rows, nseq)
                            if j == 2:
                                pe.drain().then_inc(c_free, 1)
                            pe.wait_ge(c_lo, nth(c_lo, 8 * unit + (2 * j + 2)))
                            if j == 0:
                                pe.wait_ge(c_hid, nth(c_hid, 2 * unit))
                            for hid in range(2):
                                for quarter in range(4):
                                    for w, x in ((w1H, chH), (w1H, chL), (w1L, chH)):
                                        span = slice(quarter, quarter + 2 * nwin - 1, 2)
                                        rhs = x[:, j % 2, :, span, :] if nseq == 2 else x[:, j % 2, 0, span, :]
                                        last = nc.tensor.matmul(ps[:, 4 + hid, 0:nseq * nwin * GROUPS],
                                                                w[:, 4 * quarter + j, hid * P:(hid + 1) * P], rhs,
                                                                start=j == 0 and quarter == 0 and w is w1H and x is chH,
                                                                stop=j == 3 and quarter == 3 and w is w1L)
                            last.then_inc(c_mm, 1)
                        pe.drain().then_inc(c_acc, 1)

                    pe.wait_ge(c_in[1], C_IN[1] * (2 * l + kv) + 80)
                    pe.wait_ge(w1_lo, 8 * l + (4 * kv + 4))
                    pe.wait_ge(w2_in, 32 * l + (16 * kv + 16))
                    compress(10 * l + 5 * kv, 1, 68, 1, NWP + 2)
                    project(10 * l + 5 * kv, 1, NWP)
                    with pe.Fori(0, 2) as pp:
                        for par in range(2):
                            unit = 10 * l + 2 * pp + (5 * kv + par + 1)
                            if par == 0:
                                pe.wait_ge(c_in[0], C_IN[0] * (2 * l + kv) + 256 * pp + 256)
                            else:
                                pe.wait_ge(c_in[1], C_IN[1] * (2 * l + kv) + 256 * pp + (256 + 80))
                            compress(unit, par, P, 2, NWS, before=(2, NWS) if par else None)
                            if par == 1:
                                project(unit, 2, NWS)
                end_phase(pe, l, 4)
                end_phase(pe, l, 5)

                def tp_job(k, parts):
                    pe.wait_ge(tp_free[k % 2], nth(tp_free[k % 2], 7 * l + (k // 2 - 3)))
                    pe.sem_inc(passed, 1)
                    for out, src, n in parts:
                        last = nc.tensor.transpose(out, src, ident[0:n, 0:n])
                    last.then_inc(tp[k % 2], 1)

                def q_cols(tt, rows, gp, r):
                    return zq[0:rows, tt, (4 * gp + r) * P:(4 * gp + r + 1) * P]

                for k in range(8):
                    tp_job(k, [(ps[:, k % 8, tt * P:(tt + 1) * P], q_cols(tt, P, k // 4, k % 4), P) for tt in range(NT)])
                for k in range(8, 12):
                    c0 = (Z_KS, Z_KW)[(k - 8) // 2] + (k % 2) * P
                    tp_job(k, [(ps[:, k % 8, tt * P:(tt + 1) * P], zk[:, tt, c0:c0 + P], P) for tt in range(NT)])
                tp_job(12, [(ps[:, 4, n * NSAM:(n + 1) * NSAM], q_cols(NT, NSAM, n // 4, n % 4), NSAM) for n in range(8)])
                tp_job(13, [(ps[:, 5, n * NSAM:(n + 1) * NSAM],
                             zk[0:NSAM, NT, (Z_KS, Z_KW)[n // 2] + (n % 2) * P:(Z_KS, Z_KW)[n // 2] + (n % 2 + 1) * P], NSAM) for n in range(4)])
                end_phase(pe, l, 6)

                for g in range(2):
                    rows = slice(64 * g, 64 * g + 64)
                    for h in range(KT):
                        for u in range(NT):
                            o = (h * NT + u) * 32
                            last = nc.tensor.matmul(ps[:, 4 + 2 * g + o // 512, o % 512:o % 512 + 32], qT[rows, h, u * P:(u + 1) * P],
                                                    kcT_p[rows, h // REP, :], start=True, stop=True)
                last.then_inc(pa_c, 1)

                def scores(first, gp, k):
                    g, u = k % 2, k % 8 // 2
                    gp = (gp + k // 8) % 2
                    rows = slice(64 * g, 64 * g + 64)
                    pe.wait_ge(pa_exp, nth(pa_exp, 130 * l + 2 * first + (2 * k - 2)))
                    for br in range(2):
                        nc.tensor.matmul(ps[:, 2 * g + br, u * P:(u + 1) * P], mask2[:, 0, :], mask2[:, 1, :], start=True, stop=False)
                        last = nc.tensor.matmul(ps[:, 2 * g + br, u * P:(u + 1) * P], qst[rows, gp, u * P:(u + 1) * P], kT[rows, br, gp, u * P:(u + 1) * P],
                                         start=False, stop=True)
                        if u:
                            last = nc.tensor.matmul(ps[:, 2 * g + br, 0:u * P], qst[rows, gp, u * P:(u + 1) * P], kT[rows, br, gp, 0:u * P],
                                                    start=True, stop=True)
                    last.then_inc(pa_s, 1)

                def y_back(tile, bank):
                    pe.wait_ge(pa_y, nth(pa_y, tile))
                    nc.tensor.transpose(ps[:, bank, 384:512], yy[:, bank % 2, :], ident).then_inc(pa_yt, 1)

                pe.wait_ge(pa_q, 9 * l + 1)
                scores(0, 0, 0)
                scores(0, 0, 1)
                pe.wait_ge(pa_cn, l + 1)
                for n in range(2 * KT):
                    last = nc.tensor.transpose(ps[:, 4 + n // 4, (n % 4) * P:(n % 4 + 1) * P],
                                               cs[:, 4 * n:4 * n + 4, :].rearrange("p a b -> p (a b)"), ident)
                last.then_inc(pa_ct, 1)
                for n in range(2):
                    pe.wait_ge(pa_ctev[n], l + 1)
                pe.sem_inc(passed, 1)
                def turn(unit, k, n):
                    u = k // 2
                    br, kt = divmod(n, u + 1)
                    if kt == 0:
                        pe.wait_ge(pa_exp, nth(pa_exp, 2 * unit + (2 * k + br + 1) + 2 * l))
                        pe.wait_ge(pa_te, nth(pa_te, 2 * unit + (2 * k + br - 1)))
                    last = nc.tensor.transpose(ps[:, 4 + br, kt * P:(kt + 1) * P], pr[:, k % 2, br, kt * P:(kt + 1) * P], ident)
                    if kt == u:
                        last.then_inc(pa_t, 1)

                def output(unit, gp, k, n):
                    g, u = k % 2, k // 2
                    head = 2 * gp + g
                    if n == 0:
                        q4 = slice(32 * u, 32 * u + 32)
                        nc.tensor.matmul(ps[:, 6 + u % 2, g * 3 * HD:g * 3 * HD + HD], cTs[q4, gp, g, :], vc_p[q4, head * HD:(head + 1) * HD],
                                         start=True, stop=True)
                        return
                    br, kt = divmod(n - 1, u + 1)
                    if kt == 0:
                        pe.wait_ge(pa_te, nth(pa_te, 2 * unit + (2 * k + br + 1)))
                    o, c0 = (g * 3 + br + 1) * HD, (Z_VS, Z_VW)[br] + head * HD
                    last = nc.tensor.matmul(ps[:, 6 + u % 2, o:o + HD], prT[:, k % 2, br, kt * P:(kt + 1) * P], zk[:, kt, c0:c0 + HD],
                                            start=kt == 0, stop=kt == u)
                    if n == 2 * (u + 1):
                        last.then_inc(pa_pv, 1)

                with pe.Fori(0, REP) as r:
                    for gp in range(2):
                        unit = 64 * l + 16 * r + 8 * gp
                        for k in range(9):
                            if k % 2 == 0 and k < 8:
                                y_back(32 * l + 8 * r + (4 * gp + (k - 4) // 2 + 1), 6 + (k // 2) % 2)
                            if k == 1:
                                pe.wait_ge(pa_cst, 9 * l + 2 * r + (gp + 1))
                            if k % 2 == 1:
                                pe.wait_ge(pa_yo, nth(pa_yo, 34 * l + 8 * r + (4 * gp + (k - 1) // 2 + 1)))
                            turns = 2 * (k // 2 + 1) if k < 8 else 0
                            outputs = 2 * ((k - 1) // 2 + 1) + 1 if k else 0
                            for n in range(max(turns, outputs)):
                                if n < turns:
                                    turn(unit, k, n)
                                if n < outputs:
                                    output(unit, gp, k - 1, n)
                            if k == 6:
                                pe.wait_ge(pa_q, 9 * l + 2 * r + (gp + 2))
                            if k < 8:
                                scores(16 * r + 8 * gp, gp, k + 2)
                y_back(32 * l + 31, 6)
                y_back(32 * l + 32, 7)
                end_phase(pe, l, 7)

                for pair in range(4):
                    last = nc.tensor.matmul(ps[:, 7, pair * 48:(pair + 1) * 48], C("pick", NSAM)[:, pair * P:(pair + 1) * P],
                                            zk[0:NSAM, NT, Z_G:Z_G + 48], start=True, stop=True)
                last.then_inc(sa_g, 1)
                pe.wait_ge(sa_gr, l + 1)
                pe.sem_inc(passed, 1)
                with pe.Fori(0, 2) as pp:
                    for par in range(2):
                        it = 4 * l + 2 * pp + par
                        pe.wait_ge(sa_q, it + 1)
                        for s in range(2):
                            for gp in range(2):
                                nc.tensor.matmul(ps[:, 3, 0:NWS], qs[:, gp, s, :], kcT_s[:, gp, ds(4 * pp + (2 * par + s), 1), 0:NWS],
                                                 start=s + gp == 0, stop=s + gp == 2)
                        for br in range(2):
                            for s in range(2):
                                for gp in range(2):
                                    last = nc.tensor.matmul(ps[:, 3, 64 + br * NSAM:64 + (br + 1) * NSAM], qs[:, gp, s, :], knT[:, 2 * br + gp, :],
                                                            start=s + gp == 0, stop=s + gp == 2)
                        last.then_inc(sa_c, 1)
                        jobs = [(half, s, gp) for half in range(3) for s in range(2) for gp in range(2)]

                        def key_tp(k):
                            half, s, gp = jobs[k]
                            pe.wait_ge(sa_ke, nth(sa_ke, 12 * it + (k - 1)))
                            if k == 0:
                                pe.wait_ge(s_kv[par], 512 * l + 256 * pp + 256)
                            if k == 8:
                                pe.wait_ge(s_win, 32 * it + 32)
                            for t in range(4):
                                src = swin[:, s, t, gp * P:(gp + 1) * P] if half == 2 else skv[:, par, s, 4 * half + t, gp * P:(gp + 1) * P]
                                last = nc.tensor.transpose(ps[:, 4 + k % 2, t * P:(t + 1) * P], src, ident)
                            last.then_inc(sa_kt, 1)

                        key_tp(0)
                        for k, (half, s, gp) in enumerate(jobs):
                            if k + 1 < len(jobs):
                                key_tp(k + 1)
                            pe.wait_ge(sa_ke, nth(sa_ke, 12 * it + (k + 1)))
                            nc.tensor.matmul(ps[:, half, :], qs[:, gp, s, :], skT[:, k % 2, :], start=s + gp == 0, stop=s + gp == 2
                                             ).then_inc(sa_s, 1)
                            if k == 4:
                                pe.wait_ge(sa_im, it + 1)
                                nc.tensor.matmul(ps[:, 3, 256:270], C("same"), small[:, 32:46], start=True, stop=True).then_inc(sa_imp, 1)
                        pe.wait_ge(sa_e, 2 * it + 1)
                        pe.sem_inc(passed, 1)
                        nc.tensor.transpose(ps[0:NWS, 4, 0:P], pc[:, 0:NWS], ident)
                        nc.tensor.transpose(ps[0:NSAM, 4, P:2 * P], ssel[:, PAST:PAST + NSAM], ident).then_inc(sa_t, 1)
                        for half in range(2):
                            if half:
                                pe.wait_ge(sa_te, 5 * it + 1)
                            for t in range(4):
                                o = (4 * half + t) * P
                                last = nc.tensor.transpose(ps[:, 5 - half, t * P:(t + 1) * P], ssel[:, o:o + P], ident)
                            last.then_inc(sa_t, 1)
                        pe.wait_ge(sa_e, 2 * it + 2)
                        pe.wait_ge(sa_te, 5 * it + 2)
                        for t in range(4):
                            last = nc.tensor.transpose(ps[:, 5, t * P:(t + 1) * P], swsc[:, t * P:(t + 1) * P], ident)
                        last.then_inc(sa_t, 1)
                        pe.wait_ge(sa_te, 5 * it + 3)
                        pe.sem_inc(passed, 1)
                        nc.tensor.transpose(ps[0:NSAM, 4, 0:P], swsc[:, WIN:WIN + NSAM], ident).then_inc(sa_t, 1)
                        for s in range(2):
                            rows = slice(64 * s, 64 * s + 64)
                            nc.tensor.matmul(ps[rows, 6, 0:KV], spT[0:NWS, 13, rows], vcst[0:NWS, s * KV:(s + 1) * KV], start=True, stop=True)
                            for t in range(8):
                                nc.tensor.matmul(ps[rows, 6, KV:2 * KV], spT[:, t, rows], skv[:, par, s, t, KV:2 * KV], start=t == 0, stop=False)
                            nc.tensor.matmul(ps[rows, 6, KV:2 * KV], spT[0:NSAM, 12, rows], zk[0:NSAM, NT, Z_VS:Z_VS + KV], start=False, stop=True)
                        pe.wait_ge(sa_te, 5 * it + 5)
                        for s in range(2):
                            rows = slice(64 * s, 64 * s + 64)
                            for t in range(4):
                                nc.tensor.matmul(ps[rows, 7, 0:KV], spT[:, 8 + t, rows], swin[:, s, t, KV:2 * KV], start=t == 0, stop=False)
                            last = nc.tensor.matmul(ps[rows, 7, 0:KV], spT[0:NSAM, 14, rows], zk[0:NSAM, NT, Z_VW:Z_VW + KV], start=False, stop=True)
                        last.then_inc(sa_o, 1)
                        pe.drain().then_inc(s_fin, 1)
                        pe.wait_ge(sa_y, it + 1)
                        for gp in range(2):
                            last = nc.tensor.transpose(ps[:, 5, gp * P:(gp + 1) * P], sy[:, gp * P:(gp + 1) * P], ident)
                        last.then_inc(sa_yt, 1)
                        pe.wait_ge(sa_ys, it + 1)
                end_phase(pe, l, 8)

                end_phase(pe, l, 9)
                with pe.Fori(0, 2) as i:
                    for n in range(2):
                        pe.wait_ge(w_lo, nth(w_lo, l * NB + 2 * i + (B_ZB + n + 1)))
                        for jj in range(2):
                            pe.wait_ge(zb_done, nth(zb_done, 8 * l + 4 * i + (2 * n + jj - 3)))
                            fm_tile(n, jj, 2 * (2 * n + jj), hH, hL).then_inc(zb, 1)
                        pe.drain().then_inc(w_done, 1)
                end_phase(pe, l, 10)
                merge(1, B_MB, (hH, hL), (aH, aL))
                end_phase(pe, l, 11)
                end_phase(pe, l, 12)
                with pe.Fori(0, 2) as i:
                    for n in range(2):
                        pe.wait_ge(w_lo, nth(w_lo, l * NB + 2 * i + (B_WO + n + 1)))
                        for jj in range(2):
                            pe.wait_ge(wo_done, nth(wo_done, 8 * l + 4 * i + (2 * n + jj - 3)))
                            fm_tile(n, jj, 2 * (2 * n + jj), aH, aL).then_inc(wo, 1)
                        pe.drain().then_inc(w_done, 1)
                pe.wait_ge(p_in, 32 * l + 32)
                pe.wait_ge(wo_done, nth(wo_done, 8 * l + 8))
                for c in range(2):
                    for tt in range(5):
                        rows = P if tt < NT else NSAM
                        last = nc.tensor.transpose(ps[:, 2 * c + tt // NT, (tt % NT) * P:(tt % NT) * P + rows],
                                                   pin[0:rows, tt, c * P:(c + 1) * P], ident[0:rows, 0:rows])
                last.then_inc(p_tp, 1)
                end_phase(pe, l, 13)
                with pe.Fori(0, 4) as i:
                    for n in range(2):
                        pe.wait_ge(w_lo, nth(w_lo, l * NB + 2 * i + (B_PL + n + 1)))
                        for jj in range(2):
                            pe.wait_ge(pl_done, nth(pl_done, 8 * l + 2 * i + (jj - 1)))
                            last = fm_tile(n, jj, 2 * (2 * n + jj), *((pH, pL, 2) if n else (aH, aL, KT)))
                            last.then_inc(pl, 1)
                        pe.drain().then_inc(w_done, 1)
                end_phase(pe, l, 14)

            norm_sum(NL)
            for tt in range(5):
                rows = P if tt < NT else NSAM
                pe.wait_ge(y_ready, 1)
                pe.wait_ge(y_act, nth(y_act, tt - 3))
                pe.wait_ge(y_dve, nth(y_dve, tt - 3))
                for c in range(KT):
                    last = nc.tensor.transpose(ps[0:rows, 2 * (tt % 4) + c // 4, (c % 4) * P:(c % 4 + 1) * P],
                                               xT[:, c, tt * P:tt * P + rows], ident)
                last.then_inc(y_tp, 1)

        @block.scalar
        def _(act):
            def norm_std(l):
                for c in range(KT):
                    act.wait_ge(sq_used, nth(sq_used, l * KT + (c - 1)))
                    act.activation(sq[:, c % 2, :], xT[:, c, :], ACT.Square).then_inc(sq_ready, 1)
                act.wait_ge(ss_ready, l + 1)
                act.activation(halves(rstd[:]), bank2(0), ACT.Sqrt, bias=C("eps"), scale=1.0 / D).then_inc(std_ready, 1)

            def split_h(n):
                for c in range(KT):
                    act.wait_ge(h_f, KT * n + (c + 1))
                    act.activation(hH[:, c, :], t_f[:, c % 2, :], ACT.Copy).then_inc(h_hi, 1)

            def split(n, src):
                for c in range(KT):
                    act.activation(aH[:, c, :], src[:, c, :], ACT.Copy).then_inc(sp_hi, 1)

            act.wait_ge(s_const, 16)
            act.wait_ge(s_zero, 1)
            act.activation(mask2[:, 0, :], ident, ACT.Copy)
            act.activation(mask2[:, 1, :], C("causal"), ACT.Copy)
            for c in range(KT):
                act.wait_ge(x_tp, c + 1)
                act.activation(xT[:, c, 0:SEQ], ps[:, 2 * (c % 4), :], ACT.Copy)
                act.activation(xT[:, c, SEQ:TOK], ps[:, 2 * (c % 4) + 1, 0:NSAM], ACT.Copy).then_inc(x_free, 1)
            end_phase(act, 0, -1)

            with act.Fori(0, NL) as l:
                norm_std(l)
                make_high(act, l, pb(B_CONV, 0, 0), 0)
                split_h(2 * l)
                end_phase(act, l, 0)
                with act.Fori(0, 4) as i:
                    n = 4 * l + i
                    for kind in range(4):
                        make_high(act, l, pb(B_CONV, 2 * i + (kind + 1) // 2, (kind + 1) % 2), (kind + 1) % 2)
                        for jj in range(2):
                            act.wait_ge(cv, 8 * n + (2 * kind + jj + 1))
                            bank = bank2(2 * ((2 * kind + jj) % 4))
                            if kind == 0:
                                act.wait_ge(cv_used, nth(cv_used, 2 * n + (jj - 1)))
                            if kind < 3:
                                act.activation(halves(cv_in[:, kind, jj, :]), bank, ACT.Copy).then_inc(cv_act, 1)
                            else:
                                act.activation(halves(cv_in[:, 3, jj, :]), bank, ACT.Sigmoid).then_inc(cv_sg, 1)
                        if kind == 3:
                            for jj in range(2):
                                act.wait_ge(cv_f, 2 * n + (jj + 1))
                                act.activation(one(aH, 2 * i + jj), cv_in[:, 1, jj, :], ACT.Copy).then_inc(cv_hi, 1)
                end_phase(act, l, 1)

                def gates(which, first_block):
                    with act.Fori(0, 4) as i:
                        for n in range(2):
                            make_high(act, l, pb(first_block, i + (n + 1) // 2, (n + 1) % 2), (n + 1) % 2)
                            if n == 0:
                                for jj in range(2):
                                    act.wait_ge(mg, 32 * l + 4 * i + (16 * which + jj + 1))
                                    act.wait_ge(mg_dve, nth(mg_dve, 16 * l + 2 * i + (8 * which + jj - 1)))
                                    act.activation(halves(t_f[:, jj, :]), bank2(2 * jj), ACT.Sigmoid).then_inc(mg_sg, 1)

                gates(0, B_MA)
                end_phase(act, l, 2)
                act.wait_ge(tail_tp, l + 1)
                act.activation(tail_rows[:, 0:SEQ], ps[0:18, 6, :], ACT.Copy).then_inc(tail_cp, 1)
                act.activation(tail_rows[:, SEQ:D], ps[0:18, 7, :], ACT.Copy).then_inc(tail_cp, 1)

                def copy_out(b, half, n, dst, width):
                    col = 2 * width * half + n * width
                    for tt in range(5):
                        rows = P if tt < NT else NSAM
                        act.wait_ge(tm, l * (5 * TM_BLOCKS) + 10 * half + (5 * (b + n) + tt + 1))
                        if dst is zq:
                            out = zq[0:rows, tt, ds(2 * BW * half, 2 * BW)].rearrange("p (r g d) -> p g r d", g=2, d=HD)[:, n]
                            src = ps[0:rows, tt, 0:BW].rearrange("p (r d) -> p r d", d=HD)
                        else:
                            out, src = dst[0:rows, tt, ds(col, width)], ps[0:rows, tt, 0:width]
                        act.activation(out, src, ACT.Copy).then_inc(tm_ev, 1)

                with act.Fori(0, NQB // 2) as i:
                    for n in range(2):
                        make_high(act, l, pb(B_TM, i + (n + 1) // 2, (n + 1) % 2), (n + 1) % 2, width=(BW, WW)[n])
                        copy_out(0, i, n, zq, BW)
                with act.Fori(0, NKB // 2 - 1) as i:
                    for n in range(2):
                        make_high(act, l, pb(B_TM + NQB, i + (n + 1) // 2, (n + 1) % 2), (n + 1) % 2, width=WW)
                        copy_out(NQB, i, n, zk, WW)
                make_high(act, l, pb(B_TM + NQB, NKB // 2 - 1, 1), 1, width=WW)
                for n in range(2):
                    copy_out(NQB, NKB // 2 - 1, n, zk, WW)
                act.drain()
                act.activation(zk[:, 0:NT, Z_G:Z_G + 48], zk[:, 0:NT, Z_G:Z_G + 48], ACT.Sigmoid)
                act.activation(zk[0:NSAM, NT, Z_G:Z_G + 48], zk[0:NSAM, NT, Z_G:Z_G + 48], ACT.Sigmoid)
                act.wait_ge(tail_out, 32 * l + 32)
                act.sem_inc(passed, 1)
                end_phase(act, l, 3)

                for kv in range(2):
                    act.wait_ge(w1_in, 32 * l + (16 * kv + 16))
                    act.wait_ge(c_mm, nth(c_mm, 40 * l + 20 * kv))
                    w1r = craw[:, 0].rearrange("p s t c -> p (s t c)").rearrange("p (k h) -> p k h", k=16)
                    for n in range(4):
                        act.activation(w1H[:, 4 * n:4 * n + 4, :], w1r[:, 4 * n:4 * n + 4, :], ACT.Copy).then_inc(w1_hi, 1)

                    def chunks_high(unit, rows, nseq):
                        for j in range(4):
                            act.wait_ge(c_mm, nth(c_mm, 4 * unit + (j - 1)))
                            for s in range(nseq):
                                act.wait_ge(c_tp, 8 * unit + (2 * j + s + 1))
                                for t in range(2):
                                    for g in range(2):
                                        src = ps[64 * g:64 * g + 64, (2 * j + s) % 4, 2 * t * P:2 * (t + 1) * P].rearrange("p (a h) -> p h a", a=2)[:, 0:rows, :]
                                        dst = chH[64 * t:64 * t + 64, j % 2, s, 0:rows, g:GROUPS:2]
                                        last = act.activation(dst, src, ACT.Copy)
                                last.then_inc(c_hi, 1)
                            if nseq == 1:
                                act.drain().then_inc(c_hi, 1)

                    def hidden_gate(unit, n):
                        act.wait_ge(c_acc, unit + 1)
                        for hid in range(2):
                            act.activation(hsg[:, hid, 0:n], ps[:, 4 + hid, 0:n], ACT.Sigmoid, bias=hb[:, hid:hid + 1]).then_inc(c_sg, 1)

                    chunks_high(10 * l + 5 * kv, 68, 1)
                    act.wait_ge(pos_ready, 2 * l + (kv + 1))
                    hidden_gate(10 * l + 5 * kv, NWP * GROUPS)
                    with act.Fori(0, 2) as pp:
                        for par in range(2):
                            unit = 10 * l + 2 * pp + (5 * kv + par + 1)
                            chunks_high(unit, P, 2)
                            hidden_gate(unit, 2 * NWS * GROUPS)
                end_phase(act, l, 4)
                end_phase(act, l, 5)

                for k in range(0, 14, 2):
                    act.wait_ge(tp[0], 7 * l + (k // 2 + 1))
                    if k < 8:
                        act.activation(qT[:, k, :], ps[:, k % 8, :], ACT.Copy, scale=SCALE).then_inc(tp_free[0], 1)
                    elif k < 12:
                        act.activation(kT[:, (k - 8) // 2, 0, :], ps[:, k % 8, :], ACT.Copy).then_inc(tp_free[0], 1)
                    else:
                        act.activation(qsT[:].rearrange("p k t -> p (k t)"), ps[:, 4, 0:KT * NSAM], ACT.Copy).then_inc(tp_free[0], 1)
                end_phase(act, l, 6)

                def exps(unit, k):
                    b, g, u = k % 2, k % 2, k % 8 // 2
                    n = P * (u + 1)
                    for br in range(2):
                        o = 8 + (u % 2) * 4 + g * 2 + br
                        act.activation(pr[:, b, br, 0:n], ps[:, 2 * b + br, 0:n], ACT.Exp, bias=small[:, 2 * b + br:2 * b + br + 1],
                                       accum_out=small[:, o:o + 1]).then_inc(pa_exp, 1)

                act.wait_ge(pa_csub, l + 1)
                act.activation(cs[:], cs[:], ACT.Exp).then_inc(pa_cexp, 1)
                act.wait_ge(pa_nm, 66 * l + 1)
                exps(64 * l, 0)
                act.wait_ge(pa_ct, l + 1)
                act.activation(cT[:, 0].rearrange("p h q -> p (h q)"), ps[:, 4:6, :].rearrange("p a b -> p (a b)"), ACT.Copy).then_inc(pa_ctev[0], 1)
                with act.Fori(0, REP) as r:
                    for gp in range(2):
                        unit = 64 * l + 16 * r + 8 * gp
                        for k in range(8):
                            u = k // 2
                            act.wait_ge(pa_nm, 66 * l + 16 * r + (8 * gp + k + 2))
                            act.wait_ge(pa_t, nth(pa_t, 2 * unit + 2 * k))
                            if k % 2 == 1:
                                act.wait_ge(pa_o, nth(pa_o, 32 * l + 8 * r + (4 * gp + u)))
                            exps(unit, k + 1)
                            for br in range(2):
                                act.wait_ge(pa_t, nth(pa_t, 2 * unit + (2 * k + br + 1)))
                                act.wait_ge(pa_pv, nth(pa_pv, unit + (k - 1)))
                                act.activation(prT[:, k % 2, br, 0:P * (u + 1)], ps[:, 4 + br, 0:P * (u + 1)], ACT.Copy).then_inc(pa_te, 1)
                            if k % 2 == 0:
                                v = (k - 4) // 2
                                act.wait_ge(pa_yt, nth(pa_yt, 34 * l + 8 * r + (4 * gp + v + 3)))
                                flat = yT[:].rearrange("p k t -> p (k t)")
                                if v >= 0:
                                    out = flat[:, ds(TOK * r + (4 * gp * TOK + v * P), P)]
                                elif gp == 1:
                                    out = flat[:, ds(TOK * r + (v + 4) * P, P)]
                                else:
                                    out = flat[:, ds(TOK * r + (3 * TOK + (v + 4) * P), P)]
                                act.activation(out, ps[:, 6 + v % 2, 384:512], ACT.Copy).then_inc(pa_yo, 1)
                for n in range(2):
                    act.wait_ge(pa_yt, nth(pa_yt, 34 * l + (33 + n)))
                    act.activation(yT[:, KT - 1, (2 + n) * P:(3 + n) * P], ps[:, 6 + n, 384:512], ACT.Copy).then_inc(pa_yo, 1)
                end_phase(act, l, 7)

                with act.Fori(0, 2) as pp:
                    for par in range(2):
                        it = 4 * l + 2 * pp + par
                        act.wait_ge(sa_nm, it + 1)
                        act.activation(pc[:, 0:NWS], ps[:, 3, 0:NWS], ACT.Exp, bias=small[:, 64:65], scale=SCALE,
                                       accum_out=small[:, 65:66])
                        act.drain().then_inc(sa_cx, 1)
                        for k in range(12):
                            act.wait_ge(sa_kt, 12 * it + (k + 1))
                            act.wait_ge(sa_s, nth(sa_s, 12 * it + (k - 1)))
                            act.activation(skT[:, k % 2, :], ps[:, 4 + k % 2, :], ACT.Copy).then_inc(sa_ke, 1)
                        act.wait_ge(sa_m, 2 * it + 1)
                        act.activation(ssel[:], ssel[:], ACT.Exp, bias=small[:, 68:69], scale=SCALE, accum_out=small[:, 70:71])
                        act.drain().then_inc(sa_e, 1)
                        for n, (bank, rows, c0, c1, slot) in enumerate(((4, NWS, 0, P, 13), (5, P, 0, 4 * P, 0), (4, P, 0, 4 * P, 4),
                                                                        (5, P, 0, 4 * P, 8), (4, NSAM, 0, P, 14))):
                            if n == 3:
                                act.wait_ge(sa_m, 2 * it + 2)
                                act.activation(swsc[:], swsc[:], ACT.Exp, bias=small[:, 69:70], scale=SCALE, accum_out=small[:, 71:72])
                                act.drain().then_inc(sa_e, 1)
                            act.wait_ge(sa_t, 5 * it + (n + 1))
                            if n == 0:
                                act.activation(spT[0:NSAM, 12, :], ps[0:NSAM, 4, P:2 * P], ACT.Copy)
                            act.activation(spT[0:rows, slot:slot + (c1 - c0) // P, :].rearrange("p a b -> p (a b)"),
                                           ps[0:rows, bank, c0:c1], ACT.Copy).then_inc(sa_te, 1)
                act.wait_ge(s_winout, 256 * l + 256)
                act.sem_inc(passed, 1)
                end_phase(act, l, 8)

                make_high(act, l, pb(B_ZB, 0, 0), 0)
                split_h(2 * l + 1)
                end_phase(act, l, 9)
                with act.Fori(0, 2) as i:
                    for n in range(2):
                        make_high(act, l, pb(B_ZB, i + (n + 1) // 2, (n + 1) % 2), (n + 1) % 2)
                        for jj in range(2):
                            q = 8 * l + 4 * i + (2 * n + jj)
                            act.wait_ge(zb, q + 1)
                            act.wait_ge(zb_done, nth(zb_done, q - 1))
                            act.activation(halves(t_f[:, jj, :]), bank2(2 * (2 * n + jj)), ACT.Sigmoid).then_inc(zb_sg, 1)
                        for jj in range(2):
                            q = 8 * l + 4 * i + (2 * n + jj)
                            act.wait_ge(zb_f, q + 1)
                            act.activation(one(aH, 4 * i + (2 * n + jj)), t_f[:, jj, :], ACT.Copy).then_inc(zb_hi, 1)
                end_phase(act, l, 10)
                gates(1, B_MB)
                end_phase(act, l, 11)
                split(2 * l, m)
                end_phase(act, l, 12)
                with act.Fori(0, 2) as i:
                    for n in range(2):
                        make_high(act, l, pb(B_WO, i + (n + 1) // 2, (n + 1) % 2), (n + 1) % 2)
                act.wait_ge(wo_done, nth(wo_done, 8 * l + 8))
                act.wait_ge(p_tp, l + 1)
                for c in range(2):
                    act.activation(pH[:, c, 0:SEQ], ps[:, 2 * c, :], ACT.Copy)
                    act.activation(pH[:, c, SEQ:TOK], ps[:, 2 * c + 1, 0:NSAM], ACT.Copy).then_inc(p_hi, 1)
                split(2 * l + 1, xT)
                end_phase(act, l, 13)

                def ple(i, prep):
                    for n in range(2):
                        if prep or n == 0:
                            make_high(act, l, pb(B_PL, i + (n + 1) // 2, (n + 1) % 2), (n + 1) % 2, nk=(2, KT)[n])
                        if n == 0:
                            for jj in range(2):
                                act.wait_ge(pl, 16 * l + 4 * i + (jj + 1))
                                act.wait_ge(pl_done, nth(pl_done, 8 * l + 2 * i + (jj - 1)))
                                act.activation(halves(t_f[:, jj, :]), bank2(2 * jj), ACT.Sigmoid).then_inc(pl_sg, 1)

                with act.Fori(0, 3) as i:
                    ple(i, True)
                ple(3, False)
                end_phase(act, l, 14)

            norm_std(NL)
            for tt in range(5):
                rows = P if tt < NT else NSAM
                act.wait_ge(y_tp, tt + 1)
                act.activation(out_rows[0:rows, tt, 0:SEQ], ps[0:rows, 2 * (tt % 4), :], ACT.Copy).then_inc(y_act, 1)

        @block.vector
        def _(dve):
            def norm_recip(l):
                dve.wait_ge(std_ready, l + 1)
                dve.reciprocal(rstd[:], rstd[:])
                dve.drain()

            def make_h(n):
                def low(c):
                    dve.wait_ge(h_hi, KT * n + (c + 1))
                    dve.tensor_tensor(hL[:, c, :], t_f[:, c % 2, :], hH[:, c, :].bitcast(F32), ALU.subtract)

                for c in range(KT):
                    if c >= 2:
                        low(c - 2)
                        dve.drain()
                    dve.scalar_tensor_tensor(out=t_f[:, c % 2, :], in0=xT[:, c, :], scalar=cols[:, c, 19:20], in1=rstd[:],
                                             op0=ALU.mult, op1=ALU.mult).then_inc(h_f, 1)
                low(KT - 2)
                low(KT - 1)

            def split(n, src):
                for c in range(KT):
                    dve.wait_ge(sp_hi, KT * n + (c + 1))
                    dve.tensor_tensor(aL[:, c, :], src[:, c, :], aH[:, c, :].bitcast(F32), ALU.subtract)

            end_phase(dve, 0, -1)
            with dve.Fori(0, NL) as l:
                dve.wait_ge(st_tp, l + 1)
                dve.tensor_copy(cols[:].rearrange("p k n -> p (k n)"), ps[:, 2, 0:21 * KT])
                norm_recip(l)
                make_low(dve, l, pb(B_CONV, 0, 0), 0)
                make_h(2 * l)
                dve.drain()
                dve.memset(cv_u[:, :, 0:2], 0.0)
                dve.drain()
                end_phase(dve, l, 0)
                with dve.Fori(0, 4) as i:
                    n = 4 * l + i
                    for kind in range(4):
                        make_low(dve, l, pb(B_CONV, 2 * i + (kind + 1) // 2, (kind + 1) % 2), (kind + 1) % 2)
                        if kind == 0:
                            for jj in range(2):
                                dve.tensor_copy(cst[:, jj, :], cols[:].rearrange("p k n -> p (k n)")[:, ds(42 * i + 21 * jj, 21)])
                            dve.drain()
                        for jj in range(2):
                            if kind == 1:
                                dve.wait_ge(cv_act, nth(cv_act, 6 * n + (3 + jj)))
                                u = cv_u[:, jj, :]
                                us = u[:, SEQ + 2:UW].rearrange("p (b t) -> p b t", t=6)
                                ca, xa = cv_in[:, 0, jj, :], cv_in[:, 1, jj, :]
                                dve.tensor_tensor(u[:, 2:SEQ + 2], ca[:, 0:SEQ], xa[:, 0:SEQ], ALU.mult)
                                dve.tensor_tensor(us[:, :, 2:6], ca[:, SEQ:TOK].rearrange("p (b t) -> p b t", t=TS),
                                                  xa[:, SEQ:TOK].rearrange("p (b t) -> p b t", t=TS), ALU.mult)
                                dve.tensor_copy(us[:, :, 0:2], cst[:, jj, 0:16].rearrange("p (b t) -> p b t", t=2))
                                dve.drain()
                                tl = tails[:].rearrange("p k n -> p (k n)")
                                dve.tensor_copy(tl[:, ds(36 * i + 18 * jj, 2)], u[:, SEQ:SEQ + 2])
                                dve.tensor_copy(tl[:, ds(36 * i + (18 * jj + 2), 16)].rearrange("p (b t) -> p b t", t=2), us[:, :, 4:6])
                            elif kind == 2:
                                dve.wait_ge(cv_act, nth(cv_act, 6 * n + (5 + jj)))
                                w = UW - 2
                                dve.tensor_scalar(cv_y[:, 0:w], cv_u[:, jj, 0:w], cst[:, jj, 16:17], None, ALU.mult)
                                for tap in (1, 2):
                                    dve.drain()
                                    dve.scalar_tensor_tensor(out=cv_y[:, 0:w], in0=cv_u[:, jj, tap:tap + w], scalar=cst[:, jj, 16 + tap:17 + tap],
                                                             in1=cv_y[:, 0:w], op0=ALU.mult, op1=ALU.add)
                                dve.drain()
                                ba = cv_in[:, 2, jj, :]
                                ys = cv_y[:, SEQ + 2:UW].rearrange("p (b t) -> p b t", t=6)[:, :, 0:TS]
                                bs = ba[:, SEQ:TOK].rearrange("p (b t) -> p b t", t=TS)
                                dve.tensor_tensor(ba[:, 0:SEQ], ba[:, 0:SEQ], cv_y[:, 0:SEQ], ALU.mult)
                                dve.tensor_tensor(bs, bs, ys, ALU.mult)
                                dve.drain()
                            elif kind == 3:
                                dve.wait_ge(cv_sg, 2 * n + (jj + 1))
                                dve.tensor_tensor(halves(cv_in[:, 0, jj, :]), bank2(4 + 2 * jj), halves(cv_in[:, 3, jj, :]), ALU.mult).then_inc(cv_dve, 1)
                                dve.drain()
                                dve.tensor_tensor(cv_in[:, 1, jj, :], cv_in[:, 0, jj, :], cv_in[:, 2, jj, :], ALU.mult).then_inc(cv_f, 1)
                        if kind == 3:
                            dve.drain()
                            for jj in range(2):
                                dve.wait_ge(cv_hi, 2 * n + (jj + 1))
                                dve.tensor_tensor(one(aL, 2 * i + jj), cv_in[:, 1, jj, :], one(aH, 2 * i + jj).bitcast(F32), ALU.subtract
                                                  ).then_inc(cv_used, 1)
                end_phase(dve, l, 1)

                def products(which, first_block):
                    with dve.Fori(0, 4) as i:
                        for n in range(2):
                            make_low(dve, l, pb(first_block, i + (n + 1) // 2, (n + 1) % 2), (n + 1) % 2)
                            if n == 1:
                                for jj in range(2):
                                    dve.wait_ge(mg_sg, 16 * l + 2 * i + (8 * which + jj + 1))
                                    dve.wait_ge(mg, 32 * l + 4 * i + (16 * which + 2 + jj + 1))
                                    if which == 0:
                                        dve.tensor_tensor(two(m, 2 * i + jj), bank2(4 + 2 * jj), halves(t_f[:, jj, :]), ALU.mult).then_inc(mg_dve, 1)
                                    else:
                                        dve.tensor_tensor(halves(t_f[:, jj, :]), bank2(4 + 2 * jj), halves(t_f[:, jj, :]), ALU.mult)
                                        dve.drain()
                                        dve.tensor_tensor(one(m, 2 * i + jj), one(m, 2 * i + jj), t_f[:, jj, :], ALU.add).then_inc(mg_dve, 1)

                products(0, B_MA)
                end_phase(dve, l, 2)

                def rope(z, rows, tts, c0, heads):
                    nt = tts[1] - tts[0]
                    v = z[0:rows, tts[0]:tts[1], ds(c0, heads * HD)].rearrange("p t (h c) -> p t h c", c=HD)
                    x1, x2 = v[:, :, :, 0:32], v[:, :, :, 32:64]
                    tab = [C(n, rows).rearrange("p (t c) -> p t c", c=32)[:, tts[0]:tts[1], :].unsqueeze(2).to_broadcast([rows, nt, heads, 32])
                           for n in ("cos", "sin")]
                    ta, tb = (rope_a[0:rows, k, 0:nt * heads * 32].rearrange("p (t h c) -> p t h c", t=nt, h=heads) for k in range(2))
                    dve.tensor_tensor(ta, x2, tab[1], ALU.mult)
                    dve.tensor_tensor(tb, x1, tab[1], ALU.mult)
                    dve.drain()
                    dve.tensor_tensor(x1, x1, tab[0], ALU.mult)
                    dve.tensor_tensor(x2, x2, tab[0], ALU.mult)
                    dve.drain()
                    dve.tensor_tensor(x1, x1, ta, ALU.subtract)
                    dve.tensor_tensor(x2, x2, tb, ALU.add)
                    dve.drain()

                def rope_all(z, c0, heads, blocks):
                    dve.wait_ge(tm_ev, nth(tm_ev, l * (5 * TM_BLOCKS) + 5 * blocks))
                    for tt in range(NT):
                        rope(z, P, (tt, tt + 1), c0, heads)
                    rope(z, NSAM, (NT, NT + 1), c0, heads)

                with dve.Fori(0, NQB // 2) as i:
                    for n in range(2):
                        make_low(dve, l, pb(B_TM, i + (n + 1) // 2, (n + 1) % 2), (n + 1) % 2, width=(BW, WW)[n])
                    rope_all(zq, 512 * i, 8, 2 * i + 2)
                with dve.Fori(0, NKB // 2 - 1) as i:
                    for n in range(2):
                        make_low(dve, l, pb(B_TM + NQB, i + (n + 1) // 2, (n + 1) % 2), (n + 1) % 2, width=WW)
                    rope_all(zk, 512 * i, 4, 2 * i + (NQB + 2))
                make_low(dve, l, pb(B_TM + NQB, NKB // 2 - 1, 1), 1, width=WW)
                rope_all(zk, Z_KW, 4, TM_BLOCKS)
                dve.drain().then_inc(z_ready, 1)
                end_phase(dve, l, 3)

                for kv in range(2):
                    w1r = craw[:, 0].rearrange("p s t c -> p (s t c)").rearrange("p (k h) -> p k h", k=16)
                    for n in range(4):
                        dve.wait_ge(w1_hi, 8 * l + (4 * kv + n + 1))
                        dve.tensor_tensor(w1L[:, 4 * n:4 * n + 4, :], w1r[:, 4 * n:4 * n + 4, :], w1H[:, 4 * n:4 * n + 4, :].bitcast(F32),
                                          ALU.subtract).then_inc(w1_lo, 1)

                    def chunks_low(unit, rows, nseq):
                        for j in range(4):
                            for s in range(nseq):
                                dve.wait_ge(c_hi, 8 * unit + (2 * j + s + 1))
                                for t in range(2):
                                    for g in range(2):
                                        src = ps[64 * g:64 * g + 64, (2 * j + s) % 4, 2 * t * P:2 * (t + 1) * P].rearrange("p (a h) -> p h a", a=2)[:, 0:rows, :]
                                        to = (slice(64 * t, 64 * t + 64), j % 2, s, slice(0, rows), slice(g, GROUPS, 2))
                                        last = dve.tensor_tensor(chL[to], src, chH[to].bitcast(F32), ALU.subtract)
                                last.then_inc(c_lo, 1)
                            if nseq == 1:
                                dve.drain().then_inc(c_lo, 1)

                    def hidden(unit, n):
                        dve.wait_ge(c_w2, nth(c_w2, unit))
                        for hid in range(2):
                            dve.wait_ge(c_sg, 2 * unit + (hid + 1))
                            dve.scalar_tensor_tensor(out=hidT[:, hid, 0:n], in0=ps[:, 4 + hid, 0:n], scalar=hb[:, hid:hid + 1],
                                                     in1=hsg[:, hid, 0:n], op0=ALU.add, op1=ALU.mult).then_inc(c_hid, 1)

                    unit = 10 * l + 5 * kv
                    chunks_low(unit, 68, 1)
                    dve.wait_ge(c_acc, unit + 1)
                    for hid in range(2):
                        dve.tensor_copy(hb[:, hid:hid + 1], ps[:, 4 + hid, (NWP + 1) * GROUPS:(NWP + 1) * GROUPS + 1])
                    dve.drain().then_inc(pos_ready, 1)
                    hidden(unit, NWP * GROUPS)
                    dve.wait_ge(c_w2, nth(c_w2, unit + 1))
                    if kv == 0:
                        src = ps[0:HD, 6, 0:NWP * GROUPS].rearrange("p (n a g) -> p g a n", a=2, g=2)
                        for g in range(2):
                            dve.tensor_copy(kcT_p[64 * g:64 * g + 64, :, 0:NWP], src[:, g])
                    else:
                        for q in range(4):
                            dve.tensor_copy(vc_p[32 * q:32 * q + NWP, :], ps[0:NWP, 6, 0:KV])
                    dve.drain().then_inc(c_out, 1)
                    with dve.Fori(0, 2) as pp:
                        for par in range(2):
                            unit = 10 * l + 2 * pp + (5 * kv + par + 1)
                            chunks_low(unit, P, 2)
                            hidden(unit, 2 * NWS * GROUPS)
                            dve.wait_ge(c_w2, nth(c_w2, unit + 1))
                            if kv == 0:
                                for s in range(2):
                                    src = ps[0:HD, 6, s * NWS * GROUPS:(s + 1) * NWS * GROUPS].rearrange("p (n a g) -> p g a n", a=2, g=2)
                                    for g in range(2):
                                        dst = kcT_s[64 * g:64 * g + 64].rearrange("p a s n -> p a (s n)")
                                        dve.tensor_copy(dst[:, :, ds(256 * pp + 64 * (2 * par + s), NWS)], src[:, g])
                            else:
                                dve.tensor_copy(vc_s[0:NWS, ds(1024 * pp + 512 * par, 512)], ps[0:NWS, 6, :])
                            dve.drain().then_inc(c_out, 1)
                end_phase(dve, l, 4)
                end_phase(dve, l, 5)

                for k in range(1, 14, 2):
                    dve.wait_ge(tp[1], 7 * l + (k // 2 + 1))
                    if k < 8:
                        dve.tensor_scalar(qT[:, k, :], ps[:, k % 8, :], SCALE, None, ALU.mult).then_inc(tp_free[1], 1)
                    elif k < 12:
                        dve.tensor_copy(kT[:, (k - 8) // 2, 1, :], ps[:, k % 8, :]).then_inc(tp_free[1], 1)
                    else:
                        dve.tensor_copy(knT[:].rearrange("p k t -> p (k t)"), ps[:, 5, 0:4 * NSAM]).then_inc(tp_free[1], 1)
                end_phase(dve, l, 6)

                def maxima(unit, k):
                    b, n = k % 2, P * (k % 8 // 2 + 1)
                    dve.wait_ge(pa_s, unit + (k + 1))
                    dve.tensor_reduce(out=small[:, 2 * b:2 * b + 2], in_=ps[:, 2 * b:2 * b + 2, 0:n], op=ALU.max, axis=AX.X, negate=True
                                      ).then_inc(pa_nm, 1)

                dve.memset(yy[:], 0.0)
                dve.wait_ge(pa_c, l + 1)
                dve.tensor_tensor(cs[:].rearrange("p (a b) n -> p a (b n)", b=NT), ps[:, 4:8, :].rearrange("p a (b n) -> p (a b) n", n=P),
                                  C("cmask").unsqueeze(1).to_broadcast([P, 2 * KT, P]), ALU.add)
                dve.drain()
                dve.tensor_reduce(out=cmx[:], in_=cs[:], op=ALU.max, axis=AX.X)
                dve.drain()
                dve.tensor_scalar(cmx[:], cmx[:], LOWEST, None, ALU.max)
                dve.drain()
                dve.tensor_tensor(cs[:], cs[:], cmx[:].unsqueeze(2).to_broadcast([P, 2 * KT * NT, 32]), ALU.subtract).then_inc(pa_csub, 1)
                maxima(66 * l, 0)
                maxima(66 * l, 1)
                dve.wait_ge(pa_cexp, l + 1)
                dve.tensor_reduce(out=cmx[:], in_=cs[:], op=ALU.add, axis=AX.X)
                dve.drain()
                dve.tensor_scalar(cmx[:], cmx[:], 1e-30, None, ALU.max)
                dve.drain()
                dve.reciprocal(cmx[:], cmx[:])
                dve.drain()
                dve.tensor_tensor(cs[:], cs[:], cmx[:].unsqueeze(2).to_broadcast([P, 2 * KT * NT, 32]), ALU.mult).then_inc(pa_cn, 1)
                dve.wait_ge(pa_ct, l + 1)
                dve.tensor_copy(cT[:, 1].rearrange("p h q -> p (h q)"), ps[:, 6:8, :].rearrange("p a b -> p (a b)")).then_inc(pa_ctev[1], 1)
                def combine(gp, r, u):
                    dve.wait_ge(pa_pv, nth(pa_pv, 64 * l + 16 * r + (8 * gp + 2 * u + 2)))
                    sums = small[:, 8 + 4 * (u % 2):12 + 4 * (u % 2)]
                    wts = small[:, 48:54].rearrange("p (g b) -> p g b", g=2)
                    inv = small[:, 24:30].rearrange("p (g b) -> p g b", g=2)
                    dve.tensor_scalar(sums, sums, 1e-30, None, ALU.max)
                    dve.drain()
                    dve.reciprocal(inv[:, :, 1:3], sums.rearrange("p (g b) -> p g b", g=2))
                    dve.drain()
                    gt = zk[:, u, Z_G + 24 * gp:Z_G + 24 * gp + 24].rearrange("p (g c) -> p g c", g=2)[:, :, ds(3 * r, 3)]
                    dve.tensor_tensor(wts, gt, inv, ALU.mult)
                    dve.drain()
                    dve.tensor_tensor(ow[:], ps[:, 6 + u % 2, 0:6 * HD].rearrange("p (k d) -> p k d", d=HD),
                                      small[:, 48:54].unsqueeze(2).to_broadcast([P, 6, HD]), ALU.mult).then_inc(pa_o, 1)
                    dve.drain()
                    dve.wait_ge(pa_yt, nth(pa_yt, 34 * l + 8 * r + (4 * gp + u + 1)))
                    dve.tensor_reduce(out=yy[:, u % 2, :].rearrange("p (g d) -> p g d", g=2),
                                      in_=ow[:].rearrange("p (g b) d -> p g d b", g=2), op=ALU.add, axis=AX.X).then_inc(pa_y, 1)

                with dve.Fori(0, REP) as r:
                    for gp in range(2):
                        for k in range(8):
                            maxima(66 * l + 16 * r + 8 * gp, k + 2)
                            if k in (2, 4, 6):
                                combine(gp, r, k // 2 - 1)
                        combine(gp, r, NT - 1)
                end_phase(dve, l, 7)

                dve.memset(pc[:, 63:64], 0.0)
                dve.wait_ge(sa_g, l + 1)
                g3 = ssel[:, 0:192].rearrange("p (a c) -> p a c", a=4)
                dve.tensor_tensor(g3, ps[:, 7, 0:192].rearrange("p (a c) -> p a c", a=4), C("gmask").unsqueeze(1).to_broadcast([P, 4, 48]), ALU.mult)
                dve.drain()
                dve.tensor_reduce(out=grow[:], in_=ssel[:, 0:192].rearrange("p (a k b) -> p a b k", a=4, b=3), op=ALU.add, axis=AX.X)
                dve.drain().then_inc(sa_gr, 1)
                with dve.Fori(0, 2) as pp:
                    for par in range(2):
                        it = 4 * l + 2 * pp + par
                        dve.wait_ge(s_fin, nth(s_fin, it))
                        for g in range(2):
                            rows = slice(64 * g, 64 * g + 64)
                            for gp in range(2):
                                for s in range(2):
                                    c0 = 64 * s + 16 * (2 * gp + g)
                                    src = qsT[rows, 4 * gp:4 * gp + 4, ds(8 * pp * 2 + (2 * par + s) * TS, TS)].rearrange("p r t -> p t r")
                                    dve.tensor_copy(qs[rows, gp, s, c0:c0 + 16].rearrange("p (t r) -> p t r", t=TS), src)
                        dve.tensor_copy(vcst[0:NWS, :], vc_s[0:NWS, ds(1024 * pp + 512 * par, 512)])
                        dve.drain().then_inc(sa_q, 1)
                        dve.wait_ge(sa_c, it + 1)
                        dve.tensor_reduce(out=small[:, 64:65], in_=ps[:, 3, 0:NWS], op=ALU.max, axis=AX.X, negate=True)
                        nm = C("nmask")[:, ds(2 * NSAM * pp + NSAM * par, NSAM)]
                        dve.tensor_tensor(ssel[:, PAST:PAST + NSAM], ps[:, 3, 64:64 + NSAM], nm, ALU.add)
                        dve.tensor_tensor(swsc[:, WIN:WIN + NSAM], ps[:, 3, 64 + NSAM:64 + 2 * NSAM], nm, ALU.add)
                        dve.drain()
                        dve.tensor_scalar(small[:, 64:65], small[:, 64:65], -LOWEST, SCALE, ALU.min, ALU.mult).then_inc(sa_nm, 1)
                        dve.wait_ge(sa_cx, it + 1)
                        dve.tensor_scalar(small[:, 65:66], small[:, 65:66], 1e-30, None, ALU.max)
                        dve.drain()
                        dve.reciprocal(small[:, 65:66], small[:, 65:66])
                        dve.drain()
                        dve.tensor_scalar(pc[:, 0:NWS], pc[:, 0:NWS], small[:, 65:66], None, ALU.mult)
                        dve.drain()
                        dve.tensor_reduce(out=small[:, 32:46], in_=pc[:, 4:60].rearrange("p (j k) -> p j k", k=4), op=ALU.add, axis=AX.X)
                        dve.drain()
                        dve.tensor_tensor(small[:, 32:46], small[:, 32:46], pc[:, 3:56:4], ALU.add).then_inc(sa_im, 1)
                        dve.wait_ge(sa_imp, it + 1)
                        imp = ps[:, 3, 256:270]
                        dve.tensor_reduce(out=small[:, 66:67], in_=imp, op=ALU.min, axis=AX.X)
                        dve.drain()
                        dve.scalar_tensor_tensor(out=small[:, 80:94], in0=imp, scalar=small[:, 66:67], in1=C("iota")[:, 1:15],
                                                 op0=ALU.is_equal, op1=ALU.mult)
                        dve.drain()
                        dve.tensor_reduce(out=small[:, 67:68], in_=small[:, 80:94], op=ALU.max, axis=AX.X)
                        dve.drain()
                        dve.tensor_scalar(small[:, 96:112], C("iota"), small[:, 67:68], NEG, ALU.is_equal, ALU.mult)
                        dve.drain()
                        dve.wait_ge(sa_s, nth(sa_s, 12 * it + 8))
                        drop = small[:, 96:112].unsqueeze(1).unsqueeze(3).to_broadcast([P, 8, 16, 8])
                        dve.tensor_tensor(ssel[:, 0:PAST].rearrange("p (t j c) -> p t j c", t=8, j=16),
                                          ps[:, 0:2, :].rearrange("p a (t j c) -> p (a t) j c", t=4, j=16), drop, ALU.add)
                        dve.drain()
                        dve.tensor_reduce(out=small[:, 68:69], in_=ssel[:], op=ALU.max, axis=AX.X, negate=True)
                        dve.drain()
                        dve.tensor_scalar(small[:, 68:69], small[:, 68:69], SCALE, None, ALU.mult).then_inc(sa_m, 1)
                        dve.wait_ge(sa_s, nth(sa_s, 12 * it + 12))
                        dve.tensor_tensor(swsc[:, 0:WIN], ps[:, 2, :], C("wmask"), ALU.add)
                        dve.drain()
                        dve.tensor_reduce(out=small[:, 69:70], in_=swsc[:], op=ALU.max, axis=AX.X, negate=True)
                        dve.drain()
                        dve.tensor_scalar(small[:, 69:70], small[:, 69:70], SCALE, None, ALU.mult).then_inc(sa_m, 1)
                        dve.wait_ge(sa_o, it + 1)
                        dve.tensor_scalar(small[:, 70:72], small[:, 70:72], 1e-30, None, ALU.max)
                        dve.drain()
                        dve.reciprocal(small[:, 77:79], small[:, 70:72])
                        dve.drain()
                        dve.tensor_tensor(small[:, 72:75], grow[:].rearrange("p a b -> p (a b)")[:, ds(6 * pp + 3 * par, 3)], small[:, 76:79], ALU.mult)
                        dve.drain()
                        dve.tensor_scalar(sy[:], ps[:, 6, 0:KV], small[:, 72:73], None, ALU.mult)
                        dve.drain()
                        dve.scalar_tensor_tensor(out=sy[:], in0=ps[:, 6, KV:2 * KV], scalar=small[:, 73:74], in1=sy[:], op0=ALU.mult, op1=ALU.add)
                        dve.drain()
                        dve.scalar_tensor_tensor(out=sy[:], in0=ps[:, 7, 0:KV], scalar=small[:, 74:75], in1=sy[:], op0=ALU.mult, op1=ALU.add
                                                 ).then_inc(sa_y, 1)
                        dve.wait_ge(sa_yt, it + 1)
                        for gp in range(2):
                            for g in range(2):
                                rows = slice(64 * g, 64 * g + 64)
                                src = ps[rows, 5, gp * P:(gp + 1) * P].rearrange("p (s g t r) -> p g r s t", s=2, g=4, t=TS)[:, 2 * gp + g]
                                dst = yT[rows, 4 * gp:4 * gp + 4, ds(16 * pp + (8 * par + SEQ), 8)].rearrange("p r (s t) -> p r s t", s=2)
                                last = dve.tensor_copy(dst, src)
                        dve.drain().then_inc(sa_ys, 1)
                dve.wait_ge(s_winout, 256 * l + 256)
                dve.sem_inc(passed, 1)
                end_phase(dve, l, 8)

                make_low(dve, l, pb(B_ZB, 0, 0), 0)
                make_h(2 * l + 1)
                end_phase(dve, l, 9)
                with dve.Fori(0, 2) as i:
                    for n in range(2):
                        make_low(dve, l, pb(B_ZB, i + (n + 1) // 2, (n + 1) % 2), (n + 1) % 2)
                        for jj in range(2):
                            q = 8 * l + 4 * i + (2 * n + jj)
                            dve.wait_ge(zb_sg, q + 1)
                            dve.tensor_tensor(halves(t_f[:, jj, :]), bank2(2 * (2 * n + jj)), halves(t_f[:, jj, :]), ALU.mult)
                            dve.drain()
                            dve.tensor_tensor(t_f[:, jj, :], t_f[:, jj, :], one(yT, 4 * i + (2 * n + jj)), ALU.mult).then_inc(zb_f, 1)
                        dve.drain()
                        for jj in range(2):
                            q = 8 * l + 4 * i + (2 * n + jj)
                            dve.wait_ge(zb_hi, q + 1)
                            c = 4 * i + (2 * n + jj)
                            dve.tensor_tensor(one(aL, c), t_f[:, jj, :], one(aH, c).bitcast(F32), ALU.subtract).then_inc(zb_done, 1)
                end_phase(dve, l, 10)
                products(1, B_MB)
                end_phase(dve, l, 11)
                split(2 * l, m)
                end_phase(dve, l, 12)
                with dve.Fori(0, 2) as i:
                    for n in range(2):
                        make_low(dve, l, pb(B_WO, i + (n + 1) // 2, (n + 1) % 2), (n + 1) % 2)
                        for jj in range(2):
                            c = 4 * i + (2 * n + jj)
                            dve.wait_ge(wo, 8 * l + c + 1)
                            dve.tensor_tensor(two(xT, c), two(xT, c), bank2(2 * (2 * n + jj)), ALU.add).then_inc(wo_done, 1)
                dve.drain()
                for c in range(2):
                    dve.wait_ge(p_hi, 2 * l + (c + 1))
                    dve.tensor_tensor(pL[:, c, 0:SEQ], ps[:, 2 * c, :], pH[:, c, 0:SEQ].bitcast(F32), ALU.subtract)
                    dve.tensor_tensor(pL[:, c, SEQ:TOK], ps[:, 2 * c + 1, 0:NSAM], pH[:, c, SEQ:TOK].bitcast(F32), ALU.subtract)
                split(2 * l + 1, xT)
                end_phase(dve, l, 13)

                def ple(i, prep):
                    for n in range(2):
                        if prep or n == 0:
                            make_low(dve, l, pb(B_PL, i + (n + 1) // 2, (n + 1) % 2), (n + 1) % 2, nk=(2, KT)[n])
                    for jj in range(2):
                        dve.wait_ge(pl_sg, 8 * l + 2 * i + (jj + 1))
                        dve.wait_ge(pl, 16 * l + 4 * i + (2 + jj + 1))
                        dve.tensor_tensor(halves(t_f[:, jj, :]), bank2(4 + 2 * jj), halves(t_f[:, jj, :]), ALU.mult)
                        dve.drain()
                        dve.tensor_tensor(one(xT, 2 * i + jj), one(xT, 2 * i + jj), t_f[:, jj, :], ALU.add).then_inc(pl_done, 1)

                with dve.Fori(0, 3) as i:
                    ple(i, True)
                ple(3, False)
                end_phase(dve, l, 14)

            norm_recip(NL)
            for c in range(KT):
                last = dve.scalar_tensor_tensor(out=xT[:, c, :], in0=xT[:, c, :], scalar=cols[:, c, 20:21], in1=rstd[:], op0=ALU.mult, op1=ALU.mult)
            dve.drain().then_inc(y_ready, 1)
            for tt in range(5):
                rows = P if tt < NT else NSAM
                dve.wait_ge(y_tp, tt + 1)
                dve.tensor_copy(out_rows[0:rows, tt, SEQ:D], ps[0:rows, 2 * (tt % 4) + 1, :]).then_inc(y_dve, 1)


INPUTS = ["x_prompt", "x_sample", "cache_kv", "state_win", "state_conv", "page_table", "p_prompt", "p_sample",
          "ln_g", "w_in", "conv_w", "cmp_pos_k", "cmp_w1_k", "cmp_w2_k", "cmp_pos_v", "cmp_w1_v", "cmp_w2_v",
          "w_out_a", "w_out_b", "w_o", "w_ple", "w_ple_gate", "final_g"]
OUTPUTS = [("y_prompt", (1, SEQ, D)), ("y_sample", (NSEQ, TS, D)),
           ("new_kv_prompt", (NL, 1, SEQ, 4, GROUPS, HD)), ("new_kv_sample", (NL, NSEQ, TS, 4, GROUPS, HD)),
           ("new_win_prompt", (NL, 1, WIN, 2, GROUPS, HD)), ("new_win_sample", (NL, NSEQ, WIN, 2, GROUPS, HD)),
           ("new_conv_prompt", (NL, 1, 2, D)), ("new_conv_sample", (NL, NSEQ, 2, D))]


def kernel(**inputs):
    import concourse.bacc as bacc
    from concourse.bass_utils import run_bass_kernel_spmd

    nc = bacc.Bacc("TRN2", target_bir_lowering=False, num_devices=1)
    arrays, aps = {}, {}
    data = {name: np.ascontiguousarray(inputs[name]) for name in INPUTS}
    data["consts"] = constants()
    for name, x in data.items():
        arrays["in_" + name] = x
        aps[name] = nc.dram_tensor("in_" + name, x.shape, mybir.dt.from_np(x.dtype), kind="ExternalInput").ap()
    for name, shape in OUTPUTS:
        aps[name] = nc.dram_tensor("out_" + name, shape, F32, kind="ExternalOutput").ap()
    build(nc, aps)
    r = run_bass_kernel_spmd(nc, [arrays], core_ids=[0])
    return tuple(r.results[0]["out_" + name] for name, _ in OUTPUTS)
```

```python
from contextlib import ExitStack

import numpy as np

import concourse.bass as bass
from concourse import mybir

F32 = mybir.dt.float32
F32R = mybir.dt.float32r
BF16 = mybir.dt.bfloat16
I32 = mybir.dt.int32
ALU = mybir.AluOpType
ACT = mybir.ActivationFunctionType
AX = mybir.AxisListType
ds = bass.ds

P = 128
D = 1024
NL = 2
SEQ = 512
NSEQ, TS = 8, 4
NSAM = NSEQ * TS
TOK = SEQ + NSAM
HALF = TOK // 2
KT = D // P
NT = SEQ // P
HD = 64
GROUPS, REP = 4, 4
KV = GROUPS * HD
PAGE = 128
NPAGE = 8
PAST = PAGE * NPAGE
WIN = 512
PLE = 256
HC = 8
NWP = SEQ // 16 - 1
NWS = PAST // 16 - 1
HID = 256
SCALE = HD ** -0.5
NEG = -1e30
LOWEST = -1e29
EPS = 1e-6

C_BA, C_CA, C_XA, C_ZA, C_Q = 0, D, 2 * D, 3 * D, 4 * D
N_TM = D + 6 * KV + 48
C_ZB = C_Q + N_TM
C_MIX = C_ZB + D
IN_COLS = C_MIX + 2 * D
N_KVG = 6 * KV + 48
Z_KC, Z_VC, Z_KS, Z_VS, Z_KW, Z_VW, Z_G = (i * KV for i in range(7))
BW = 256
WW = 264
NQB, NKB = D // BW, N_KVG // WW
TM_BLOCKS = NQB + NKB
assert NKB * WW == N_KVG

B_CONV = 0
B_MA = 16
B_TM = 24
B_ZB = 34
B_MB = 38
B_WO = 46
B_PL = 50
NB = 56
PH = 15

def _const_layout():
    at, out = 0, {}
    for name, n in (("ident", P), ("ones", P), ("cos", 5 * 32), ("sin", 5 * 32), ("causal", P),
                    ("cmask", NT * 32), ("wmask", WIN), ("nmask", 4 * NSAM), ("gmask", 48), ("same", P),
                    ("iota", 16), ("pick", 4 * P), ("eps", 1)):
        out[name] = (at, n)
        at += n
    return out, at


CONST, NCONST = _const_layout()


def constants():
    c = np.zeros((P, NCONST), np.float32)

    def put(name, a):
        at, n = CONST[name]
        c[: a.shape[0], at:at + n] = a.reshape(a.shape[0], n)

    put("ident", np.eye(P, dtype=np.float32))
    put("ones", np.ones((P, P), np.float32))
    inv = np.power(10000.0, -np.arange(32) / 32).astype(np.float32)
    pos = np.concatenate([np.arange(SEQ), np.tile(PAST + np.arange(TS), NSEQ), np.zeros(P - NSAM)]).astype(np.float32)
    ang = (pos[:, None] * inv[None, :]).astype(np.float32).reshape(5, P, 32).transpose(1, 0, 2)
    put("cos", np.cos(ang))
    put("sin", np.sin(ang))
    q = np.arange(P)
    put("causal", np.where(q[:, None] >= q[None, :], 0.0, NEG).astype(np.float32))
    n = np.arange(32)
    qq = q[:, None, None] + P * np.arange(NT)[None, :, None]
    put("cmask", np.where((16 * n[None, None, :] + 31 <= qq) & (n < NWP)[None, None, :], 0.0, NEG).astype(np.float32))
    s2, g, t, r = np.unravel_index(q, (2, GROUPS, TS, REP))
    k, p = np.unravel_index(np.arange(WIN), (4, P))
    put("wmask", np.where((4 * p + k)[None, :] > t[:, None], 0.0, NEG).astype(np.float32))
    tok = np.arange(NSAM)
    nm = [np.where((tok[None, :] // TS == (2 * pair + s2)[:, None]) & (tok[None, :] % TS <= t[:, None]), 0.0, NEG)
          for pair in range(4)]
    put("nmask", np.stack(nm, 1).astype(np.float32))
    gr = np.arange(16)
    put("gmask", np.repeat((gr[None, :] == (g * REP + r)[:, None]).astype(np.float32)[:, :, None], 3, 2))
    key = (s2 * GROUPS + g) * TS + t
    put("same", (key[:, None] == key[None, :]).astype(np.float32))
    put("iota", np.tile(np.arange(16, dtype=np.float32), (P, 1)))
    pick = np.stack([(tok[:, None] == ((2 * pair + s2) * TS + t)[None, :]) for pair in range(4)], 1)
    put("pick", pick.astype(np.float32))
    put("eps", np.full((P, 1), EPS, np.float32))
    return c


def build(nc, a):
    ctx = ExitStack()
    with ctx:
        sems = []

        def sem(name, head_start=0):
            handle = ctx.enter_context(nc.semaphore(name))
            sems.append((handle, head_start))
            return handle

        def nth(semaphore, n):
            return n + sum(head for handle, head in sems if handle is semaphore)

        base = [16512]

        def fixed(name, shape, dt=F32):
            t = nc.alloc_sbuf_tensor_at(name, shape, dt, offset=base[0])
            base[0] += (4 * int(np.prod(shape[1:])) + 31) // 32 * 32
            return t

        xT = fixed("xT", [P, KT, TOK])
        m = fixed("m", [P, KT, TOK])
        rstd = fixed("rstd", [P, TOK])
        con = fixed("con", [P, NCONST])
        cols = fixed("cols", [P, KT, 21])
        qs = fixed("qs", [P, 2, 2, 2, 32])
        kcT_s = fixed("kcT_s", [P, 2, NSEQ, 64])
        kcT_p = fixed("kcT_p", [P, 2, 32])
        vc_s = fixed("vc_s", [64, NSEQ * KV])
        vc_p = fixed("vc_p", [P, KV])
        knT = fixed("knT", [P, 4, NSAM])
        qsT = fixed("qsT", [P, KT, NSAM])
        hb = fixed("hb", [P, 2])
        small = fixed("small", [P, 128])
        grow = fixed("grow", [P, 4, 3])
        mask2 = fixed("mask2", [P, 2, P], BF16)
        pages = fixed("pages", [1, NSEQ * NPAGE], I32)
        tails = fixed("tails", [P, KT, 18])
        cst = fixed("cst", [P, 2, 21])
        D0 = base[0]

        def at(name, shape, off, dt=F32):
            return nc.alloc_sbuf_tensor_at(name, shape, dt, offset=D0 + off)

        R_Z, R_A, R_T = 86272, 103680, 138496
        w_raw = at("w_raw", [P, 2, KT, WW], 0)
        wH = at("wH", [P, 2, KT, WW], 17152, F32R)
        wL = at("wL", [P, 2, KT, WW], 34304, F32R)
        hH = at("hH", [P, KT, TOK], 51456, F32R)
        hL = at("hL", [P, KT, TOK], 68864, F32R)
        zq = at("zq", [P, 5, D], R_Z)
        zk = at("zk", [P, 5, N_KVG], R_Z + 20480)
        aH = at("aH", [P, KT, TOK], R_A, F32R)
        aL = at("aL", [P, KT, TOK], R_A + 17408, F32R)
        yT = at("yT", [P, KT, TOK], R_Z)
        xin = at("xin", [P, 5, D], R_Z)
        cv_in = at("cv_in", [P, 4, 2, TOK], R_Z)
        UW = SEQ + 2 + NSEQ * 6
        cv_u = at("cv_u", [P, 2, UW], R_T)
        cv_y = at("cv_y", [P, UW], R_T + -(-2 * UW * 4 // 32) * 32)
        sq = at("sq", [P, 2, TOK], R_T)
        ssq = at("ssq", [P, TOK], R_T + 4352)
        rows21 = at("rows21", [21, D], R_A)
        tail_rows = at("tail_rows", [18, D], R_T + 2048)
        rope_a = at("rope_a", [P, 2, 256], R_T)
        w1H = at("w1H", [P, 16, HID], 0, F32R)
        w1L = at("w1L", [P, 16, HID], 16384, F32R)
        chH = at("chH", [P, 2, 2, P, GROUPS], 32768, F32R)
        chL = at("chL", [P, 2, 2, P, GROUPS], 40960, F32R)
        craw = at("craw", [P, 2, 2, HC, KV], 49152)
        w1_raw = craw[:, 1].rearrange("p s t c -> p (s t c)").rearrange("p (k h) -> p k h", k=16)
        hidT = at("hidT", [P, 2, 504], 81920)
        hsg = at("hsg", [P, 2, 504], R_T)
        w2 = at("w2", [P, 2, HD], R_T + 4032)
        qT = at("qT", [P, KT, SEQ], 0)
        cs = at("cs", [P, 2 * KT * NT, 32], 16384)
        cT = at("cT", [P, 2, KT, P], 24576)
        cx = at("cx", [P, 4, SEQ], 49152)
        kT = at("kT", [P, 2, 2, SEQ], 32768)
        pr = at("pr", [P, 2, 2, SEQ], 40960)
        prT = at("prT", [P, 2, 2, SEQ], 49152)
        qst = at("qst", [P, 2, SEQ], 57344)
        cTs = at("cTs", [P, 2, 2, P], 61440)
        yy = at("yy", [P, 2, P], 63488)
        cmx = at("cmx", [P, 2 * KT * NT], 64512)
        ow = at("ow", [P, 6, HD], 81920)
        skv = at("skv", [P, 2, 2, HC, 2 * KV], 0)
        swin = at("swin", [P, 2, 4, 2 * KV], 65536)
        R_S = R_Z + 20480
        skT = at("skT", [P, 4, 512], R_T - 64)
        ssel = at("ssel", [P, PAST + NSAM], R_S)
        swsc = at("swsc", [P, WIN + NSAM], R_S + 4224)
        spT = at("spT", [P, 16, P], R_S + 6400)
        pc = at("pc", [P, 64], R_S + 14592)
        sy = at("sy", [P, KV], R_S + 14848)
        assert 15872 <= 4 * N_KVG * 4
        t_f = at("t_f", [P, 4, TOK], R_T)
        pin = at("pin", [P, 5, PLE], R_Z)
        pH = at("pH", [P, 2, TOK], R_Z + 5120, F32R)
        pL = at("pL", [P, 2, TOK], R_Z + 9472, F32R)
        out_rows = at("out_rows", [P, 5, D], R_Z)

        ps = ctx.enter_context(nc.psum_tensor("ps", [P, 8, 512], F32))

        def C(name, rows=P):
            o, n = CONST[name]
            return con[0:rows, o:o + n]

        ident = C("ident")

        s_const, s_x, s_zero = sem("s_const"), sem("s_x"), sem("s_zero")
        passed = sem("passed")
        phase = sem("phase")
        w_in_sem = [sem("w_loaded0"), sem("w_loaded1")]
        w_hi = sem("w_hi")
        w_lo = sem("w_lo", 2)
        w_done = sem("w_done", 2)
        x_tp, x_free = sem("x_tp"), sem("x_free", 4)
        sq_ready, sq_used, sq_sum, ss_ready, std_ready = sem("sq_ready"), sem("sq_used", 2), sem("sq_sum"), sem("ss_ready"), sem("std_ready")
        st_in, st_tp = sem("st_in"), sem("st_tp")
        h_f, h_hi, h_lo = sem("h_f"), sem("h_hi"), sem("h_lo")
        cv, cv_act, cv_sg, cv_dve = sem("cv"), sem("cv_act", 8), sem("cv_sg"), sem("cv_dve", 8)
        cv_f, cv_hi, cv_used = sem("cv_f"), sem("cv_hi"), sem("cv_used", 2)
        mg, mg_sg, mg_dve = sem("mg"), sem("mg_sg"), sem("mg_dve", 4)
        tail_tp, tail_cp, tail_out = sem("tail_tp"), sem("tail_cp"), sem("tail_out")
        tm, tm_ev = sem("tm"), sem("tm_ev", 5)
        z_ready, kv_out = sem("z_ready"), sem("kv_out")
        pg_in, w1_in, w1_hi, w1_lo, w2_in = sem("pg_in"), sem("w1_in"), sem("w1_hi"), sem("w1_lo"), sem("w2_in")
        pos_ready = sem("pos_ready")
        c_in = [sem("chunks_loaded0"), sem("chunks_loaded1")]
        c_prompt = sem("c_prompt")
        c_free = sem("c_free", 2)
        c_tp, c_hi, c_lo, c_mm = sem("c_tp"), sem("c_hi"), sem("c_lo", 4), sem("c_mm", 2)
        c_acc, c_sg, c_hid, c_w2, c_out = sem("c_acc"), sem("c_sg"), sem("c_hid", 2), sem("c_w2", 1), sem("c_out", 1)
        tp = [sem("tp_even"), sem("tp_odd")]
        tp_free = [sem("tp_even_free", 4), sem("tp_odd_free", 4)]
        pa_cm, pa_cx = sem("pa_cm"), (sem("pa_cx_act"), sem("pa_cx_dve"))
        pa_c, pa_csub, pa_cexp = sem("pa_c"), sem("pa_csub"), sem("pa_cexp")
        pa_cn, pa_ct = sem("pa_cn"), sem("pa_ct")
        pa_ctev = [sem("pa_ctev_act"), sem("pa_ctev_dve")]
        pa_q, pa_cst = sem("pa_q"), sem("pa_cst")
        pa_s = sem("pa_s")
        pa_nm = sem("pa_nm")
        pa_exp = sem("pa_exp", 4)
        pa_t, pa_te = sem("pa_t", 2), sem("pa_te", 4)
        pa_pv = sem("pa_pv", 2)
        pa_o, pa_y = sem("pa_o", 4), sem("pa_y", 2)
        pa_yt, pa_yo = sem("pa_yt", 1), sem("pa_yo", 3)
        s_kv = [sem("s_kv0"), sem("s_kv1")]
        s_win, s_winout, s_fin = sem("s_win"), sem("s_winout"), sem("s_fin", 2)
        sa_g, sa_gr, sa_q, sa_c, sa_nm, sa_cx = (sem(n) for n in ("sa_g", "sa_gr", "sa_q", "sa_c", "sa_nm", "sa_cx"))
        sa_kt, sa_ke, sa_s = sem("sa_kt"), sem("sa_ke", 2), sem("sa_s", 4)
        sa_im, sa_imp, sa_m, sa_e, sa_t, sa_te = (sem(n) for n in ("sa_im", "sa_imp", "sa_m", "sa_e", "sa_t", "sa_te"))
        sa_o, sa_y, sa_yt, sa_ys = sem("sa_o"), sem("sa_y"), sem("sa_yt", 1), sem("sa_ys")
        zb, zb_sg, zb_f, zb_hi, zb_done = sem("zb"), sem("zb_sg"), sem("zb_f"), sem("zb_hi"), sem("zb_done", 4)
        wo, wo_done = sem("wo"), sem("wo_done", 4)
        sp_hi, sp_lo, p_lo, p_in, p_tp, p_hi = sem("sp_hi"), sem("sp_lo"), sem("p_lo"), sem("p_in"), sem("p_tp"), sem("p_hi")
        pl, pl_sg, pl_done = sem("pl"), sem("pl_sg"), sem("pl_done", 4)
        y_ready, y_tp, y_act, y_dve, out_done = sem("y_ready"), sem("y_tp"), sem("y_act", 4), sem("y_dve", 4), sem("out_done")

        def phase_over(eng, l, k):
            eng.wait_ge(phase, 3 * (l * PH + k + 2))
            eng.sem_inc(passed, 1)

        def leave_phase(eng):
            eng.drain().then_inc(phase, 1)

        def end_phase(eng, l, k):
            eng.drain().then_inc(phase, 1)
            phase_over(eng, l, k)

        def wide(w, par):
            return w[:, par].rearrange("p k c -> p (k c)")[:, 0:1024].rearrange("p (k c) -> p k c", k=2)

        def ct_bank(b):
            return cT[:].rearrange("p g h q -> p (g h q)")[:, b * SEQ:(b + 1) * SEQ]

        def make_high(act, l, b, par, nk=KT, width=BW, wide_block=False):
            to, frm = (wide(wH, par), wide(w_raw, par)) if wide_block else (wH[:, par, 0:nk, 0:width], w_raw[:, par, 0:nk, 0:width])
            act.wait_ge(w_in_sem[par], 64 * (l * (NB // 2) + b // 2 + 1 if isinstance(b, int) else l * (NB // 2) + b[1] + 1))
            act.wait_ge(w_done, nth(w_done, l * NB + blk(b) - 1))
            act.activation(to, frm, ACT.Copy).then_inc(w_hi, 1)

        def make_low(dve, l, b, par, nk=KT, width=BW, wide_block=False):
            to, frm, high = (wide(w, par) if wide_block else w[:, par, 0:nk, 0:width] for w in (wL, w_raw, wH))
            dve.wait_ge(w_hi, l * NB + blk(b) + 1)
            dve.tensor_tensor(to, frm, high.bitcast(F32), ALU.subtract).then_inc(w_lo, 1)

        def blk(b):
            return b if isinstance(b, int) else 2 * b[1] + b[2]

        def pb(base_block, half, odd):
            return ("b", base_block // 2 + half, odd)

        def two(t, c):
            return t[:].rearrange("p k t -> p (k t)")[:, ds(c * TOK, TOK)].rearrange("p (a b) -> p a b", a=2)

        def one(t, c):
            return t[:].rearrange("p k t -> p (k t)")[:, ds(c * TOK, TOK)]

        def bank2(n):
            return ps[:, n:n + 2, 0:HALF]

        def halves(t):
            return t.rearrange("p (a b) -> p a b", a=2)

        def unit_shape(n):
            return (68, 1, NWP + 2) if n % 5 == 0 else (P, 2, NWS)

        def unit_slot(n):
            return (0, 0, 1, 0, 1)[n % 5]

        block = ctx.enter_context(nc.Block())

        @block.sync
        def _(sp):
            sp.dma_start(con[:], a["consts"]).then_inc(s_const, 16)
            sp.dma_start(pages[:], a["page_table"].rearrange("(o a) b -> o (a b)", o=1)).then_inc(pg_in, 16)
            sp.dma_start(xin[:, 0:NT, :], a["x_prompt"].rearrange("b (t p) d -> p (b t) d", p=P)).then_inc(s_x, 16)
            sp.dma_start(xin[0:NSAM, NT, :], a["x_sample"].rearrange("b t d -> (b t) d")).then_inc(s_x, 16)
            sp.wait_ge(pg_in, 16)
            sp.wait_ge(s_zero, 1)

            def load_w(l, b, par, src, nk=KT, width=BW):
                sp.wait_ge(w_lo, nth(w_lo, l * NB + b - 1))
                sp.dma_start(w_raw[:, par, 0:nk, 0:width], src).then_inc(w_in_sem[par], 64)

            def w_cols(name, l, col, width=BW):
                w = a[name][ds(l, 1)].rearrange("l (k p) c -> p (l k) c", p=P)
                return w[:, :, ds(col, width)]

            def page_rows(l, seq, j, first, n):
                page = sp.value_load(pages[0:1, ds(seq * NPAGE + j, 1)], min_val=0, max_val=a["cache_kv"].shape[1] - 1)
                return a["cache_kv"][ds(l, 1), ds(page, 1), :, first:first + n].rearrange("l o (c t) s g d -> c (l o t) (s g d)", t=HC)

            with sp.Fori(0, NL) as l:
                with sp.Fori(0, 4) as i:
                    for n, c0 in enumerate((C_CA, C_XA, C_BA, C_ZA)):
                        load_w(l, B_CONV + 4 * i + n, n % 2, w_cols("w_in", l, c0 + BW * i))
                with sp.Fori(0, 4) as i:
                    load_w(l, B_MA + 2 * i, 0, w_cols("w_in", l, C_MIX + BW * i))
                    load_w(l, B_MA + 2 * i + 1, 1, w_cols("w_out_a", l, BW * i))
                with sp.Fori(0, NQB // 2) as i:
                    for n in range(2):
                        load_w(l, B_TM + 2 * i + n, n, w_cols("w_in", l, 2 * BW * i + C_Q + n * BW, WW), width=WW)
                with sp.Fori(0, NKB // 2) as i:
                    for n in range(2):
                        load_w(l, B_TM + NQB + 2 * i + n, n, w_cols("w_in", l, 2 * WW * i + C_Q + D + n * WW, WW), width=WW)
                sp.wait_ge(w_done, nth(w_done, l * NB + B_TM + TM_BLOCKS))
                for kv, (w1, w2n, pos) in enumerate((("cmp_w1_k", "cmp_w2_k", "cmp_pos_k"), ("cmp_w1_v", "cmp_w2_v", "cmp_pos_v"))):
                    def load_w1():
                        sp.dma_start(w1_raw, a[w1][ds(l, 1)].rearrange("l (k s) d h -> (s d) (l k) h", s=2)).then_inc(w1_in, 16)

                    def load_pages(n, s):
                        sp.sem_inc(passed, 1)
                        for j in range(NPAGE):
                            src = page_rows(l, 2 * (n % 5) - 2 + s, j, kv, 1)
                            sp.dma_start(craw[16 * j:16 * j + 16, unit_slot(n), s], src).then_inc(c_in[unit_slot(n)], 16)

                    first = 5 * kv
                    if kv == 0:
                        load_w1()
                        sp.wait_ge(z_ready, l + 1)
                        sp.dma_start(a["new_kv_prompt"][ds(l, 1)].rearrange("l b (t p) s g d -> p (l b t) (s g d)", p=P),
                                     zk[:, 0:NT, 0:4 * KV]).then_inc(kv_out, 16)
                        sp.dma_start(a["new_win_prompt"][ds(l, 1)].rearrange("l b (t p) s g d -> p (l b t) (s g d)", p=P),
                                     zk[:, 0:NT, Z_KW:Z_KW + 2 * KV]).then_inc(kv_out, 16)
                        sp.dma_start(a["new_kv_sample"][ds(l, 1)].rearrange("l b t s g d -> (l b t) (s g d)"),
                                     zk[0:NSAM, NT, 0:4 * KV]).then_inc(kv_out, 16)
                        sp.dma_start(a["new_win_sample"][ds(l, 1), :, WIN - TS:WIN].rearrange("l b t s g d -> (l b) t (s g d)"),
                                     zk[0:NSAM, NT, Z_KW:Z_KW + 2 * KV]).then_inc(kv_out, 16)
                        sp.wait_ge(kv_out, 64 * l + 64)

                    sp.wait_ge(c_free, nth(c_free, 10 * l + max(first - 1, 0)))
                    sp.dma_start(craw[0:64, 0, 0],
                                 a["new_kv_prompt"][ds(l, 1), :, :, kv].rearrange("l b (c t) g d -> c (l b t) (g d)", t=HC)).then_inc(c_prompt, 16)
                    for g in range(GROUPS):
                        sp.dma_start(craw[64:68, 0, 0, :, g * HD:(g + 1) * HD],
                                     a[pos][ds(l, 1)].rearrange("l (c t) d -> (l c) t d", t=HC)).then_inc(c_prompt, 16)
                    load_pages(first + 1, 1)
                    if kv == 1:
                        sp.wait_ge(c_free, nth(c_free, 10 * l + first))
                        load_w1()
                    sp.wait_ge(c_free, nth(c_free, 10 * l + first + 1))
                    load_pages(first + 1, 0)
                    sp.wait_ge(c_w2, nth(c_w2, 10 * l + first))
                    sp.dma_start(w2[:], a[w2n][ds(l, 1)].rearrange("l (k p) d -> p (l k) d", p=P)).then_inc(w2_in, 16)
                    sp.wait_ge(w1_lo, 8 * l + (4 * kv + 4))
                    for n in (first + 2, first + 3, first + 4):
                        if n > first + 2:
                            sp.wait_ge(c_free, nth(c_free, 10 * l + n - 1))
                        for s in range(2):
                            load_pages(n, s)

                sp.wait_ge(pa_cst, 9 * l + 9)
                sp.sem_inc(passed, 1)
                with sp.Fori(0, 2) as pp:
                    for par in range(2):
                        if par == 1:
                            phase_over(sp, l, 7)
                        sp.wait_ge(s_fin, nth(s_fin, 4 * l + 2 * pp + (par - 1)))
                        for s in range(2):
                            for j in range(NPAGE):
                                src = page_rows(l, 4 * pp + (2 * par + s), j, 2, 2)
                                sp.dma_start(skv[16 * j:16 * j + 16, par, s], src).then_inc(s_kv[par], 16)

                phase_over(sp, l, 8)
                with sp.Fori(0, 2) as gp:
                    for n in range(2):
                        sp.wait_ge(w_lo, nth(w_lo, l * NB + 2 * gp + (B_ZB + n - 1)))
                        src = w_cols("w_in", l, 512 * gp + C_ZB, 512)
                        for g in range(2):
                            for jj in range(2):
                                to, frm = jj * P + g * HD, g * KV + (2 * n + jj) * HD
                                sp.dma_start(w_raw[:, n, :, to:to + HD], src[:, :, frm:frm + HD]).then_inc(w_in_sem[n], 16)
                with sp.Fori(0, 4) as i:
                    load_w(l, B_MB + 2 * i, 0, w_cols("w_in", l, BW * i + (C_MIX + D)))
                    sp.wait_ge(w_lo, nth(w_lo, l * NB + 2 * i + B_MB))
                    for g in range(2):
                        for gp in range(2):
                            rows = a["w_out_b"][ds(l, 1), 512 * gp + KV * g:512 * gp + KV * g + KV].rearrange("l (c d) n -> d (l c) n", d=HD)
                            sp.dma_start(w_raw[g * 64:(g + 1) * 64, 1, 4 * gp:4 * gp + 4, 0:BW], rows[:, :, ds(BW * i, BW)]).then_inc(w_in_sem[1], 16)
                with sp.Fori(0, 2) as i:
                    for n in range(2):
                        load_w(l, B_WO + 2 * i + n, n, w_cols("w_o", l, 2 * BW * i + BW * n))
                for i in range(2):
                    for n in range(2):
                        load_w(l, B_PL + 3 * i + n, (i + n) % 2, w_cols("w_ple_gate", l, BW * (2 * i + n)))
                    sp.wait_ge(w_lo, nth(w_lo, l * NB + B_PL + 3 * i + 1))
                    sp.dma_start(wide(w_raw, i), w_cols("w_ple", l, 512 * i, 512)).then_inc(w_in_sem[i], 64)

            for tt in range(5):
                sp.wait_ge(y_act, nth(y_act, tt + 1))
                sp.wait_ge(y_dve, nth(y_dve, tt + 1))
                if tt < NT:
                    sp.dma_start(a["y_prompt"][0, tt * P:(tt + 1) * P, :], out_rows[:, tt, :]).then_inc(out_done, 16)
                else:
                    sp.dma_start(a["y_sample"].rearrange("b t d -> (b t) d"), out_rows[0:NSAM, tt, :]).then_inc(out_done, 16)
            sp.wait_ge(out_done, 80)

        @block.gpsimd
        def _(pool):
            for handle, head_start in sems:
                if head_start:
                    pool.sem_inc(handle, head_start)
            pool.memset(qs[:], 0.0)
            pool.memset(vc_p[:], 0.0)
            pool.memset(kcT_p[:], 0.0)
            pool.memset(small[:], 0.0)
            pool.drain()
            pool.memset(small[:, 24:30], 1.0)
            pool.memset(small[:, 76:79], 1.0)
            pool.drain().then_inc(s_zero, 1)
            with pool.Fori(0, NL) as l:
                phase_over(pool, l, -1)
                pool.dma_start(rows21[0:16, :], a["state_conv"][ds(l, 1)].rearrange("l b t c -> (l b t) c")).then_inc(st_in, 16)
                pool.dma_start(rows21[16:19, :], a["conv_w"][ds(l, 1)].rearrange("l t c -> (l t) c")).then_inc(st_in, 16)
                pool.dma_start(rows21[19:20, :], a["ln_g"][ds(l, 1)]).then_inc(st_in, 16)
                pool.dma_start(rows21[20:21, :], a["final_g"].rearrange("(o d) -> o d", o=1)).then_inc(st_in, 16)
                pool.wait_ge(tail_cp, 2 * l + 2)
                pool.dma_start(a["new_conv_prompt"][ds(l, 1)].rearrange("l b t c -> (l b t) c"), tail_rows[0:2, :]).then_inc(tail_out, 16)
                pool.dma_start(a["new_conv_sample"][ds(l, 1)].rearrange("l b t c -> (l b t) c"), tail_rows[2:18, :]).then_inc(tail_out, 16)
                pool.wait_ge(tail_out, 32 * l + 32)
                flat_q, flat_c = qT[:].rearrange("p k t -> p (k t)"), cT[:].rearrange("p g h q -> p g (h q)")
                phase_over(pool, l, 6)
                pool.tensor_copy(qst[:, 0, :], qT[:, 0, :]).then_inc(pa_q, 1)
                for n in range(2):
                    pool.wait_ge(pa_ctev[n], 2 * l + 2)
                pool.sem_inc(passed, 1)
                pool.tensor_copy(cTs[:, 0], cT[:, :, 0, :]).then_inc(pa_cst, 1)
                with pool.Fori(0, REP) as r:
                    for gp in range(2):
                        pool.wait_ge(pa_pv, nth(pa_pv, 64 * l + 16 * r + 8 * gp))
                        pool.sem_inc(passed, 1)
                        head = (REP, 1)[gp]
                        pool.tensor_copy(qst[:, 1 - gp, :], flat_q[:, ds(SEQ * r + SEQ * head, SEQ)]).then_inc(pa_q, 1)
                        pool.tensor_copy(cTs[:, 1 - gp], flat_c[:, :, ds(P * r + P * head, P)]).then_inc(pa_cst, 1)
                with pool.Fori(0, 4) as pair:
                    pool.wait_ge(s_fin, nth(s_fin, 4 * l + pair))
                    for s in range(2):
                        pool.dma_start(swin[:, s].rearrange("p k c -> p (k c)"),
                                       a["state_win"][ds(l, 1), ds(2 * pair + s, 1)].rearrange("l b (p k) s g d -> (l b p) (k s g d)", k=4)
                                       ).then_inc(s_win, 16)
                    pool.wait_ge(s_win, 128 * l + 32 * pair + 32)
                    pool.sem_inc(passed, 1)
                    for s in range(2):
                        dst = a["new_win_sample"][ds(l, 1), ds(2 * pair + s, 1), 0:WIN - TS].rearrange("l b (p k) s g d -> (l b p) (k s g d)", k=4)
                        for lo, hi in ((1, 113), (113, 128)):
                            pool.dma_start(dst[lo - 1:hi - 1], swin[lo:hi, s].rearrange("p k c -> p (k c)")).then_inc(s_winout, 16)
                    pool.wait_ge(s_winout, 256 * l + 64 * pair + 64)
                phase_over(pool, l, 10)
                pool.dma_start(pin[:, 0:NT, :], a["p_prompt"][ds(l, 1)].rearrange("l b (t p) d -> p (l b t) d", p=P)).then_inc(p_in, 16)
                pool.dma_start(pin[0:NSAM, NT, :], a["p_sample"][ds(l, 1)].rearrange("l b t d -> (l b t) d")).then_inc(p_in, 16)

        @block.tensor
        def _(pe):
            def norm_sum(l):
                pe.wait_ge(sq_sum, l + 1)
                for hf in range(2):
                    last = nc.tensor.matmul(ps[:, hf, 0:HALF], C("ones"), ssq[:, hf * HALF:(hf + 1) * HALF], start=True, stop=True)
                last.then_inc(ss_ready, 1)

            def fm_tile(par, jj, bank, xH, xL, nk=KT, parts=None, before=0):
                for k in range(nk):
                    if parts is not None:
                        pe.wait_ge(parts, before + (k + 1))
                    for w, x in ((wH, xH), (wH, xL), (wL, xH)):
                        st = w[:, par, k, jj * P:(jj + 1) * P]
                        for hf in range(2):
                            last = nc.tensor.matmul(ps[:, bank + hf, 0:HALF], st, x[:, k, hf * HALF:(hf + 1) * HALF],
                                                    start=k == 0 and w is wH and x is xH, stop=k == nk - 1 and w is wL)
                return last

            pe.wait_ge(s_const, 16)
            pe.wait_ge(s_x, 32)
            for c in range(KT):
                pe.wait_ge(x_free, nth(x_free, c - 3))
                for tt in range(5):
                    rows = P if tt < NT else NSAM
                    last = nc.tensor.transpose(ps[:, 2 * (c % 4) + tt // NT, (tt % NT) * P:(tt % NT) * P + rows],
                                               xin[0:rows, tt, c * P:(c + 1) * P], ident[0:rows, 0:rows])
                last.then_inc(x_tp, 1)
            end_phase(pe, 0, -1)

            with pe.Fori(0, NL) as l:
                pe.wait_ge(st_in, 64 * l + 64)
                pe.sem_inc(passed, 1)
                for c in range(KT):
                    last = nc.tensor.transpose(ps[:, 2, c * 21:(c + 1) * 21], rows21[:, c * P:(c + 1) * P], ident[0:21, 0:21])
                last.then_inc(st_tp, 1)
                norm_sum(l)
                leave_phase(pe)
                with pe.Fori(0, 4) as i:
                    for kind in range(4):
                        pe.wait_ge(w_lo, nth(w_lo, l * NB + 4 * i + (B_CONV + kind + 1)))
                        for jj in range(2):
                            q = 2 * kind + jj
                            if kind == 0:
                                pe.wait_ge(cv_act, nth(cv_act, 24 * l + 6 * i + (jj - 1)))
                            elif kind == 1:
                                pe.wait_ge(cv_dve, nth(cv_dve, 8 * l + 2 * i + (jj - 1)))
                            else:
                                pe.wait_ge(cv_act, nth(cv_act, 24 * l + 6 * i + (q - 3)))
                            last = fm_tile(kind % 2, jj, 2 * (q % 4), hH, hL, parts=h_lo if q == 0 else None, before=16 * l)
                            if jj == 0:
                                last.then_inc(cv, 1)
                        last.then_inc(cv, 1)
                        pe.drain().then_inc(w_done, 1)
                end_phase(pe, l, 1)

                def merge(which, first_block, gate, branch):
                    with pe.Fori(0, 4) as i:
                        for n in range(2):
                            pe.wait_ge(w_lo, nth(w_lo, l * NB + 2 * i + (first_block + n + 1)))
                            for jj in range(2):
                                pe.wait_ge(mg_dve, nth(mg_dve, 16 * l + 2 * i + (8 * which + jj - 1)))
                                last = fm_tile(n, jj, 2 * (2 * n + jj), *(branch if n else gate))
                                last.then_inc(mg, 1)
                            pe.drain().then_inc(w_done, 1)

                merge(0, B_MA, (hH, hL), (aH, aL))
                end_phase(pe, l, 2)
                for c in range(KT):
                    last = nc.tensor.transpose(ps[0:18, 6 + c // 4, (c % 4) * P:(c % 4 + 1) * P], tails[:, c, :], ident)
                last.then_inc(tail_tp, 1)

                def token_major(b, half, n, width):
                    pe.wait_ge(w_lo, nth(w_lo, l * NB + 2 * half + (B_TM + b + n + 1)))
                    for tt in range(5):
                        rows = P if tt < NT else NSAM
                        pe.wait_ge(tm_ev, nth(tm_ev, l * (5 * TM_BLOCKS) + 10 * half + (5 * (b + n) + tt - 4)))
                        for k in range(KT):
                            for w, x in ((wH, hH), (wL, hH), (wH, hL)):
                                last = nc.tensor.matmul(ps[0:rows, tt, 0:width], x[:, k, tt * P:tt * P + rows], w[:, n, k, 0:width],
                                                        start=k == 0 and w is wH and x is hH, stop=k == KT - 1 and x is hL)
                        last.then_inc(tm, 1)
                    pe.drain().then_inc(w_done, 1)

                with pe.Fori(0, NQB // 2) as i:
                    for n in range(2):
                        token_major(0, i, n, BW)
                with pe.Fori(0, NKB // 2) as i:
                    for n in range(2):
                        token_major(NQB, i, n, WW)
                end_phase(pe, l, 3)


                def chunk_tp(n, j):
                    unit = 10 * l + n
                    rows, nseq, _ = unit_shape(n)
                    if j == 0 and nseq == 1:
                        pe.wait_ge(c_prompt, 160 * l + (80 * (n // 5) + 80))
                    elif j == 0:
                        pe.wait_ge(c_in[unit_slot(n)], 1024 * l + (512 * (n // 5) + 256 * ((n % 5 + 1) // 2)))
                    for s in range(nseq):
                        m = 8 * n + 2 * j + s
                        pe.wait_ge(c_lo, nth(c_lo, 80 * l + max(m - 2, 0)))
                        for k in range(4):
                            t, g2 = k // 2, k % 2
                            last = nc.tensor.transpose(ps[:, m % 3, k * P:k * P + rows],
                                                       craw[0:rows, unit_slot(n), s, 2 * j + t, g2 * P:(g2 + 1) * P], ident[0:rows, 0:rows])
                        last.then_inc(c_tp, 1)
                    if nseq == 1:
                        pe.drain().then_inc(c_tp, 1)
                    if j == 3:
                        pe.drain().then_inc(c_free, 1)

                def first_layer(n, j):
                    unit = 10 * l + n
                    rows, nseq, nwin = unit_shape(n)
                    pe.wait_ge(c_lo, nth(c_lo, 8 * unit + (2 * j + 2)))
                    if n % 5 == 0:
                        pe.wait_ge(w1_lo, 8 * l + (4 * (n // 5) + j + 1))
                    if j == 0:
                        pe.wait_ge(c_hid, nth(c_hid, 2 * unit - 2))
                    for hid in range(2):
                        if hid == 1 and 4 * n + j < 38:
                            chunk_tp(n + (j + 2) // 4, (j + 2) % 4)
                        for quarter in range(4):
                            for w, x in ((w1H, chH), (w1H, chL), (w1L, chH)):
                                span = slice(quarter, quarter + 2 * nwin - 1, 2)
                                rhs = x[:, j % 2, :, span, :] if nseq == 2 else x[:, j % 2, 0, span, :]
                                last = nc.tensor.matmul(ps[:, 4 + 2 * (n % 2) + hid, 0:nseq * nwin * GROUPS],
                                                        w[:, 4 * quarter + j, hid * P:(hid + 1) * P], rhs,
                                                        start=j == 0 and quarter == 0 and w is w1H and x is chH,
                                                        stop=j == 3 and quarter == 3 and w is w1L)
                    last.then_inc(c_mm, 1)
                    if j == 3:
                        pe.drain().then_inc(c_acc, 1)

                def second_layer(n):
                    unit = 10 * l + n
                    _, nseq, nwin = unit_shape(n)
                    nwin = min(nwin, NWP) if nseq == 1 else nwin
                    cols = nseq * nwin * GROUPS
                    pe.wait_ge(c_hid, nth(c_hid, 2 * unit + 2))
                    pe.wait_ge(c_out, nth(c_out, unit))
                    pe.wait_ge(w2_in, 32 * l + 16 * (n // 5) + 16)
                    if n < 5:
                        for hid in range(2):
                            last = nc.tensor.matmul(ps[0:HD, 3, 0:cols], w2[:, hid, :], hidT[:, hid, 0:cols], start=hid == 0, stop=hid == 1)
                    else:
                        for s in range(nseq):
                            for g in range(GROUPS):
                                first = s * nwin * GROUPS + g
                                o = (s * GROUPS + g) * HD
                                for hid in range(2):
                                    last = nc.tensor.matmul(ps[0:nwin, 3, o:o + HD],
                                                            hidT[:, hid, first:first + (nwin - 1) * GROUPS + 1:GROUPS], w2[:, hid, :],
                                                            start=hid == 0, stop=hid == 1)
                    last.then_inc(c_w2, 1)

                chunk_tp(0, 0)
                chunk_tp(0, 1)
                for n in range(10):
                    first_layer(n, 0)
                    if n:
                        second_layer(n - 1)
                    for j in range(1, 4):
                        first_layer(n, j)
                second_layer(9)
                end_phase(pe, l, 4)
                end_phase(pe, l, 5)

                def tp_job(k, parts):
                    pe.wait_ge(tp_free[k % 2], nth(tp_free[k % 2], 7 * l + (k // 2 - 3)))
                    pe.sem_inc(passed, 1)
                    for out, src, n in parts:
                        last = nc.tensor.transpose(out, src, ident[0:n, 0:n])
                    last.then_inc(tp[k % 2], 1)

                def q_cols(tt, rows, gp, r):
                    return zq[0:rows, tt, (4 * gp + r) * P:(4 * gp + r + 1) * P]

                for k in range(8):
                    tp_job(k, [(ps[:, k % 8, tt * P:(tt + 1) * P], q_cols(tt, P, k // 4, k % 4), P) for tt in range(NT)])
                for k in range(8, 12):
                    c0 = (Z_KS, Z_KW)[(k - 8) // 2] + (k % 2) * P
                    tp_job(k, [(ps[:, k % 8, tt * P:(tt + 1) * P], zk[:, tt, c0:c0 + P], P) for tt in range(NT)])
                tp_job(12, [(ps[:, 4, n * NSAM:(n + 1) * NSAM], q_cols(NT, NSAM, n // 4, n % 4), NSAM) for n in range(8)])
                tp_job(13, [(ps[:, 5, n * NSAM:(n + 1) * NSAM],
                             zk[0:NSAM, NT, (Z_KS, Z_KW)[n // 2] + (n % 2) * P:(Z_KS, Z_KW)[n // 2] + (n % 2 + 1) * P], NSAM) for n in range(4)])
                end_phase(pe, l, 6)

                for b in range(4):
                    rows = slice(64 * (b // 2), 64 * (b // 2) + 64)
                    for c in range(4):
                        last = nc.tensor.matmul(ps[32 * c:32 * c + 32, b, :], kcT_p[rows, b % 2, :], qT[rows, REP * (b % 2) + c, :],
                                                start=True, stop=True)
                    last.then_inc(pa_cm, 1)
                for b in range(4):
                    pe.wait_ge(pa_cx[b % 2], 2 * l + (b // 2 + 1))
                    for u in range(NT):
                        last = nc.tensor.transpose(ps[:, 4 + b, u * P:(u + 1) * P], cx[:, b, u * P:(u + 1) * P], ident)
                    last.then_inc(pa_c, 1)

                def scores(first, gp, k):
                    g, u = k % 2, k % 8 // 2
                    gp = (gp + k // 8) % 2
                    rows = slice(64 * g, 64 * g + 64)
                    pe.wait_ge(pa_exp, nth(pa_exp, 130 * l + 2 * first + (2 * k - 2)))
                    for br in range(2):
                        nc.tensor.matmul(ps[:, 2 * g + br, u * P:(u + 1) * P], mask2[:, 0, :], mask2[:, 1, :], start=True, stop=False)
                        last = nc.tensor.matmul(ps[:, 2 * g + br, u * P:(u + 1) * P], qst[rows, gp, u * P:(u + 1) * P], kT[rows, br, gp, u * P:(u + 1) * P],
                                         start=False, stop=True)
                        if u:
                            last = nc.tensor.matmul(ps[:, 2 * g + br, 0:u * P], qst[rows, gp, u * P:(u + 1) * P], kT[rows, br, gp, 0:u * P],
                                                    start=True, stop=True)
                    last.then_inc(pa_s, 1)

                def y_back(tile, bank):
                    pe.wait_ge(pa_y, nth(pa_y, tile))
                    nc.tensor.transpose(ps[:, bank, 384:512], yy[:, bank % 2, :], ident).then_inc(pa_yt, 1)

                pe.wait_ge(pa_q, 9 * l + 1)
                scores(0, 0, 0)
                scores(0, 0, 1)
                pe.wait_ge(pa_csub, l + 1)
                for n in range(10):
                    nc.tensor.matmul(ps[:, 4, :], ident, qT[:, 0, :], start=True, stop=True)
                pe.wait_ge(pa_cn, l + 1)
                for n in range(2 * KT):
                    last = nc.tensor.transpose(ps[:, 4 + n // 4, (n % 4) * P:(n % 4 + 1) * P],
                                               cs[:, 4 * n:4 * n + 4, :].rearrange("p a b -> p (a b)"), ident)
                    if n % 4 == 3:
                        last.then_inc(pa_ct, 1)
                for n in range(2):
                    pe.wait_ge(pa_ctev[n], 2 * l + 2)
                pe.sem_inc(passed, 1)
                def turn(unit, k, n):
                    u = k // 2
                    br, kt = divmod(n, u + 1)
                    if kt == 0:
                        pe.wait_ge(pa_exp, nth(pa_exp, 2 * unit + (2 * k + br + 1) + 2 * l))
                        pe.wait_ge(pa_te, nth(pa_te, 2 * unit + (2 * k + br - 1)))
                    last = nc.tensor.transpose(ps[:, 4 + br, kt * P:(kt + 1) * P], pr[:, k % 2, br, kt * P:(kt + 1) * P], ident)
                    if kt == u:
                        last.then_inc(pa_t, 1)

                def output(unit, gp, k, n):
                    g, u = k % 2, k // 2
                    head = 2 * gp + g
                    if n == 0:
                        q4 = slice(32 * u, 32 * u + 32)
                        nc.tensor.matmul(ps[:, 6 + u % 2, g * 3 * HD:g * 3 * HD + HD], cTs[q4, gp, g, :], vc_p[q4, head * HD:(head + 1) * HD],
                                         start=True, stop=True)
                        return
                    br, kt = divmod(n - 1, u + 1)
                    if kt == 0:
                        pe.wait_ge(pa_te, nth(pa_te, 2 * unit + (2 * k + br + 1)))
                    o, c0 = (g * 3 + br + 1) * HD, (Z_VS, Z_VW)[br] + head * HD
                    last = nc.tensor.matmul(ps[:, 6 + u % 2, o:o + HD], prT[:, k % 2, br, kt * P:(kt + 1) * P], zk[:, kt, c0:c0 + HD],
                                            start=kt == 0, stop=kt == u)
                    if n == 2 * (u + 1):
                        last.then_inc(pa_pv, 1)

                with pe.Fori(0, REP) as r:
                    for gp in range(2):
                        unit = 64 * l + 16 * r + 8 * gp
                        for k in range(9):
                            if k % 2 == 0 and k < 8:
                                y_back(32 * l + 8 * r + (4 * gp + (k - 4) // 2 + 1), 6 + (k // 2) % 2)
                            if k % 2 == 1:
                                scores(16 * r + 8 * gp, gp, k + 2)
                            if k == 1:
                                pe.wait_ge(pa_cst, 9 * l + 2 * r + (gp + 1))
                            if k % 2 == 1:
                                pe.wait_ge(pa_yo, nth(pa_yo, 34 * l + 8 * r + (4 * gp + (k - 1) // 2 + 1)))
                            turns = 2 * (k // 2 + 1) if k < 8 else 0
                            outputs = 2 * ((k - 1) // 2 + 1) + 1 if k else 0
                            for n in range(max(turns, outputs)):
                                if n < turns:
                                    turn(unit, k, n)
                                if n < outputs:
                                    output(unit, gp, k - 1, n)
                            if k == 6:
                                pe.wait_ge(pa_q, 9 * l + 2 * r + (gp + 2))
                            if k % 2 == 0 and k < 8:
                                scores(16 * r + 8 * gp, gp, k + 2)
                y_back(32 * l + 31, 6)
                y_back(32 * l + 32, 7)
                end_phase(pe, l, 7)

                for pair in range(4):
                    last = nc.tensor.matmul(ps[:, 7, pair * 48:(pair + 1) * 48], C("pick", NSAM)[:, pair * P:(pair + 1) * P],
                                            zk[0:NSAM, NT, Z_G:Z_G + 48], start=True, stop=True)
                last.then_inc(sa_g, 1)
                pe.wait_ge(sa_gr, l + 1)
                pe.sem_inc(passed, 1)
                def turn_back(pair):
                    pe.wait_ge(sa_y, 4 * l + (pair + 1))
                    for gp in range(2):
                        last = nc.tensor.transpose(ps[:, 7, gp * P:(gp + 1) * P], sy[:, gp * P:(gp + 1) * P], ident)
                    last.then_inc(sa_yt, 1)

                for pair in range(4):
                    par, it = pair % 2, 4 * l + pair
                    pe.wait_ge(sa_q, it + 1)
                    strips = [(s, gp, slice(64 * s + 32 * gp, 64 * s + 32 * gp + 32)) for s in range(2) for gp in range(2)]
                    for s, gp, rows in strips:
                        nc.tensor.matmul(ps[rows, 3, 0:NWS], qs[:, par, gp, s, :], kcT_s[:, gp, 2 * pair + s, 0:NWS], start=True, stop=True)
                    for s, gp, rows in strips:
                        last = nc.tensor.matmul(ps[rows, 3, 64:64 + 2 * NSAM], qs[:, par, gp, s, :], knT[:, gp:4:2, :], start=True, stop=True)
                    last.then_inc(sa_c, 1)
                    jobs = [(half, s, gp) for half in range(3) for s in range(2) for gp in range(2)]

                    def key_tp(k):
                        half, s, gp = jobs[k]
                        pe.wait_ge(sa_ke, nth(sa_ke, 12 * it + (k - 1)))
                        if k == 0:
                            pe.wait_ge(s_kv[par], 512 * l + (256 * (pair // 2) + 256))
                        if k == 8:
                            pe.wait_ge(s_win, 32 * it + 32)
                        for t in range(4):
                            src = swin[:, s, t, gp * P:(gp + 1) * P] if half == 2 else skv[:, par, s, 4 * half + t, gp * P:(gp + 1) * P]
                            last = nc.tensor.transpose(ps[:, 4 + k % 2, t * P:(t + 1) * P], src, ident)
                        last.then_inc(sa_kt, 1)

                    for k in range(4):
                        key_tp(k)
                    for half in range(3):
                        for k in range(4 * half + 4, min(4 * half + 6, 12)):
                            key_tp(k)
                        for n, (s, gp, rows) in enumerate(strips):
                            pe.wait_ge(sa_ke, nth(sa_ke, 12 * it + (4 * half + n + 1)))
                            nc.tensor.matmul(ps[rows, half, :], qs[:, par, gp, s, :], skT[:, n, :], start=True, stop=True).then_inc(sa_s, 1)
                        for k in range(4 * half + 6, min(4 * half + 8, 12)):
                            key_tp(k)
                        if half == 1:
                            pe.wait_ge(sa_im, it + 1)
                            nc.tensor.matmul(ps[:, 3, 256:270], C("same"), small[:, 32:46], start=True, stop=True).then_inc(sa_imp, 1)
                    if pair:
                        turn_back(pair - 1)
                    for _ in range(5):
                        nc.tensor.matmul(ps[:, 4, :], ident, skT[:, 0, :], start=True, stop=True)
                    pe.wait_ge(sa_e, 2 * it + 1)
                    pe.sem_inc(passed, 1)
                    nc.tensor.transpose(ps[0:NWS, 4, 0:P], pc[:, 0:NWS], ident)
                    nc.tensor.transpose(ps[0:NSAM, 4, P:2 * P], ssel[:, PAST:PAST + NSAM], ident).then_inc(sa_t, 1)
                    for half in range(2):
                        if half:
                            pe.wait_ge(sa_te, 5 * it + 1)
                        for t in range(4):
                            o = (4 * half + t) * P
                            last = nc.tensor.transpose(ps[:, 5 - half, t * P:(t + 1) * P], ssel[:, o:o + P], ident)
                        last.then_inc(sa_t, 1)
                    pe.wait_ge(sa_e, 2 * it + 2)
                    pe.wait_ge(sa_te, 5 * it + 2)
                    for t in range(4):
                        last = nc.tensor.transpose(ps[:, 5, t * P:(t + 1) * P], swsc[:, t * P:(t + 1) * P], ident)
                    last.then_inc(sa_t, 1)
                    pe.wait_ge(sa_te, 5 * it + 3)
                    pe.sem_inc(passed, 1)
                    nc.tensor.transpose(ps[0:NSAM, 4, 0:P], swsc[:, WIN:WIN + NSAM], ident).then_inc(sa_t, 1)
                    halves_of = [(s, slice(64 * s, 64 * s + 64)) for s in range(2)]
                    for s, rows in halves_of:
                        nc.tensor.matmul(ps[rows, 6, 0:KV], spT[0:NWS, 13, rows], vc_s[0:NWS, (2 * pair + s) * KV:(2 * pair + s + 1) * KV], start=True, stop=True)
                    for t in range(8):
                        for s, rows in halves_of:
                            nc.tensor.matmul(ps[rows, 6, KV:2 * KV], spT[:, t, rows], skv[:, par, s, t, KV:2 * KV], start=t == 0, stop=False)
                    for s, rows in halves_of:
                        nc.tensor.matmul(ps[rows, 6, KV:2 * KV], spT[0:NSAM, 12, rows], zk[0:NSAM, NT, Z_VS:Z_VS + KV], start=False, stop=True)
                    pe.wait_ge(sa_te, 5 * it + 5)
                    if pair:
                        pe.wait_ge(sa_ys, it)
                    for t in range(4):
                        for s, rows in halves_of:
                            nc.tensor.matmul(ps[rows, 7, 0:KV], spT[:, 8 + t, rows], swin[:, s, t, KV:2 * KV], start=t == 0, stop=False)
                    for s, rows in halves_of:
                        last = nc.tensor.matmul(ps[rows, 7, 0:KV], spT[0:NSAM, 14, rows], zk[0:NSAM, NT, Z_VW:Z_VW + KV], start=False, stop=True)
                    last.then_inc(sa_o, 1)
                    pe.drain().then_inc(s_fin, 1)
                turn_back(3)
                end_phase(pe, l, 8)

                leave_phase(pe)
                with pe.Fori(0, 2) as i:
                    for n in range(2):
                        pe.wait_ge(w_lo, nth(w_lo, l * NB + 2 * i + (B_ZB + n + 1)))
                        for jj in range(2):
                            pe.wait_ge(zb_done, nth(zb_done, 8 * l + 4 * i + (2 * n + jj - 3)))
                            fm_tile(n, jj, 2 * (2 * n + jj), hH, hL, parts=h_lo if n + jj == 0 else None, before=16 * l + 8).then_inc(zb, 1)
                        pe.drain().then_inc(w_done, 1)
                end_phase(pe, l, 10)
                merge(1, B_MB, (hH, hL), (aH, aL))
                end_phase(pe, l, 11)
                leave_phase(pe)
                with pe.Fori(0, 2) as i:
                    for n in range(2):
                        pe.wait_ge(w_lo, nth(w_lo, l * NB + 2 * i + (B_WO + n + 1)))
                        for jj in range(2):
                            pe.wait_ge(wo_done, nth(wo_done, 8 * l + 4 * i + (2 * n + jj - 3)))
                            fm_tile(n, jj, 2 * (2 * n + jj), aH, aL, parts=sp_lo if n + jj == 0 else None, before=16 * l).then_inc(wo, 1)
                        pe.drain().then_inc(w_done, 1)
                pe.wait_ge(p_in, 32 * l + 32)
                pe.wait_ge(wo_done, nth(wo_done, 8 * l + 8))
                for c in range(2):
                    for tt in range(5):
                        rows = P if tt < NT else NSAM
                        last = nc.tensor.transpose(ps[:, 2 * c + tt // NT, (tt % NT) * P:(tt % NT) * P + rows],
                                                   pin[0:rows, tt, c * P:(c + 1) * P], ident[0:rows, 0:rows])
                last.then_inc(p_tp, 1)
                leave_phase(pe)
                pe.wait_ge(p_lo, l + 1)
                pe.sem_inc(passed, 1)
                for i in range(2):
                    for n in range(2):
                        pe.wait_ge(w_lo, nth(w_lo, l * NB + (B_PL + 3 * i + n + 1)))
                        for jj in range(2):
                            q = 2 * n + jj
                            pe.wait_ge(pl_done, nth(pl_done, 8 * l + (4 * i + q - 3)))
                            fm_tile((i + n) % 2, jj, 2 * q, aH, aL, parts=sp_lo if i + q == 0 else None, before=16 * l + 8).then_inc(pl, 1)
                        pe.drain().then_inc(w_done, 1)
                    pe.wait_ge(w_lo, nth(w_lo, l * NB + (B_PL + 3 * i + 3)))
                    for q in range(4):
                        pe.wait_ge(pl_sg, 8 * l + (4 * i + q + 1))
                        for k in range(2):
                            for w, x in ((wH, pH), (wH, pL), (wL, pH)):
                                for hf in range(2):
                                    last = nc.tensor.matmul(ps[:, 2 * q + hf, 0:HALF], wide(w, i)[:, k, q * P:(q + 1) * P],
                                                            x[:, k, hf * HALF:(hf + 1) * HALF],
                                                            start=k == 0 and w is wH and x is pH, stop=k == 1 and w is wL)
                        last.then_inc(pl, 1)
                    pe.drain().then_inc(w_done, 1)
                end_phase(pe, l, 14)

            norm_sum(NL)
            for tt in range(5):
                rows = P if tt < NT else NSAM
                pe.wait_ge(y_ready, 1)
                pe.wait_ge(y_act, nth(y_act, tt - 3))
                pe.wait_ge(y_dve, nth(y_dve, tt - 3))
                for c in range(KT):
                    last = nc.tensor.transpose(ps[0:rows, 2 * (tt % 4) + c // 4, (c % 4) * P:(c % 4 + 1) * P],
                                               xT[:, c, tt * P:tt * P + rows], ident)
                last.then_inc(y_tp, 1)

        @block.scalar
        def _(act):
            def norm_std(l):
                for c in range(KT):
                    act.wait_ge(sq_used, nth(sq_used, l * KT + (c - 1)))
                    act.activation(sq[:, c % 2, :], xT[:, c, :], ACT.Square).then_inc(sq_ready, 1)
                act.wait_ge(ss_ready, l + 1)
                act.activation(halves(rstd[:]), bank2(0), ACT.Sqrt, bias=C("eps"), scale=1.0 / D).then_inc(std_ready, 1)

            def split_h(n):
                for c in range(KT):
                    act.wait_ge(h_f, KT * n + (c + 1))
                    act.activation(hH[:, c, :], t_f[:, c % 2, :], ACT.Copy).then_inc(h_hi, 1)

            def split(n, src):
                for c in range(KT):
                    act.activation(aH[:, c, :], src[:, c, :], ACT.Copy).then_inc(sp_hi, 1)

            act.wait_ge(s_const, 16)
            act.wait_ge(s_zero, 1)
            act.activation(mask2[:, 0, :], ident, ACT.Copy)
            act.activation(mask2[:, 1, :], C("causal"), ACT.Copy)
            for c in range(KT):
                act.wait_ge(x_tp, c + 1)
                act.activation(xT[:, c, 0:SEQ], ps[:, 2 * (c % 4), :], ACT.Copy)
                act.activation(xT[:, c, SEQ:TOK], ps[:, 2 * (c % 4) + 1, 0:NSAM], ACT.Copy).then_inc(x_free, 1)
            end_phase(act, 0, -1)

            with act.Fori(0, NL) as l:
                make_high(act, l, pb(B_CONV, 0, 0), 0)
                norm_std(l)
                split_h(2 * l)
                end_phase(act, l, 0)
                with act.Fori(0, 4) as i:
                    n = 4 * l + i
                    for kind in range(4):
                        make_high(act, l, pb(B_CONV, 2 * i + (kind + 1) // 2, (kind + 1) % 2), (kind + 1) % 2)
                        for jj in range(2):
                            act.wait_ge(cv, 8 * n + (2 * kind + jj + 1))
                            bank = bank2(2 * ((2 * kind + jj) % 4))
                            if kind == 0:
                                act.wait_ge(cv_used, nth(cv_used, 2 * n + (jj - 1)))
                            if kind < 3:
                                act.activation(halves(cv_in[:, kind, jj, :]), bank, ACT.Copy).then_inc(cv_act, 1)
                            else:
                                act.activation(halves(cv_in[:, 3, jj, :]), bank, ACT.Sigmoid).then_inc(cv_sg, 1)
                        if kind == 3:
                            for jj in range(2):
                                act.wait_ge(cv_f, 2 * n + (jj + 1))
                                act.activation(one(aH, 2 * i + jj), cv_in[:, 1, jj, :], ACT.Copy).then_inc(cv_hi, 1)
                end_phase(act, l, 1)

                def gates(which, first_block):
                    with act.Fori(0, 4) as i:
                        for n in range(2):
                            make_high(act, l, pb(first_block, i + (n + 1) // 2, (n + 1) % 2), (n + 1) % 2)
                            if n == 0:
                                for jj in range(2):
                                    act.wait_ge(mg, 32 * l + 4 * i + (16 * which + jj + 1))
                                    act.wait_ge(mg_dve, nth(mg_dve, 16 * l + 2 * i + (8 * which + jj - 1)))
                                    act.activation(halves(t_f[:, jj, :]), bank2(2 * jj), ACT.Sigmoid).then_inc(mg_sg, 1)

                gates(0, B_MA)
                end_phase(act, l, 2)
                act.wait_ge(tail_tp, l + 1)
                act.activation(tail_rows[:, 0:SEQ], ps[0:18, 6, :], ACT.Copy).then_inc(tail_cp, 1)
                act.activation(tail_rows[:, SEQ:D], ps[0:18, 7, :], ACT.Copy).then_inc(tail_cp, 1)

                def copy_out(b, half, n, dst, width):
                    col = 2 * width * half + n * width
                    for tt in range(5):
                        rows = P if tt < NT else NSAM
                        act.wait_ge(tm, l * (5 * TM_BLOCKS) + 10 * half + (5 * (b + n) + tt + 1))
                        if dst is zq:
                            out = zq[0:rows, tt, ds(2 * BW * half, 2 * BW)].rearrange("p (r g d) -> p g r d", g=2, d=HD)[:, n]
                            src = ps[0:rows, tt, 0:BW].rearrange("p (r d) -> p r d", d=HD)
                        else:
                            out, src = dst[0:rows, tt, ds(col, width)], ps[0:rows, tt, 0:width]
                        act.activation(out, src, ACT.Copy).then_inc(tm_ev, 1)

                with act.Fori(0, NQB // 2) as i:
                    for n in range(2):
                        make_high(act, l, pb(B_TM, i + (n + 1) // 2, (n + 1) % 2), (n + 1) % 2, width=(BW, WW)[n])
                        copy_out(0, i, n, zq, BW)
                with act.Fori(0, NKB // 2 - 1) as i:
                    for n in range(2):
                        make_high(act, l, pb(B_TM + NQB, i + (n + 1) // 2, (n + 1) % 2), (n + 1) % 2, width=WW)
                        copy_out(NQB, i, n, zk, WW)
                make_high(act, l, pb(B_TM + NQB, NKB // 2 - 1, 1), 1, width=WW)
                for n in range(2):
                    copy_out(NQB, NKB // 2 - 1, n, zk, WW)
                act.drain()
                act.activation(zk[:, 0:NT, Z_G:Z_G + 48], zk[:, 0:NT, Z_G:Z_G + 48], ACT.Sigmoid)
                act.activation(zk[0:NSAM, NT, Z_G:Z_G + 48], zk[0:NSAM, NT, Z_G:Z_G + 48], ACT.Sigmoid)
                act.wait_ge(tail_out, 32 * l + 32)
                act.sem_inc(passed, 1)
                end_phase(act, l, 3)

                def w1_high(kv, j):
                    act.wait_ge(w1_in, 32 * l + (16 * kv + 16))
                    if kv:
                        act.wait_ge(c_mm, nth(c_mm, 40 * l + (17 + j)))
                    act.activation(w1H[:, j:16:4, :], w1_raw[:, j:16:4, :], ACT.Copy).then_inc(w1_hi, 1)

                def chunks_high(n, j):
                    unit = 10 * l + n
                    rows, nseq, _ = unit_shape(n)
                    act.wait_ge(c_mm, nth(c_mm, 4 * unit + (j - 1)))
                    for s in range(nseq):
                        m = 8 * n + 2 * j + s
                        act.wait_ge(c_tp, 80 * l + (m + 1))
                        for t in range(2):
                            for g in range(2):
                                src = ps[64 * g:64 * g + 64, m % 3, 2 * t * P:2 * (t + 1) * P].rearrange("p (a h) -> p h a", a=2)[:, 0:rows, :]
                                dst = chH[64 * t:64 * t + 64, j % 2, s, 0:rows, g:GROUPS:2]
                                last = act.activation(dst, src, ACT.Copy)
                        last.then_inc(c_hi, 1)
                    if nseq == 1:
                        act.drain().then_inc(c_hi, 1)

                def hidden_gate(n):
                    unit = 10 * l + n
                    cols = NWP * GROUPS if n % 5 == 0 else 2 * NWS * GROUPS
                    act.wait_ge(c_acc, unit + 1)
                    act.wait_ge(c_hid, nth(c_hid, 2 * unit))
                    if n % 5 == 0:
                        act.wait_ge(pos_ready, 2 * l + (n // 5 + 1))
                    for hid in range(2):
                        act.activation(hsg[:, hid, 0:cols], ps[:, 4 + 2 * (n % 2) + hid, 0:cols], ACT.Sigmoid, bias=hb[:, hid:hid + 1]).then_inc(c_sg, 1)

                for j in range(4):
                    w1_high(0, j)
                chunks_high(0, 0)
                chunks_high(0, 1)
                for n in range(10):
                    chunks_high(n, 2)
                    chunks_high(n, 3)
                    if n == 4:
                        w1_high(1, 0)
                        w1_high(1, 1)
                    for j in range(2):
                        if n < 9:
                            chunks_high(n + 1, j)
                        if n == 4:
                            w1_high(1, 2 + j)
                    hidden_gate(n)
                end_phase(act, l, 4)
                end_phase(act, l, 5)

                for k in range(0, 14, 2):
                    act.wait_ge(tp[0], 7 * l + (k // 2 + 1))
                    if k < 8:
                        act.activation(qT[:, k, :], ps[:, k % 8, :], ACT.Copy, scale=SCALE).then_inc(tp_free[0], 1)
                    elif k < 12:
                        act.activation(kT[:, (k - 8) // 2, 0, :], ps[:, k % 8, :], ACT.Copy).then_inc(tp_free[0], 1)
                    else:
                        act.activation(qsT[:].rearrange("p k t -> p (k t)"), ps[:, 4, 0:KT * NSAM], ACT.Copy).then_inc(tp_free[0], 1)
                end_phase(act, l, 6)

                def exps(unit, k):
                    b, g, u = k % 2, k % 2, k % 8 // 2
                    n = P * (u + 1)
                    for br in range(2):
                        o = 8 + u * 4 + g * 2 + br
                        act.activation(pr[:, b, br, 0:n], ps[:, 2 * b + br, 0:n], ACT.Exp, bias=small[:, 2 * b + br:2 * b + br + 1],
                                       accum_out=small[:, o:o + 1]).then_inc(pa_exp, 1)

                for b in (0, 2):
                    act.wait_ge(pa_cm, 4 * l + (b + 1))
                    act.activation(cx[:, b, :], ps[:, b, :], ACT.Copy).then_inc(pa_cx[0], 1)
                act.wait_ge(pa_csub, l + 1)
                act.activation(cs[:], cs[:], ACT.Exp).then_inc(pa_cexp, 1)
                act.wait_ge(pa_nm, 66 * l + 1)
                exps(64 * l, 0)
                for b in (0, 2):
                    act.wait_ge(pa_ct, 4 * l + (b + 1))
                    act.activation(ct_bank(b), ps[:, 4 + b, :], ACT.Copy).then_inc(pa_ctev[0], 1)
                with act.Fori(0, REP) as r:
                    for gp in range(2):
                        unit = 64 * l + 16 * r + 8 * gp
                        for k in range(8):
                            u = k // 2
                            act.wait_ge(pa_nm, 66 * l + 16 * r + (8 * gp + k + 2))
                            act.wait_ge(pa_t, nth(pa_t, 2 * unit + 2 * k))
                            if k % 2 == 1:
                                act.wait_ge(pa_o, nth(pa_o, 32 * l + 8 * r + (4 * gp + u - 2)))
                            exps(unit, k + 1)
                            for br in range(2):
                                act.wait_ge(pa_t, nth(pa_t, 2 * unit + (2 * k + br + 1)))
                                act.wait_ge(pa_pv, nth(pa_pv, unit + (k - 1)))
                                act.activation(prT[:, k % 2, br, 0:P * (u + 1)], ps[:, 4 + br, 0:P * (u + 1)], ACT.Copy).then_inc(pa_te, 1)
                            if k % 2 == 0:
                                v = (k - 4) // 2
                                act.wait_ge(pa_yt, nth(pa_yt, 34 * l + 8 * r + (4 * gp + v + 3)))
                                flat = yT[:].rearrange("p k t -> p (k t)")
                                if v >= 0:
                                    out = flat[:, ds(TOK * r + (4 * gp * TOK + v * P), P)]
                                elif gp == 1:
                                    out = flat[:, ds(TOK * r + (v + 4) * P, P)]
                                else:
                                    out = flat[:, ds(TOK * r + (3 * TOK + (v + 4) * P), P)]
                                act.activation(out, ps[:, 6 + v % 2, 384:512], ACT.Copy).then_inc(pa_yo, 1)
                for n in range(2):
                    act.wait_ge(pa_yt, nth(pa_yt, 34 * l + (33 + n)))
                    act.activation(yT[:, KT - 1, (2 + n) * P:(3 + n) * P], ps[:, 6 + n, 384:512], ACT.Copy).then_inc(pa_yo, 1)
                end_phase(act, l, 7)

                for pair in range(4):
                    it = 4 * l + pair
                    act.wait_ge(sa_nm, it + 1)
                    act.activation(pc[:, 0:NWS], ps[:, 3, 0:NWS], ACT.Exp, bias=small[:, 64:65], scale=SCALE,
                                   accum_out=small[:, 65:66])
                    act.drain().then_inc(sa_cx, 1)
                    for k in range(12):
                        act.wait_ge(sa_kt, 12 * it + (k + 1))
                        act.wait_ge(sa_s, nth(sa_s, 12 * it + (k - 3)))
                        act.activation(skT[:, k % 4, :], ps[:, 4 + k % 2, :], ACT.Copy).then_inc(sa_ke, 1)
                    act.wait_ge(sa_m, 2 * it + 1)
                    act.activation(ssel[:], ssel[:], ACT.Exp, bias=small[:, 68:69], scale=SCALE, accum_out=small[:, 70:71])
                    act.drain().then_inc(sa_e, 1)
                    for n, (bank, rows, c0, c1, slot) in enumerate(((4, NWS, 0, P, 13), (5, P, 0, 4 * P, 0), (4, P, 0, 4 * P, 4),
                                                                    (5, P, 0, 4 * P, 8), (4, NSAM, 0, P, 14))):
                        if n == 3:
                            act.wait_ge(sa_m, 2 * it + 2)
                            act.activation(swsc[:], swsc[:], ACT.Exp, bias=small[:, 69:70], scale=SCALE, accum_out=small[:, 71:72])
                            act.drain().then_inc(sa_e, 1)
                        act.wait_ge(sa_t, 5 * it + (n + 1))
                        if n == 0:
                            act.activation(spT[0:NSAM, 12, :], ps[0:NSAM, 4, P:2 * P], ACT.Copy)
                        act.activation(spT[0:rows, slot:slot + (c1 - c0) // P, :].rearrange("p a b -> p (a b)"),
                                       ps[0:rows, bank, c0:c1], ACT.Copy).then_inc(sa_te, 1)
                act.wait_ge(s_winout, 256 * l + 256)
                act.sem_inc(passed, 1)
                end_phase(act, l, 8)

                split_h(2 * l + 1)
                make_high(act, l, pb(B_ZB, 0, 0), 0)
                end_phase(act, l, 9)
                with act.Fori(0, 2) as i:
                    for n in range(2):
                        make_high(act, l, pb(B_ZB, i + (n + 1) // 2, (n + 1) % 2), (n + 1) % 2)
                        for jj in range(2):
                            q = 8 * l + 4 * i + (2 * n + jj)
                            act.wait_ge(zb, q + 1)
                            act.wait_ge(zb_done, nth(zb_done, q - 1))
                            act.activation(halves(t_f[:, jj, :]), bank2(2 * (2 * n + jj)), ACT.Sigmoid).then_inc(zb_sg, 1)
                        for jj in range(2):
                            q = 8 * l + 4 * i + (2 * n + jj)
                            act.wait_ge(zb_f, q + 1)
                            act.activation(one(aH, 4 * i + (2 * n + jj)), t_f[:, jj, :], ACT.Copy).then_inc(zb_hi, 1)
                end_phase(act, l, 10)
                gates(1, B_MB)
                end_phase(act, l, 11)
                split(2 * l, m)
                end_phase(act, l, 12)
                with act.Fori(0, 2) as i:
                    for n in range(2):
                        make_high(act, l, pb(B_WO, i + (n + 1) // 2, (n + 1) % 2), (n + 1) % 2)
                act.wait_ge(wo_done, nth(wo_done, 8 * l + 8))
                act.wait_ge(p_tp, l + 1)
                for c in range(2):
                    act.activation(pH[:, c, 0:SEQ], ps[:, 2 * c, :], ACT.Copy)
                    act.activation(pH[:, c, SEQ:TOK], ps[:, 2 * c + 1, 0:NSAM], ACT.Copy).then_inc(p_hi, 1)
                split(2 * l + 1, xT)
                end_phase(act, l, 13)

                def prep_ple(m):
                    if m % 3 == 2:
                        make_high(act, l, B_PL + m, m % 2, wide_block=True)
                    else:
                        make_high(act, l, B_PL + m, m % 2)

                for i in range(2):
                    for n in range(2):
                        prep_ple(3 * i + n + 1)
                        for jj in range(2):
                            q = 2 * n + jj
                            act.wait_ge(pl, 16 * l + (8 * i + q + 1))
                            act.wait_ge(pl_done, nth(pl_done, 8 * l + (4 * i + q - 3)))
                            act.activation(halves(t_f[:, q, :]), bank2(2 * q), ACT.Sigmoid).then_inc(pl_sg, 1)
                    if i == 0:
                        prep_ple(3)
                end_phase(act, l, 14)

            norm_std(NL)
            for tt in range(5):
                rows = P if tt < NT else NSAM
                act.wait_ge(y_tp, tt + 1)
                act.activation(out_rows[0:rows, tt, 0:SEQ], ps[0:rows, 2 * (tt % 4), :], ACT.Copy).then_inc(y_act, 1)

        @block.vector
        def _(dve):
            def norm_add(l):
                for c in range(KT):
                    dve.wait_ge(sq_ready, l * KT + (c + 1))
                    if c == 0:
                        dve.tensor_copy(ssq[:], sq[:, 0, :]).then_inc(sq_used, 1)
                    else:
                        dve.tensor_tensor(ssq[:], ssq[:], sq[:, c % 2, :], ALU.add).then_inc(sq_used, 1)
                    dve.drain()
                dve.drain().then_inc(sq_sum, 1)

            def norm_recip(l):
                dve.wait_ge(std_ready, l + 1)
                dve.reciprocal(rstd[:], rstd[:])
                dve.drain()

            def make_h(n):
                def low(c):
                    dve.wait_ge(h_hi, KT * n + (c + 1))
                    dve.tensor_tensor(hL[:, c, :], t_f[:, c % 2, :], hH[:, c, :].bitcast(F32), ALU.subtract).then_inc(h_lo, 1)

                for c in range(KT):
                    if c >= 2:
                        low(c - 2)
                        dve.drain()
                    dve.scalar_tensor_tensor(out=t_f[:, c % 2, :], in0=xT[:, c, :], scalar=cols[:, c, 19:20], in1=rstd[:],
                                             op0=ALU.mult, op1=ALU.mult).then_inc(h_f, 1)
                low(KT - 2)
                low(KT - 1)

            def split(n, src):
                for c in range(KT):
                    dve.wait_ge(sp_hi, KT * n + (c + 1))
                    dve.tensor_tensor(aL[:, c, :], src[:, c, :], aH[:, c, :].bitcast(F32), ALU.subtract).then_inc(sp_lo, 1)

            end_phase(dve, 0, -1)
            with dve.Fori(0, NL) as l:
                dve.wait_ge(st_tp, l + 1)
                dve.tensor_copy(cols[:].rearrange("p k n -> p (k n)"), ps[:, 2, 0:21 * KT])
                make_low(dve, l, pb(B_CONV, 0, 0), 0)
                norm_add(l)
                norm_recip(l)
                make_h(2 * l)
                dve.drain()
                dve.memset(cv_u[:, :, 0:2], 0.0)
                dve.drain()
                end_phase(dve, l, 0)
                with dve.Fori(0, 4) as i:
                    n = 4 * l + i
                    for kind in range(4):
                        make_low(dve, l, pb(B_CONV, 2 * i + (kind + 1) // 2, (kind + 1) % 2), (kind + 1) % 2)
                        if kind == 0:
                            for jj in range(2):
                                dve.tensor_copy(cst[:, jj, :], cols[:].rearrange("p k n -> p (k n)")[:, ds(42 * i + 21 * jj, 21)])
                            dve.drain()
                        for jj in range(2):
                            if kind == 1:
                                dve.wait_ge(cv_act, nth(cv_act, 6 * n + (3 + jj)))
                                u = cv_u[:, jj, :]
                                us = u[:, SEQ + 2:UW].rearrange("p (b t) -> p b t", t=6)
                                ca, xa = cv_in[:, 0, jj, :], cv_in[:, 1, jj, :]
                                dve.tensor_tensor(u[:, 2:SEQ + 2], ca[:, 0:SEQ], xa[:, 0:SEQ], ALU.mult)
                                dve.tensor_tensor(us[:, :, 2:6], ca[:, SEQ:TOK].rearrange("p (b t) -> p b t", t=TS),
                                                  xa[:, SEQ:TOK].rearrange("p (b t) -> p b t", t=TS), ALU.mult)
                                dve.tensor_copy(us[:, :, 0:2], cst[:, jj, 0:16].rearrange("p (b t) -> p b t", t=2))
                                dve.drain()
                                tl = tails[:].rearrange("p k n -> p (k n)")
                                dve.tensor_copy(tl[:, ds(36 * i + 18 * jj, 2)], u[:, SEQ:SEQ + 2])
                                dve.tensor_copy(tl[:, ds(36 * i + (18 * jj + 2), 16)].rearrange("p (b t) -> p b t", t=2), us[:, :, 4:6])
                            elif kind == 2:
                                dve.wait_ge(cv_act, nth(cv_act, 6 * n + (5 + jj)))
                                w = UW - 2
                                dve.tensor_scalar(cv_y[:, 0:w], cv_u[:, jj, 0:w], cst[:, jj, 16:17], None, ALU.mult)
                                for tap in (1, 2):
                                    dve.drain()
                                    dve.scalar_tensor_tensor(out=cv_y[:, 0:w], in0=cv_u[:, jj, tap:tap + w], scalar=cst[:, jj, 16 + tap:17 + tap],
                                                             in1=cv_y[:, 0:w], op0=ALU.mult, op1=ALU.add)
                                dve.drain()
                                ba = cv_in[:, 2, jj, :]
                                ys = cv_y[:, SEQ + 2:UW].rearrange("p (b t) -> p b t", t=6)[:, :, 0:TS]
                                bs = ba[:, SEQ:TOK].rearrange("p (b t) -> p b t", t=TS)
                                dve.tensor_tensor(ba[:, 0:SEQ], ba[:, 0:SEQ], cv_y[:, 0:SEQ], ALU.mult)
                                dve.tensor_tensor(bs, bs, ys, ALU.mult)
                                dve.drain()
                            elif kind == 3:
                                dve.wait_ge(cv_sg, 2 * n + (jj + 1))
                                dve.tensor_tensor(halves(cv_in[:, 0, jj, :]), bank2(4 + 2 * jj), halves(cv_in[:, 3, jj, :]), ALU.mult).then_inc(cv_dve, 1)
                                dve.drain()
                                dve.tensor_tensor(cv_in[:, 1, jj, :], cv_in[:, 0, jj, :], cv_in[:, 2, jj, :], ALU.mult).then_inc(cv_f, 1)
                        if kind == 3:
                            dve.drain()
                            for jj in range(2):
                                dve.wait_ge(cv_hi, 2 * n + (jj + 1))
                                dve.tensor_tensor(one(aL, 2 * i + jj), cv_in[:, 1, jj, :], one(aH, 2 * i + jj).bitcast(F32), ALU.subtract
                                                  ).then_inc(cv_used, 1)
                end_phase(dve, l, 1)

                def products(which, first_block):
                    with dve.Fori(0, 4) as i:
                        for n in range(2):
                            make_low(dve, l, pb(first_block, i + (n + 1) // 2, (n + 1) % 2), (n + 1) % 2)
                            if n == 1:
                                for jj in range(2):
                                    dve.wait_ge(mg_sg, 16 * l + 2 * i + (8 * which + jj + 1))
                                    dve.wait_ge(mg, 32 * l + 4 * i + (16 * which + 2 + jj + 1))
                                    if which == 0:
                                        dve.tensor_tensor(two(m, 2 * i + jj), bank2(4 + 2 * jj), halves(t_f[:, jj, :]), ALU.mult).then_inc(mg_dve, 1)
                                    else:
                                        dve.tensor_tensor(halves(t_f[:, jj, :]), bank2(4 + 2 * jj), halves(t_f[:, jj, :]), ALU.mult)
                                        dve.drain()
                                        dve.tensor_tensor(one(m, 2 * i + jj), one(m, 2 * i + jj), t_f[:, jj, :], ALU.add).then_inc(mg_dve, 1)

                products(0, B_MA)
                end_phase(dve, l, 2)

                def rope(z, rows, tts, c0, heads):
                    nt = tts[1] - tts[0]
                    v = z[0:rows, tts[0]:tts[1], ds(c0, heads * HD)].rearrange("p t (h c) -> p t h c", c=HD)
                    x1, x2 = v[:, :, :, 0:32], v[:, :, :, 32:64]
                    tab = [C(n, rows).rearrange("p (t c) -> p t c", c=32)[:, tts[0]:tts[1], :].unsqueeze(2).to_broadcast([rows, nt, heads, 32])
                           for n in ("cos", "sin")]
                    ta, tb = (rope_a[0:rows, k, 0:nt * heads * 32].rearrange("p (t h c) -> p t h c", t=nt, h=heads) for k in range(2))
                    dve.tensor_tensor(ta, x2, tab[1], ALU.mult)
                    dve.tensor_tensor(tb, x1, tab[1], ALU.mult)
                    dve.drain()
                    dve.tensor_tensor(x1, x1, tab[0], ALU.mult)
                    dve.tensor_tensor(x2, x2, tab[0], ALU.mult)
                    dve.drain()
                    dve.tensor_tensor(x1, x1, ta, ALU.subtract)
                    dve.tensor_tensor(x2, x2, tb, ALU.add)
                    dve.drain()

                def rope_all(z, c0, heads, blocks):
                    dve.wait_ge(tm_ev, nth(tm_ev, l * (5 * TM_BLOCKS) + 5 * blocks))
                    for tt in range(NT):
                        rope(z, P, (tt, tt + 1), c0, heads)
                    rope(z, NSAM, (NT, NT + 1), c0, heads)

                with dve.Fori(0, NQB // 2) as i:
                    for n in range(2):
                        make_low(dve, l, pb(B_TM, i + (n + 1) // 2, (n + 1) % 2), (n + 1) % 2, width=(BW, WW)[n])
                    rope_all(zq, 512 * i, 8, 2 * i + 2)
                with dve.Fori(0, NKB // 2 - 1) as i:
                    for n in range(2):
                        make_low(dve, l, pb(B_TM + NQB, i + (n + 1) // 2, (n + 1) % 2), (n + 1) % 2, width=WW)
                    rope_all(zk, 512 * i, 4, 2 * i + (NQB + 2))
                make_low(dve, l, pb(B_TM + NQB, NKB // 2 - 1, 1), 1, width=WW)
                rope_all(zk, Z_KW, 4, TM_BLOCKS - 1)
                dve.wait_ge(tm_ev, nth(tm_ev, l * (5 * TM_BLOCKS) + 5 * TM_BLOCKS))
                dve.sem_inc(passed, 1)
                dve.drain().then_inc(z_ready, 1)
                end_phase(dve, l, 3)

                def w1_low(kv, j):
                    dve.wait_ge(w1_hi, 8 * l + (4 * kv + j + 1))
                    dve.tensor_tensor(w1L[:, j:16:4, :], w1_raw[:, j:16:4, :], w1H[:, j:16:4, :].bitcast(F32), ALU.subtract).then_inc(w1_lo, 1)

                def chunks_low(n, j):
                    rows, nseq, _ = unit_shape(n)
                    for s in range(nseq):
                        m = 8 * n + 2 * j + s
                        dve.wait_ge(c_hi, 80 * l + (m + 1))
                        for t in range(2):
                            for g in range(2):
                                src = ps[64 * g:64 * g + 64, m % 3, 2 * t * P:2 * (t + 1) * P].rearrange("p (a h) -> p h a", a=2)[:, 0:rows, :]
                                to = (slice(64 * t, 64 * t + 64), j % 2, s, slice(0, rows), slice(g, GROUPS, 2))
                                last = dve.tensor_tensor(chL[to], src, chH[to].bitcast(F32), ALU.subtract)
                        last.then_inc(c_lo, 1)
                    if nseq == 1:
                        dve.drain().then_inc(c_lo, 1)

                def hidden(n):
                    unit = 10 * l + n
                    cols = NWP * GROUPS if n % 5 == 0 else 2 * NWS * GROUPS
                    bank = 4 + 2 * (n % 2)
                    if n % 5 == 0:
                        dve.wait_ge(c_acc, unit + 1)
                        for hid in range(2):
                            dve.tensor_copy(hb[:, hid:hid + 1], ps[:, bank + hid, (NWP + 1) * GROUPS:(NWP + 1) * GROUPS + 1])
                        dve.drain().then_inc(pos_ready, 1)
                    dve.wait_ge(c_w2, nth(c_w2, unit))
                    for hid in range(2):
                        dve.wait_ge(c_sg, 2 * unit + (hid + 1))
                        dve.scalar_tensor_tensor(out=hidT[:, hid, 0:cols], in0=ps[:, bank + hid, 0:cols], scalar=hb[:, hid:hid + 1],
                                                 in1=hsg[:, hid, 0:cols], op0=ALU.add, op1=ALU.mult).then_inc(c_hid, 1)

                def compressed_out(n):
                    dve.wait_ge(c_w2, nth(c_w2, 10 * l + n + 1))
                    first = 2 * (n % 5) - 2
                    if n == 0:
                        src = ps[0:HD, 3, 0:NWP * GROUPS].rearrange("p (n a g) -> p g a n", a=2, g=2)
                        for g in range(2):
                            dve.tensor_copy(kcT_p[64 * g:64 * g + 64, :, 0:NWP], src[:, g])
                    elif n < 5:
                        for s in range(2):
                            src = ps[0:HD, 3, s * NWS * GROUPS:(s + 1) * NWS * GROUPS].rearrange("p (n a g) -> p g a n", a=2, g=2)
                            for g in range(2):
                                dve.tensor_copy(kcT_s[64 * g:64 * g + 64, :, first + s, 0:NWS], src[:, g])
                    elif n == 5:
                        for q in range(4):
                            dve.tensor_copy(vc_p[32 * q:32 * q + NWP, :], ps[0:NWP, 3, 0:KV])
                    else:
                        dve.tensor_copy(vc_s[0:NWS, first * KV:(first + 2) * KV], ps[0:NWS, 3, :])
                    dve.drain().then_inc(c_out, 1)

                for j in range(4):
                    w1_low(0, j)
                chunks_low(0, 0)
                chunks_low(0, 1)
                for n in range(10):
                    chunks_low(n, 2)
                    if n:
                        compressed_out(n - 1)
                    chunks_low(n, 3)
                    if n == 4:
                        w1_low(1, 0)
                        w1_low(1, 1)
                    for j in range(2):
                        if n < 9:
                            chunks_low(n + 1, j)
                        if n == 4:
                            w1_low(1, 2 + j)
                    hidden(n)
                compressed_out(9)
                end_phase(dve, l, 4)
                end_phase(dve, l, 5)

                for k in range(1, 14, 2):
                    dve.wait_ge(tp[1], 7 * l + (k // 2 + 1))
                    if k < 8:
                        dve.tensor_scalar(qT[:, k, :], ps[:, k % 8, :], SCALE, None, ALU.mult).then_inc(tp_free[1], 1)
                    elif k < 12:
                        dve.tensor_copy(kT[:, (k - 8) // 2, 1, :], ps[:, k % 8, :]).then_inc(tp_free[1], 1)
                    else:
                        dve.tensor_copy(knT[:].rearrange("p k t -> p (k t)"), ps[:, 5, 0:4 * NSAM]).then_inc(tp_free[1], 1)
                end_phase(dve, l, 6)

                def maxima(unit, k):
                    b, n = k % 2, P * (k % 8 // 2 + 1)
                    dve.wait_ge(pa_s, unit + (k + 1))
                    dve.tensor_reduce(out=small[:, 2 * b:2 * b + 2], in_=ps[:, 2 * b:2 * b + 2, 0:n], op=ALU.max, axis=AX.X, negate=True
                                      ).then_inc(pa_nm, 1)

                dve.memset(yy[:], 0.0)
                for b in (1, 3):
                    dve.wait_ge(pa_cm, 4 * l + (b + 1))
                    dve.tensor_copy(cx[:, b, :], ps[:, b, :]).then_inc(pa_cx[1], 1)
                for b in range(4):
                    dve.wait_ge(pa_c, 4 * l + (b + 1))
                    dve.tensor_tensor(cs[:, 16 * b:16 * b + 16, :].rearrange("p (c u) n -> p c u n", u=NT),
                                      ps[:, 4 + b, :].rearrange("p (u c n) -> p c u n", u=NT, n=32),
                                      C("cmask").rearrange("p (u n) -> p u n", u=NT).unsqueeze(1).to_broadcast([P, 4, NT, 32]), ALU.add)
                dve.drain()
                dve.tensor_reduce(out=cmx[:], in_=cs[:], op=ALU.max, axis=AX.X)
                dve.drain()
                dve.tensor_scalar(cmx[:], cmx[:], LOWEST, None, ALU.max)
                dve.drain()
                dve.tensor_tensor(cs[:], cs[:], cmx[:].unsqueeze(2).to_broadcast([P, 2 * KT * NT, 32]), ALU.subtract).then_inc(pa_csub, 1)
                maxima(66 * l, 0)
                maxima(66 * l, 1)
                dve.wait_ge(pa_cexp, l + 1)
                dve.tensor_reduce(out=cmx[:], in_=cs[:], op=ALU.add, axis=AX.X)
                dve.drain()
                dve.tensor_scalar(cmx[:], cmx[:], 1e-30, None, ALU.max)
                dve.drain()
                dve.reciprocal(cmx[:], cmx[:])
                dve.drain()
                dve.tensor_tensor(cs[:], cs[:], cmx[:].unsqueeze(2).to_broadcast([P, 2 * KT * NT, 32]), ALU.mult).then_inc(pa_cn, 1)
                for b in (1, 3):
                    dve.wait_ge(pa_ct, 4 * l + (b + 1))
                    dve.tensor_copy(ct_bank(b), ps[:, 4 + b, :]).then_inc(pa_ctev[1], 1)
                def combine(gp, r, u):
                    dve.wait_ge(pa_pv, nth(pa_pv, 64 * l + 16 * r + (8 * gp + 2 * u + 2)))
                    sums = small[:, 8 + 4 * u:12 + 4 * u]
                    wts = small[:, 48:54].rearrange("p (g b) -> p g b", g=2)
                    inv = small[:, 24:30].rearrange("p (g b) -> p g b", g=2)
                    dve.tensor_scalar(sums, sums, 1e-30, None, ALU.max)
                    dve.drain()
                    dve.reciprocal(inv[:, :, 1:3], sums.rearrange("p (g b) -> p g b", g=2))
                    dve.drain()
                    gt = zk[:, u, Z_G + 24 * gp:Z_G + 24 * gp + 24].rearrange("p (g c) -> p g c", g=2)[:, :, ds(3 * r, 3)]
                    dve.tensor_tensor(wts, gt, inv, ALU.mult)
                    dve.drain()
                    dve.tensor_tensor(ow[:], ps[:, 6 + u % 2, 0:6 * HD].rearrange("p (k d) -> p k d", d=HD),
                                      small[:, 48:54].unsqueeze(2).to_broadcast([P, 6, HD]), ALU.mult).then_inc(pa_o, 1)
                    dve.drain()
                    dve.wait_ge(pa_yt, nth(pa_yt, 34 * l + 8 * r + (4 * gp + u + 1)))
                    dve.tensor_reduce(out=yy[:, u % 2, :].rearrange("p (g d) -> p g d", g=2),
                                      in_=ow[:].rearrange("p (g b) d -> p g d b", g=2), op=ALU.add, axis=AX.X).then_inc(pa_y, 1)

                with dve.Fori(0, REP) as r:
                    for gp in range(2):
                        for k in range(8):
                            maxima(66 * l + 16 * r + 8 * gp, k + 2)
                            if k in (2, 4, 6):
                                combine(gp, r, k // 2 - 1)
                        combine(gp, r, NT - 1)
                end_phase(dve, l, 7)

                dve.memset(pc[:, 63:64], 0.0)
                dve.wait_ge(sa_g, l + 1)
                g3 = ssel[:, 0:192].rearrange("p (a c) -> p a c", a=4)
                dve.tensor_tensor(g3, ps[:, 7, 0:192].rearrange("p (a c) -> p a c", a=4), C("gmask").unsqueeze(1).to_broadcast([P, 4, 48]), ALU.mult)
                dve.drain()
                dve.tensor_reduce(out=grow[:], in_=ssel[:, 0:192].rearrange("p (a k b) -> p a b k", a=4, b=3), op=ALU.add, axis=AX.X)
                dve.drain().then_inc(sa_gr, 1)
                def combine_pair(pair):
                    dve.wait_ge(sa_o, 4 * l + (pair + 1))
                    dve.tensor_scalar(small[:, 70:72], small[:, 70:72], 1e-30, None, ALU.max)
                    dve.drain()
                    dve.reciprocal(small[:, 77:79], small[:, 70:72])
                    dve.drain()
                    dve.tensor_tensor(small[:, 72:75], grow[:, pair, :], small[:, 76:79], ALU.mult)
                    dve.drain()
                    dve.wait_ge(sa_yt, nth(sa_yt, 4 * l + pair))
                    dve.tensor_scalar(sy[:], ps[:, 6, 0:KV], small[:, 72:73], None, ALU.mult)
                    dve.drain()
                    dve.scalar_tensor_tensor(out=sy[:], in0=ps[:, 6, KV:2 * KV], scalar=small[:, 73:74], in1=sy[:], op0=ALU.mult, op1=ALU.add)
                    dve.drain()
                    dve.scalar_tensor_tensor(out=sy[:], in0=ps[:, 7, 0:KV], scalar=small[:, 74:75], in1=sy[:], op0=ALU.mult, op1=ALU.add
                                             ).then_inc(sa_y, 1)

                def copy_turned(pair):
                    dve.wait_ge(sa_yt, nth(sa_yt, 4 * l + (pair + 1)))
                    for gp in range(2):
                        for g in range(2):
                            rows = slice(64 * g, 64 * g + 64)
                            src = ps[rows, 7, gp * P:(gp + 1) * P].rearrange("p (s g t r) -> p g r s t", s=2, g=4, t=TS)[:, 2 * gp + g]
                            dst = yT[rows, 4 * gp:4 * gp + 4, SEQ + 8 * pair:SEQ + 8 * pair + 8].rearrange("p r (s t) -> p r s t", s=2)
                            last = dve.tensor_copy(dst, src)
                    dve.drain().then_inc(sa_ys, 1)

                for pair in range(4):
                    par, it = pair % 2, 4 * l + pair
                    for g in range(2):
                        rows = slice(64 * g, 64 * g + 64)
                        for gp in range(2):
                            for s in range(2):
                                src = qsT[rows, 4 * gp:4 * gp + 4, (2 * pair + s) * TS:(2 * pair + s + 1) * TS].rearrange("p r t -> p t r")
                                last = dve.tensor_copy(qs[rows, par, gp, s, 16 * g:16 * g + 16].rearrange("p (t r) -> p t r", t=TS), src)
                    last.then_inc(sa_q, 1)
                    if pair:
                        combine_pair(pair - 1)
                    dve.wait_ge(sa_c, it + 1)
                    dve.tensor_reduce(out=small[:, 64:65], in_=ps[:, 3, 0:NWS], op=ALU.max, axis=AX.X, negate=True)
                    nm = C("nmask")[:, NSAM * pair:NSAM * (pair + 1)]
                    dve.tensor_tensor(ssel[:, PAST:PAST + NSAM], ps[:, 3, 64:64 + NSAM], nm, ALU.add)
                    dve.tensor_tensor(swsc[:, WIN:WIN + NSAM], ps[:, 3, 64 + NSAM:64 + 2 * NSAM], nm, ALU.add)
                    dve.drain()
                    dve.tensor_scalar(small[:, 64:65], small[:, 64:65], -LOWEST, SCALE, ALU.min, ALU.mult).then_inc(sa_nm, 1)
                    dve.wait_ge(sa_cx, it + 1)
                    dve.tensor_scalar(small[:, 65:66], small[:, 65:66], 1e-30, None, ALU.max)
                    dve.drain()
                    dve.reciprocal(small[:, 65:66], small[:, 65:66])
                    dve.drain()
                    dve.tensor_scalar(pc[:, 0:NWS], pc[:, 0:NWS], small[:, 65:66], None, ALU.mult)
                    dve.drain()
                    dve.tensor_reduce(out=small[:, 32:46], in_=pc[:, 4:60].rearrange("p (j k) -> p j k", k=4), op=ALU.add, axis=AX.X)
                    dve.drain()
                    dve.tensor_tensor(small[:, 32:46], small[:, 32:46], pc[:, 3:56:4], ALU.add).then_inc(sa_im, 1)
                    dve.wait_ge(sa_imp, it + 1)
                    imp = ps[:, 3, 256:270]
                    dve.tensor_reduce(out=small[:, 66:67], in_=imp, op=ALU.min, axis=AX.X)
                    dve.drain()
                    dve.scalar_tensor_tensor(out=small[:, 80:94], in0=imp, scalar=small[:, 66:67], in1=C("iota")[:, 1:15],
                                             op0=ALU.is_equal, op1=ALU.mult)
                    dve.drain()
                    dve.tensor_reduce(out=small[:, 67:68], in_=small[:, 80:94], op=ALU.max, axis=AX.X)
                    dve.drain()
                    dve.tensor_scalar(small[:, 96:112], C("iota"), small[:, 67:68], NEG, ALU.is_equal, ALU.mult)
                    dve.drain()
                    dve.wait_ge(sa_s, nth(sa_s, 12 * it + 8))
                    drop = small[:, 96:112].unsqueeze(1).unsqueeze(3).to_broadcast([P, 8, 16, 8])
                    dve.tensor_tensor(ssel[:, 0:PAST].rearrange("p (t j c) -> p t j c", t=8, j=16),
                                      ps[:, 0:2, :].rearrange("p a (t j c) -> p (a t) j c", t=4, j=16), drop, ALU.add)
                    dve.drain()
                    dve.tensor_reduce(out=small[:, 68:69], in_=ssel[:], op=ALU.max, axis=AX.X, negate=True)
                    dve.drain()
                    dve.tensor_scalar(small[:, 68:69], small[:, 68:69], SCALE, None, ALU.mult).then_inc(sa_m, 1)
                    dve.wait_ge(sa_s, nth(sa_s, 12 * it + 12))
                    dve.tensor_tensor(swsc[:, 0:WIN], ps[:, 2, :], C("wmask"), ALU.add)
                    dve.drain()
                    dve.tensor_reduce(out=small[:, 69:70], in_=swsc[:], op=ALU.max, axis=AX.X, negate=True)
                    dve.drain()
                    dve.tensor_scalar(small[:, 69:70], small[:, 69:70], SCALE, None, ALU.mult).then_inc(sa_m, 1)
                    if pair:
                        copy_turned(pair - 1)
                combine_pair(3)
                copy_turned(3)
                dve.wait_ge(s_winout, 256 * l + 256)
                dve.sem_inc(passed, 1)
                end_phase(dve, l, 8)

                make_h(2 * l + 1)
                make_low(dve, l, pb(B_ZB, 0, 0), 0)
                end_phase(dve, l, 9)
                with dve.Fori(0, 2) as i:
                    for n in range(2):
                        make_low(dve, l, pb(B_ZB, i + (n + 1) // 2, (n + 1) % 2), (n + 1) % 2)
                        for jj in range(2):
                            q = 8 * l + 4 * i + (2 * n + jj)
                            dve.wait_ge(zb_sg, q + 1)
                            dve.tensor_tensor(halves(t_f[:, jj, :]), bank2(2 * (2 * n + jj)), halves(t_f[:, jj, :]), ALU.mult)
                            dve.drain()
                            dve.tensor_tensor(t_f[:, jj, :], t_f[:, jj, :], one(yT, 4 * i + (2 * n + jj)), ALU.mult).then_inc(zb_f, 1)
                        dve.drain()
                        for jj in range(2):
                            q = 8 * l + 4 * i + (2 * n + jj)
                            dve.wait_ge(zb_hi, q + 1)
                            c = 4 * i + (2 * n + jj)
                            dve.tensor_tensor(one(aL, c), t_f[:, jj, :], one(aH, c).bitcast(F32), ALU.subtract).then_inc(zb_done, 1)
                end_phase(dve, l, 10)
                products(1, B_MB)
                end_phase(dve, l, 11)
                split(2 * l, m)
                end_phase(dve, l, 12)
                with dve.Fori(0, 2) as i:
                    for n in range(2):
                        make_low(dve, l, pb(B_WO, i + (n + 1) // 2, (n + 1) % 2), (n + 1) % 2)
                        for jj in range(2):
                            c = 4 * i + (2 * n + jj)
                            dve.wait_ge(wo, 8 * l + c + 1)
                            dve.tensor_tensor(two(xT, c), two(xT, c), bank2(2 * (2 * n + jj)), ALU.add).then_inc(wo_done, 1)
                dve.drain()
                for c in range(2):
                    dve.wait_ge(p_hi, 2 * l + (c + 1))
                    dve.tensor_tensor(pL[:, c, 0:SEQ], ps[:, 2 * c, :], pH[:, c, 0:SEQ].bitcast(F32), ALU.subtract)
                    dve.tensor_tensor(pL[:, c, SEQ:TOK], ps[:, 2 * c + 1, 0:NSAM], pH[:, c, SEQ:TOK].bitcast(F32), ALU.subtract)
                dve.drain().then_inc(p_lo, 1)
                split(2 * l + 1, xT)
                end_phase(dve, l, 13)

                def prep_ple(m):
                    if m % 3 == 2:
                        make_low(dve, l, B_PL + m, m % 2, wide_block=True)
                    else:
                        make_low(dve, l, B_PL + m, m % 2)

                for i in range(2):
                    prep_ple(3 * i + 1)
                    prep_ple(3 * i + 2)
                    if i == 0:
                        prep_ple(3)
                    for q in range(4):
                        dve.wait_ge(pl_sg, 8 * l + (4 * i + q + 1))
                        dve.wait_ge(pl, 16 * l + (8 * i + 4 + q + 1))
                        dve.tensor_tensor(halves(t_f[:, q, :]), bank2(2 * q), halves(t_f[:, q, :]), ALU.mult)
                        dve.drain()
                        dve.tensor_tensor(one(xT, 4 * i + q), one(xT, 4 * i + q), t_f[:, q, :], ALU.add).then_inc(pl_done, 1)
                end_phase(dve, l, 14)

            norm_add(NL)
            norm_recip(NL)
            for c in range(KT):
                last = dve.scalar_tensor_tensor(out=xT[:, c, :], in0=xT[:, c, :], scalar=cols[:, c, 20:21], in1=rstd[:], op0=ALU.mult, op1=ALU.mult)
            dve.drain().then_inc(y_ready, 1)
            for tt in range(5):
                rows = P if tt < NT else NSAM
                dve.wait_ge(y_tp, tt + 1)
                dve.tensor_copy(out_rows[0:rows, tt, SEQ:D], ps[0:rows, 2 * (tt % 4) + 1, :]).then_inc(y_dve, 1)


INPUTS = ["x_prompt", "x_sample", "cache_kv", "state_win", "state_conv", "page_table", "p_prompt", "p_sample",
          "ln_g", "w_in", "conv_w", "cmp_pos_k", "cmp_w1_k", "cmp_w2_k", "cmp_pos_v", "cmp_w1_v", "cmp_w2_v",
          "w_out_a", "w_out_b", "w_o", "w_ple", "w_ple_gate", "final_g"]
OUTPUTS = [("y_prompt", (1, SEQ, D)), ("y_sample", (NSEQ, TS, D)),
           ("new_kv_prompt", (NL, 1, SEQ, 4, GROUPS, HD)), ("new_kv_sample", (NL, NSEQ, TS, 4, GROUPS, HD)),
           ("new_win_prompt", (NL, 1, WIN, 2, GROUPS, HD)), ("new_win_sample", (NL, NSEQ, WIN, 2, GROUPS, HD)),
           ("new_conv_prompt", (NL, 1, 2, D)), ("new_conv_sample", (NL, NSEQ, 2, D))]


def kernel(**inputs):
    import concourse.bacc as bacc
    from concourse.bass_utils import run_bass_kernel_spmd

    nc = bacc.Bacc("TRN2", target_bir_lowering=False, num_devices=1)
    arrays, aps = {}, {}
    data = {name: np.ascontiguousarray(inputs[name]) for name in INPUTS}
    data["consts"] = constants()
    for name, x in data.items():
        arrays["in_" + name] = x
        aps[name] = nc.dram_tensor("in_" + name, x.shape, mybir.dt.from_np(x.dtype), kind="ExternalInput").ap()
    for name, shape in OUTPUTS:
        aps[name] = nc.dram_tensor("out_" + name, shape, F32, kind="ExternalOutput").ap()
    build(nc, aps)
    r = run_bass_kernel_spmd(nc, [arrays], core_ids=[0])
    return tuple(r.results[0]["out_" + name] for name, _ in OUTPUTS)
```
